# Optimizing a Trainium2 kernel written in Bass

```python
import math
import jax, jax.numpy as jnp
from jax import lax
import numpy as np

D_MODEL = 1024
BATCH = 1
SEQ = 1024
DEPTH = 1

HEAD_DIM = 64
ATTN_HEADS_PER_GROUP = 8
DILATED_GROUPS = ((128, 1), (512, 4), (2048, 16))
N_GROUPS = 3
ATTN_WIDTH = ATTN_HEADS_PER_GROUP * HEAD_DIM
N_ATTN_HEADS = N_GROUPS * ATTN_HEADS_PER_GROUP
QBLOCK = 128
N_BUCKETS = 32
MAX_DISTANCE = 2048
RWKV_HEADS = 8
RWKV_HEAD_SIZE = 64
RWKV_WIDTH = RWKV_HEADS * RWKV_HEAD_SIZE
DECAY_LORA = 64
AAA_LORA = 64
GN_EPS = 64e-5
RMS_EPS = 1e-6

QKV_COLS = 3 * N_GROUPS * ATTN_WIDTH
OFF_ATTN_GATE = QKV_COLS
OFF_RWKV = OFF_ATTN_GATE + ATTN_WIDTH
RWKV_SHIFT_COLS = 3 * RWKV_WIDTH + DECAY_LORA + AAA_LORA
OFF_RWKV_GATE = OFF_RWKV + RWKV_SHIFT_COLS
OFF_MERGE = OFF_RWKV_GATE + RWKV_WIDTH
IN_COLS = OFF_MERGE + 2 * D_MODEL


def rms_norm(x, g):
    xf = x.astype(jnp.float32)
    y = xf * lax.rsqrt(jnp.mean(xf * xf, axis=-1, keepdims=True) + RMS_EPS) * g.astype(jnp.float32)
    return y.astype(x.dtype)

def t5_causal_bucket(dist):
    d = np.maximum(np.asarray(dist), 0)
    max_exact = N_BUCKETS // 2
    ratio = np.log(np.maximum(d, 1).astype(np.float32) / max_exact) / np.float32(math.log(MAX_DISTANCE / max_exact))
    large = max_exact + (ratio * (N_BUCKETS - max_exact)).astype(np.int32)
    large = np.minimum(large, N_BUCKETS - 1)
    return np.where(d < max_exact, d, large).astype(np.int32)

def dilated_group_attention(q, k, v, bias_table_g, window, dilation):
    B, S, H, Dh = q.shape
    L = S // dilation
    steps = window // dilation
    nb = -(-L // QBLOCK)
    Lp = nb * QBLOCK

    def to_blocks(t):
        t = t.reshape(B, L, dilation, H, Dh).transpose(0, 2, 3, 1, 4)
        t = jnp.pad(t, ((0, 0), (0, 0), (0, 0), (0, Lp - L), (0, 0)))
        return t.reshape(B, dilation, H, nb, QBLOCK, Dh)

    def with_prev(t):
        prev = jnp.pad(t, ((0, 0), (0, 0), (0, 0), (1, 0), (0, 0), (0, 0)))[:, :, :, :-1]
        return jnp.concatenate([prev, t], axis=4)

    qb = to_blocks(q)
    kb = with_prev(to_blocks(k))
    vb = with_prev(to_blocks(v))

    qi = np.arange(QBLOCK)[:, None] + QBLOCK
    ki = np.arange(2 * QBLOCK)[None, :]
    rel = qi - ki
    band = (rel >= 0) & (rel <= steps)
    has_prev = (np.arange(nb)[:, None, None] > 0) | (ki >= QBLOCK)[None]
    valid = band[None] & has_prev
    bucket = t5_causal_bucket(np.maximum(rel, 0) * dilation)
    bias = bias_table_g.astype(jnp.float32)[bucket].transpose(2, 0, 1)

    scale = 1.0 / math.sqrt(Dh)
    logits = jnp.einsum('bdhnqc,bdhnkc->bdhnqk', qb, kb) * scale + bias[None, None, :, None]
    logits = jnp.where(valid, logits, -jnp.inf)
    m = jnp.max(logits, axis=-1)
    p = jnp.exp(logits - m[..., None])
    s = jnp.sum(p, axis=-1)
    num = jnp.einsum('bdhnqk,bdhnkc->bdhnqc', p, vb)

    def unblock(t):
        C = t.shape[-1]
        t = t.reshape(B, dilation, H, Lp, C)[:, :, :, :L]
        return t.transpose(0, 3, 1, 2, 4).reshape(B, S, H, C)

    return unblock(num), unblock(s[..., None])[..., 0], unblock(m[..., None])[..., 0]

def rwkv7_scan(r, decay, k, v, a_in, b_in):
    B, S, H, N = r.shape
    xs = tuple(t.transpose(1, 0, 2, 3) for t in (r, decay, k, v, a_in, b_in))

    def step(state, inp):
        r_t, w_t, k_t, v_t, a_t, b_t = inp
        sa = jnp.einsum('bhvk,bhk->bhv', state, a_t)
        state = (state * w_t[:, :, None, :] + sa[..., None] * b_t[:, :, None, :]
                 + v_t[..., None] * k_t[:, :, None, :])
        y = jnp.einsum('bhvk,bhk->bhv', state, r_t)
        return state, y

    s0 = jnp.zeros((B, H, N, N), jnp.float32)
    _, ys = lax.scan(step, s0, xs)
    return ys.transpose(1, 0, 2, 3)

def first_inputs(seed: int = 0) -> dict:
    key = jax.random.key(seed)
    ks = jax.random.split(key, 20)
    f32 = jnp.float32
    nrm = lambda k, shape: jax.random.normal(k, shape, f32)
    L = DEPTH
    return {
        "x": nrm(ks[0], (BATCH, SEQ, D_MODEL)),
        "pre_norm_gain": 1.0 + 0.05 * nrm(ks[1], (L, D_MODEL)),
        "w_in": nrm(ks[2], (L, D_MODEL, IN_COLS)) * D_MODEL ** -0.5,
        "rel_bias": 0.5 * nrm(ks[3], (N_BUCKETS, N_ATTN_HEADS)),
        "rwkv_shift_mix": jax.random.uniform(ks[4], (L, RWKV_SHIFT_COLS), f32),
        "rwkv_w0": jax.random.uniform(ks[5], (L, RWKV_WIDTH), f32, -6.0, 1.0),
        "rwkv_w_up": nrm(ks[6], (L, DECAY_LORA, RWKV_WIDTH)) * 0.5 * DECAY_LORA ** -0.5,
        "rwkv_a0": 0.5 * nrm(ks[7], (L, RWKV_WIDTH)),
        "rwkv_a_up": nrm(ks[8], (L, AAA_LORA, RWKV_WIDTH)) * 0.5 * AAA_LORA ** -0.5,
        "rwkv_k_k": 0.85 + 0.05 * nrm(ks[9], (L, RWKV_WIDTH)),
        "rwkv_k_a": 1.0 + 0.05 * nrm(ks[10], (L, RWKV_WIDTH)),
        "rwkv_r_k": 0.1 * nrm(ks[11], (L, RWKV_HEADS, RWKV_HEAD_SIZE)),
        "rwkv_ln_w": 1.0 + 0.05 * nrm(ks[12], (L, RWKV_WIDTH)),
        "rwkv_ln_b": 0.01 * nrm(ks[13], (L, RWKV_WIDTH)),
        "w_up_attn": nrm(ks[14], (L, ATTN_WIDTH, D_MODEL)) * ATTN_WIDTH ** -0.5,
        "w_up_rwkv": nrm(ks[15], (L, RWKV_WIDTH, D_MODEL)) * RWKV_WIDTH ** -0.5,
        "w_out": nrm(ks[16], (L, D_MODEL, D_MODEL)) * D_MODEL ** -0.5,
        "post_norm_gain": 1.0 + 0.05 * nrm(ks[17], (L, D_MODEL)),
    }

def first_block(x, pre_norm_gain, w_in, rel_bias, rwkv_shift_mix, rwkv_w0, rwkv_w_up,
              rwkv_a0, rwkv_a_up, rwkv_k_k, rwkv_k_a, rwkv_r_k, rwkv_ln_w, rwkv_ln_b,
              w_up_attn, w_up_rwkv, w_out, post_norm_gain):
    B, S, D = x.shape
    f32 = jnp.float32
    for l in range(DEPTH):
        h = rms_norm(x, pre_norm_gain[l])
        proj = h @ w_in[l]

        qkv = proj[..., :QKV_COLS].astype(f32).reshape(
            B, S, 3, N_GROUPS, ATTN_HEADS_PER_GROUP, HEAD_DIM)
        nums, dens, maxes = [], [], []
        for g, (window, dilation) in enumerate(DILATED_GROUPS):
            table_g = rel_bias[:, g * ATTN_HEADS_PER_GROUP:(g + 1) * ATTN_HEADS_PER_GROUP]
            num, den, mx = dilated_group_attention(
                qkv[:, :, 0, g], qkv[:, :, 1, g], qkv[:, :, 2, g], table_g, window, dilation)
            nums.append(num); dens.append(den); maxes.append(mx)
        m_all = jnp.max(jnp.stack(maxes), axis=0)
        wts = [jnp.exp(mx - m_all) for mx in maxes]
        num_tot = sum(w[..., None] * n for w, n in zip(wts, nums))
        den_tot = sum(w * d for w, d in zip(wts, dens))
        o_attn = (num_tot / den_tot[..., None]).reshape(B, S, ATTN_WIDTH).astype(x.dtype)
        z_attn = proj[..., OFF_ATTN_GATE:OFF_RWKV]
        y_attn = (o_attn * jax.nn.silu(z_attn)) @ w_up_attn[l]

        pr = proj[..., OFF_RWKV:OFF_RWKV_GATE].astype(f32)
        pr_prev = jnp.pad(pr, ((0, 0), (1, 0), (0, 0)))[:, :-1]
        pr = pr + (pr_prev - pr) * rwkv_shift_mix[l].astype(f32)
        r = pr[..., :RWKV_WIDTH]
        k = pr[..., RWKV_WIDTH:2 * RWKV_WIDTH]
        v = pr[..., 2 * RWKV_WIDTH:3 * RWKV_WIDTH]
        w_low = pr[..., 3 * RWKV_WIDTH:3 * RWKV_WIDTH + DECAY_LORA]
        a_low = pr[..., 3 * RWKV_WIDTH + DECAY_LORA:]
        w_log = -jax.nn.softplus(-(rwkv_w0[l].astype(f32) + jnp.tanh(w_low) @ rwkv_w_up[l].astype(f32))) - 0.5
        decay = jnp.exp(-jnp.exp(w_log))
        a = jax.nn.sigmoid(rwkv_a0[l].astype(f32) + a_low @ rwkv_a_up[l].astype(f32))
        hs = (B, S, RWKV_HEADS, RWKV_HEAD_SIZE)
        kk = (k * rwkv_k_k[l].astype(f32)).reshape(hs)
        kk = kk / jnp.maximum(jnp.linalg.norm(kk, axis=-1, keepdims=True), 1e-12)
        k = k * (1.0 + (a - 1.0) * rwkv_k_a[l].astype(f32))
        r4, k4, v4 = r.reshape(hs), k.reshape(hs), v.reshape(hs)
        y = rwkv7_scan(r4, decay.reshape(hs), k4, v4, -kk, kk * a.reshape(hs))
        mu = jnp.mean(y, axis=-1, keepdims=True)
        var = jnp.mean(jnp.square(y - mu), axis=-1, keepdims=True)
        y = ((y - mu) * lax.rsqrt(var + GN_EPS)).reshape(B, S, RWKV_WIDTH)
        y = y * rwkv_ln_w[l].astype(f32) + rwkv_ln_b[l].astype(f32)
        bonus = jnp.sum(r4 * k4 * rwkv_r_k[l].astype(f32), axis=-1, keepdims=True) * v4
        o_rwkv = (y + bonus.reshape(B, S, RWKV_WIDTH)).astype(x.dtype)
        z_rwkv = proj[..., OFF_RWKV_GATE:OFF_MERGE]
        y_rwkv = (o_rwkv * jax.nn.silu(z_rwkv)) @ w_up_rwkv[l]

        g_attn = proj[..., OFF_MERGE:OFF_MERGE + D_MODEL]
        g_rwkv = proj[..., OFF_MERGE + D_MODEL:]
        merged = jax.nn.sigmoid(g_attn) * y_attn + jax.nn.sigmoid(g_rwkv) * y_rwkv
        out = merged @ w_out[l]
        x = x + rms_norm(out, post_norm_gain[l])
    return x


DEPTH_2 = 2

N_A_LAYERS = DEPTH_2 // 2
N_B_LAYERS = DEPTH_2 - N_A_LAYERS

CHUNK = 128
A_WIDTH = 2 * D_MODEL
A_GROUPS = 8
A_GROUP_CH = A_WIDTH // A_GROUPS

N_Q_HEADS = D_MODEL // HEAD_DIM
N_KV_HEADS = 4
Q_PER_KV = N_Q_HEADS // N_KV_HEADS
B_WIDTH = N_Q_HEADS * HEAD_DIM
KV_WIDTH = N_KV_HEADS * HEAD_DIM
WINDOW = 128
BLOCK = 128

EPS = 1e-6


def rms_norm_2(x, g):
    xf = x.astype(jnp.float32)
    y = xf * lax.rsqrt(jnp.mean(xf * xf, axis=-1, keepdims=True) + EPS)
    return (y * g.astype(jnp.float32)).astype(x.dtype)

def layer_norm(x, g, b):
    xf = x.astype(jnp.float32)
    mu = jnp.mean(xf, axis=-1, keepdims=True)
    var = jnp.mean(jnp.square(xf - mu), axis=-1, keepdims=True)
    y = (xf - mu) * lax.rsqrt(var + EPS)
    return (y * g.astype(jnp.float32) + b.astype(jnp.float32)).astype(x.dtype)

def alibi_slopes(n_heads):
    return jnp.asarray(np.array([2.0 ** (-8.0 * (h + 1) / n_heads) for h in range(n_heads)], dtype=np.float32))

def gmlp_mixer(h, w_in, ln_g, ln_b, w_s, b_s, w_out):
    bsz, s_len, _ = h.shape
    u, v, z = jnp.split(h @ w_in, 3, axis=-1)
    u = jax.nn.gelu(u)
    v = layer_norm(jax.nn.gelu(v), ln_g, ln_b)
    n_chunks = s_len // CHUNK
    v = v.reshape(bsz, n_chunks, CHUNK, A_GROUPS, A_GROUP_CH)
    causal = jnp.tril(jnp.ones((CHUNK, CHUNK), dtype=bool))
    w_causal = jnp.where(causal[None], w_s, 0.0).astype(v.dtype)
    s = jnp.einsum('gts,bnsgc->bntgc', w_causal, v) + b_s.T[:, :, None].astype(v.dtype)
    s = s.reshape(bsz, s_len, A_WIDTH)
    y = u * s * jax.nn.silu(z)
    return y @ w_out

def swa_mixer(h, k, v, w_in, sinks, w_out):
    bsz, s_len, _ = h.shape
    q, z = jnp.split(h @ w_in, 2, axis=-1)
    q = q * (HEAD_DIM ** -0.5)
    n_blocks = s_len // BLOCK
    q_blocks = q.reshape(bsz, n_blocks, BLOCK, N_KV_HEADS, Q_PER_KV, HEAD_DIM).transpose(1, 0, 2, 3, 4, 5)
    pad = jnp.zeros((bsz, BLOCK, N_KV_HEADS, HEAD_DIM), k.dtype)
    k_pad = jnp.concatenate([pad, k], axis=1)
    v_pad = jnp.concatenate([pad, v], axis=1)

    r = jnp.arange(BLOCK)[:, None]
    c = jnp.arange(2 * BLOCK)[None, :]
    dist = BLOCK + r - c
    in_window = (dist >= 0) & (dist < WINDOW)
    slopes = alibi_slopes(N_Q_HEADS).reshape(N_KV_HEADS, Q_PER_KV)
    alibi = -slopes[:, :, None, None] * dist.astype(jnp.float32)
    sink = sinks.astype(jnp.float32).reshape(N_KV_HEADS, Q_PER_KV)[None, :, :, None]

    def block_fn(args):
        i, qb = args
        start = i * BLOCK
        kb = lax.dynamic_slice_in_dim(k_pad, start, 2 * BLOCK, axis=1)
        vb = lax.dynamic_slice_in_dim(v_pad, start, 2 * BLOCK, axis=1)
        logits = jnp.einsum('btkgd,bskd->bkgts', qb, kb).astype(jnp.float32) + alibi
        valid = in_window & ((start - BLOCK + c) >= 0)
        logits = jnp.where(valid, logits, -jnp.inf)
        m = jnp.maximum(jnp.max(logits, axis=-1), sink)
        p = jnp.exp(logits - m[..., None])
        denom = jnp.sum(p, axis=-1) + jnp.exp(sink - m)
        o = jnp.einsum('bkgts,bskd->btkgd', p.astype(vb.dtype), vb).astype(jnp.float32)
        o = o / denom.transpose(0, 3, 1, 2)[..., None]
        return o.astype(h.dtype)

    out = lax.map(block_fn, (jnp.arange(n_blocks), q_blocks))
    out = out.transpose(1, 0, 2, 3, 4, 5).reshape(bsz, s_len, B_WIDTH)
    y = out * jax.nn.silu(z)
    return y @ w_out

def second_inputs(seed: int = 0) -> dict:
    key = jax.random.key(seed)
    ks = jax.random.split(key, 20)
    f32 = jnp.float32
    nrm = lambda k, shape, scale: jax.random.normal(k, shape, f32) * scale
    x = jax.random.normal(ks[0], (BATCH, SEQ, D_MODEL), f32)
    a_w_in = nrm(ks[1], (N_A_LAYERS, D_MODEL, 3 * A_WIDTH), D_MODEL ** -0.5)
    a_ln_g = 1.0 + nrm(ks[2], (N_A_LAYERS, A_WIDTH), 0.05)
    a_ln_b = nrm(ks[3], (N_A_LAYERS, A_WIDTH), 0.02)
    a_w_s = nrm(ks[4], (N_A_LAYERS, A_GROUPS, CHUNK, CHUNK), CHUNK ** -0.5)
    a_b_s = 1.0 + nrm(ks[5], (N_A_LAYERS, A_GROUPS, CHUNK), 0.1)
    a_w_out = nrm(ks[6], (N_A_LAYERS, A_WIDTH, D_MODEL), A_WIDTH ** -0.5)
    a_pre_g = 1.0 + nrm(ks[7], (N_A_LAYERS, D_MODEL), 0.05)
    a_post_g = 1.0 + nrm(ks[8], (N_A_LAYERS, D_MODEL), 0.05)
    kv_norm_g = 1.0 + nrm(ks[9], (D_MODEL,), 0.05)
    w_k = nrm(ks[10], (D_MODEL, KV_WIDTH), D_MODEL ** -0.5)
    w_v = nrm(ks[11], (D_MODEL, KV_WIDTH), D_MODEL ** -0.5)
    b_w_in = nrm(ks[12], (N_B_LAYERS, D_MODEL, 2 * B_WIDTH), D_MODEL ** -0.5)
    b_sinks = nrm(ks[13], (N_B_LAYERS, N_Q_HEADS), 0.5)
    b_w_out = nrm(ks[14], (N_B_LAYERS, B_WIDTH, D_MODEL), B_WIDTH ** -0.5)
    b_pre_g = 1.0 + nrm(ks[15], (N_B_LAYERS, D_MODEL), 0.05)
    b_post_g = 1.0 + nrm(ks[16], (N_B_LAYERS, D_MODEL), 0.05)
    return {"x": x, "a_w_in": a_w_in, "a_ln_g": a_ln_g, "a_ln_b": a_ln_b, "a_w_s": a_w_s,
            "a_b_s": a_b_s, "a_w_out": a_w_out, "a_pre_g": a_pre_g, "a_post_g": a_post_g,
            "kv_norm_g": kv_norm_g, "w_k": w_k, "w_v": w_v, "b_w_in": b_w_in, "b_sinks": b_sinks,
            "b_w_out": b_w_out, "b_pre_g": b_pre_g, "b_post_g": b_post_g}

def second_block(x, a_w_in, a_ln_g, a_ln_b, a_w_s, a_b_s, a_w_out, a_pre_g, a_post_g,
              kv_norm_g, w_k, w_v, b_w_in, b_sinks, b_w_out, b_pre_g, b_post_g):
    bsz, s_len, _ = x.shape
    h = x
    k_shared = None
    v_shared = None
    for layer in range(DEPTH_2):
        if layer < N_A_LAYERS:
            i = layer
            y = gmlp_mixer(rms_norm_2(h, a_pre_g[i]), a_w_in[i], a_ln_g[i], a_ln_b[i],
                           a_w_s[i], a_b_s[i], a_w_out[i])
            h = h + rms_norm_2(y, a_post_g[i])
            if layer == N_A_LAYERS - 1:
                kv_in = rms_norm_2(h, kv_norm_g)
                k_shared = (kv_in @ w_k).reshape(bsz, s_len, N_KV_HEADS, HEAD_DIM)
                v_shared = (kv_in @ w_v).reshape(bsz, s_len, N_KV_HEADS, HEAD_DIM)
        else:
            j = layer - N_A_LAYERS
            y = swa_mixer(rms_norm_2(h, b_pre_g[j]), k_shared, v_shared,
                          b_w_in[j], b_sinks[j], b_w_out[j])
            h = h + rms_norm_2(y, b_post_g[j])
    return h


def setup_inputs(seed=0):
    out = dict(first_inputs(seed))
    for name, value in second_inputs(seed + 1).items():
        if name != "x":
            out[name + "_2"] = value
    return out


def reference(
    x, pre_norm_gain, w_in, rel_bias, rwkv_shift_mix, rwkv_w0, rwkv_w_up, rwkv_a0, rwkv_a_up,
    rwkv_k_k, rwkv_k_a, rwkv_r_k, rwkv_ln_w, rwkv_ln_b, w_up_attn, w_up_rwkv, w_out,
    post_norm_gain, a_w_in_2, a_ln_g_2, a_ln_b_2, a_w_s_2, a_b_s_2, a_w_out_2, a_pre_g_2,
    a_post_g_2, kv_norm_g_2, w_k_2, w_v_2, b_w_in_2, b_sinks_2, b_w_out_2, b_pre_g_2,
    b_post_g_2,
):
    x = first_block(
        x, pre_norm_gain, w_in, rel_bias, rwkv_shift_mix, rwkv_w0, rwkv_w_up, rwkv_a0,
        rwkv_a_up, rwkv_k_k, rwkv_k_a, rwkv_r_k, rwkv_ln_w, rwkv_ln_b, w_up_attn, w_up_rwkv,
        w_out, post_norm_gain,
    )
    return second_block(
        x, a_w_in_2, a_ln_g_2, a_ln_b_2, a_w_s_2, a_b_s_2, a_w_out_2, a_pre_g_2, a_post_g_2,
        kv_norm_g_2, w_k_2, w_v_2, b_w_in_2, b_sinks_2, b_w_out_2, b_pre_g_2, b_post_g_2,
    )


_drawn_inputs = setup_inputs


def setup_inputs(seed=0):
    import zlib

    import numpy as np

    out = dict(_drawn_inputs(seed))
    spreads = {}
    factors = {'rwkv_ln_b': 5.25, 'a_ln_g_2': 2.926, 'a_ln_b_2': 6.997}
    for name, (base, spread) in spreads.items():
        noise = np.random.default_rng([zlib.crc32(name.encode()), seed]).standard_normal(out[name].shape)
        drawn = base * np.exp(spread * noise) if base else spread * noise
        out[name] = __import__('jax').numpy.asarray(drawn.astype(out[name].dtype))
    for name, factor in factors.items():
        out[name] = (out[name] * factor).astype(out[name].dtype)
    return out
```

```python
from contextlib import ExitStack
import math

import numpy as np
import concourse.bass as bass
from concourse import mybir

F32 = mybir.dt.float32
F32R = mybir.dt.float32r
ALU = mybir.AluOpType
ACT = mybir.ActivationFunctionType

P = 128
T = 1024
D = 1024
HALF = 512
KT = D // P
PAIRS = 4
GROUPS = 3
DILATION = (1, 4, 16)
ATTN = 512
C = 64
NCH = T // C
LINE = 384
OFF_Q, OFF_K, OFF_V = 0, 1536, 3072
OFF_ZA, OFF_R, OFF_RK, OFF_RV, OFF_LORA, OFF_ZR = 4608, 5120, 5632, 6144, 6656, 6784
OFF_GA, OFF_GR = 7296, 8320
AW = 2048
QP = 8
FAR = 1e30
EPS = 1e-6
GN_EPS = 64e-5
KB = 1024


def shape_constants():
    r = np.arange(P)
    j = r % C
    t = np.arange(C)
    ident = np.eye(P)
    blocks = (r[:, None] // C == r[None, :] // C)
    ones = np.ones((P, P))
    strict, incl = j[:, None] < t[None, :], j[:, None] <= t[None, :]
    levels = []
    s = 1
    while s < C:
        levels.append((t[None, :] // (2 * s) == j[:, None] // (2 * s)) & (t[None, :] // s % 2 == 1) & (j[:, None] // s % 2 == 0))
        s *= 2
    ident2 = j[:, None] == t[None, :]
    causal = r[:, None] <= r[None, :]
    q, c = r[:, None], np.arange(2 * P)[None, :]
    dist = P + q - c
    far = np.where((dist >= 0) & (dist < P), dist, FAR)
    packed = np.concatenate([np.asarray(x, np.float32) for x in (ident, blocks, ones, strict, incl, *levels, ident2, causal, far)], axis=1)
    rel = 255 - np.arange(LINE)
    hot = np.zeros((33, GROUPS, LINE), np.float32)
    for g, dil in enumerate(DILATION):
        d = np.maximum(rel, 0) * dil
        ratio = np.log(np.maximum(d, 1).astype(np.float32) / 16) / np.float32(math.log(2048 / 16))
        large = np.minimum(16 + (ratio * 16).astype(np.int32), 31)
        bucket = np.where(d < 16, d, large)
        ok = (rel >= 0) & (rel <= P)
        hot[bucket, g, np.arange(LINE)] = ok
        hot[32, g] = np.where(ok, 0.0, -FAR)
    return packed, hot


NCONST = 128 * 3 + 64 * 2 + 64 * 6 + 64 + 128 + 256


class Own:

    def __init__(self, eng, chain):
        self.eng, self.chain, self.count = eng, chain, {}

    def __call__(self, ins, signal=None):
        s, n = signal if isinstance(signal, tuple) else (signal, None)
        s = self.chain if s is None else s
        ins.then_inc(s, 1)
        n = self.count.get(s.name, 0) + 1 if n is None else n
        self.count[s.name] = n
        self.eng.wait_ge(s, n)


def build(nc, d, out, stop=99):
    ctx = ExitStack()
    with ctx:
        base = (nc.sbuf_base + 255) // 256 * 256

        def at(name, kb, shape, dt=F32):
            n = int(np.prod(shape[1:])) * 4
            assert kb * KB + n <= 207 * KB + 512, (name, kb, n)
            return nc.alloc_sbuf_tensor_at(name, list(shape), dt, offset=base + int(kb * KB))

        def sem(name):
            return ctx.enter_context(nc.semaphore(name))

        G = [nc.alloc_psum_tensor(f"gemm{h}", [P, HALF], F32) for h in range(2)]
        S2 = nc.alloc_psum_tensor("scores", [P, 2 * HALF], F32)
        PT2 = nc.alloc_psum_tensor("probs_t", [P, 2 * HALF], F32)
        PV = nc.alloc_psum_tensor("weighted", [P, HALF], F32)
        MB = nc.alloc_psum_tensor("max_rows", [P, HALF], F32)

        raw = at("w_raw", 0, [P, 2, KT, P])
        whi = at("w_hi", 8, [P, 2, KT, P], F32R)
        wlo = at("w_lo", 16, [P, 2, KT, P], F32R)
        cst = at("consts_sb", 24, [P, NCONST])
        o_ = 0
        ident = cst[:, 0:128]
        blocks = cst[:, 128:256]
        ones = cst[:, 256:384]
        mask_a = cst[:, 384:512]
        level = [cst[:, 512 + 64 * i:576 + 64 * i] for i in range(6)]
        ident2 = cst[:, 896:960]
        causal = cst[:, 960:1088]
        far = cst[:, 1088:1344]
        prm = at("params", 24 + 5.5, [P, 256])
        stat = at("stats", 24 + 6.5, [P, 384])
        gain = {n: prm[:, 8 * i:8 * i + 8] for i, n in enumerate(
            ("pre_norm_gain", "post_norm_gain", "a_pre_g_2", "a_post_g_2", "kv_norm_g_2", "b_pre_g_2", "b_post_g_2"))}
        mix = prm[:, 56:69]
        chan = {n: prm[:, 69 + 4 * i:73 + 4 * i] for i, n in enumerate(
            ("rwkv_w0", "rwkv_a0", "rwkv_k_k", "rwkv_k_a", "rwkv_r_k", "rwkv_ln_w", "rwkv_ln_b"))}
        ln_g, ln_b = prm[:, 97:113], prm[:, 113:129]
        half_w0, half_a0 = prm[:, 132:136], prm[:, 136:140]
        sink, neg_sink = prm[:, 144:160], prm[:, 160:176]

        h1hi, h1lo = at("h1_hi", 32, [P, KT, T], F32R), at("h1_lo", 64, [P, KT, T], F32R)
        xt = at("x_rows", 96, [P, 8, D])
        sq0 = at("x_squares", 128, [P, D])
        hot_sb = at("hot_sb", 136, [33, GROUPS, LINE])
        rb33 = at("bias_table", 142, [33, 24])
        prm_rows, prm_rows2 = at("param_rows", 176, [113, P]), at("param_rows2", 177, [16, P])
        lines = at("bias_lines", 184, [8, GROUPS, LINE])
        qT, kT = at("q_t", 128, [P, 2, T]), at("k_t", 136, [P, 2, T])
        vT = at("v_t", 144, [P, T])
        vaug = at("v_and_ones", 148, [P, 2, 8, 192])
        bias_t = at("bias_tile", 160, [P, 2, 2, 256])
        negl = at("neg_logits", 164, [P, 4, 256])
        prob = at("prob", 168, [P, 4, 256])
        ptsb = at("prob_t_sb", 172, [P, 4, 256])
        accu = at("num_den", 176, [P, 2, T])
        nmax = at("neg_max", 184, [P, 2, T])
        nnew = at("neg_max_new", 192, [P, HALF])
        eab = at("rescale", 194, [P, 2, HALF])
        zs = at("z_silu", 198, [P, T])
        og = at("o_gated", 202, [P, T])
        rd = at("recip_den", 96, [P, T])
        t1 = at("scaled_new", 100, [P, HALF])
        negm = stat[:, 64:88]
        upw = at("lora_up", 126, [P, 512])
        oF = at("o_f32", 96, [P, 8, T])
        lora = at("lora", 96, [P, T])
        reset = at("chunk_reset", 100, [P, T])
        bon = at("bonus", 104, [P, T])
        yT = at("y_t", 108, [P, T])
        AM = at("a_mats", 128, [P, 2, NCH, 3, C])
        BK = at("b_k", 152, [P, NCH, 2, C])
        vpad = at("v_padded", 160, [P, C + T + C])
        rawt = at("rwkv_raw", 164.5, [P, 1 + T])
        rT, rkT = at("r_t", 169, [P, T]), at("rk_t", 173, [P, T])
        t0, tb = at("tmp0", 177, [P, T]), at("tmp1", 181, [P, T])
        logw, cum = at("log_decay", 185, [P, T]), at("cum_decay", 189, [P, T])
        aT, kk = at("a_t", 193, [P, T]), at("kk_t", 197, [P, T])
        ec = at("e_cum", 201, [P, T])
        BKt = at("bk_rows", 164.5, [P, NCH, P])
        SV = at("state_and_v", 172.5, [P, 2, 2, NCH, C])
        Tm, TT = at("inv", 188.5, [P, NCH, C]), at("inv_t", 192.5, [P, NCH, C])
        Xs = at("inv_x", 196.5, [P, NCH, C])
        AmT = at("a_level", 152, [P, NCH, C])
        Aab = at("a_ab", 200.5, [P, NCH, C])
        xs = at("scan_x", 205, [P, C])
        se = at("scan_state", 205.5, [P, C])
        e_end = stat[:, 96:112]
        yc, ysq = at("y_centred", 164.5, [P, T]), at("y_squares", 168.5, [P, T])
        zr = at("zr_silu", 173, [P, T])
        ohi, olo = at("o_hi", 128, [P, 8, T], F32R), at("o_lo", 96, [P, 8, T], F32R)
        merged = at("merged", 160, [P, KT, T])
        tga, tgr = at("tanh_ga", 192, [P, T]), at("tanh_gr", 196, [P, T])
        m1 = at("merge_part", 200, [P, T])
        mhi, mlo = at("merged_hi", 32, [P, KT, T], F32R), at("merged_lo", 64, [P, KT, T], F32R)
        y1 = at("block1_out", 96, [P, KT, T])
        xt2 = at("x_rows_again", 160, [P, 8, D])
        nsq = at("norm_squares", 192, [P, T])
        nsum = at("norm_sum", 196, [P, T])
        nrs = at("norm_rstd", 200, [P, T])
        h2hi, h2lo = at("h2_hi", 32, [P, KT, T], F32R), at("h2_lo", 64, [P, KT, T], F32R)
        vln = at("mlp_v", 128, [P, 8, AW])
        wsT = at("ws_t", 96, [P, 8, P])
        rowsum = at("ws_rowsum", 100, [P, 8, P])
        bsb = at("bs_rows", 104, [P, 8, P])
        wsr = at("ws_raw", 108, [P, 8, P])
        btile = at("b_tile", 112, [P, P])
        zg = at("mlp_z", 116, [P, T])
        ug = at("mlp_u", 192, [P, T])
        sg = at("mlp_s", 196, [P, T])
        vg = at("mlp_vg", 200, [P, T])
        yhi, ylo = at("mlp_y_hi", 32, [P, 16, T], F32R), at("mlp_y_lo", 128, [P, 8, AW], F32R)
        y2 = at("block2a_out", 96, [P, KT, T])
        res = at("residual", 128, [P, KT, T])
        kvhi, kvlo = at("hkv_hi", 128, [P, KT, T], F32R), at("hkv_lo", 160, [P, KT, T], F32R)
        h3hi, h3lo = at("h3_hi", 32, [P, KT, T], F32R), at("h3_lo", 64, [P, KT, T], F32R)
        kd = at("k_dup", 96, [P, 4, T])
        vt2 = at("v_rows", 112, [P, 8, 256])
        q2 = at("q2_t", 120, [P, 2, T])
        v2T = at("v2_t", 192, [P, T])
        ys = at("swa_y", 128, [P, QP, T])
        zs2 = at("z2_silu", 160, [P, 2, T])
        neg2 = at("neg_logits2", 168, [P, 4, 256])
        pr2 = at("prob2", 172, [P, 4, 256])
        pts2 = at("prob2_t", 176, [P, 4, 256])
        alibi = at("alibi_tile", 180, [P, 2, 2, 256])
        yshi, yslo = at("swa_y_hi", 32, [P, QP, T], F32R), at("swa_y_lo", 128, [P, QP, T], F32R)
        y3 = at("block2b_out", 64, [P, KT, T])
        x3 = at("x3_again", 160, [P, KT, T])
        orow = at("out_rows", 96, [P, 8, D])

        lines_d = nc.dram_tensor("lines_scratch", (GROUPS, 8, P, LINE), F32).ap()
        oA_d = nc.dram_tensor("attn_out_scratch", (PAIRS, P, T), F32).ap()
        x2_d = nc.dram_tensor("x2_scratch", (P, KT, T), F32).ap()
        x3_d = nc.dram_tensor("x3_scratch", (P, KT, T), F32).ap()

        units = []

        def unit(name, w, rows, col, nk=KT):
            units.append((name, w[rows:rows + nk * P, col:col + P].rearrange("(k p) n -> p k n", p=P), nk))

        w_in = d["w_in"][0]
        for p in range(PAIRS):
            for g in range(GROUPS):
                for off in (OFF_Q, OFF_K, OFF_V):
                    unit("qkv", w_in, 0, off + g * ATTN + p * P)
            unit("za", w_in, 0, OFF_ZA + p * P)
        U_R = len(units)
        unit("lora", w_in, 0, OFF_LORA)
        for p in range(PAIRS):
            for off in (OFF_R, OFF_RK, OFF_RV, OFF_ZR):
                unit("rwkv", w_in, 0, off + p * P)
        U_M = len(units)
        for j in range(KT):
            unit("ga", w_in, 0, OFF_GA + j * P)
            unit("gr", w_in, 0, OFF_GR + j * P)
            unit("ua", d["w_up_attn"][0], 0, j * P, 4)
            unit("ur", d["w_up_rwkv"][0], 0, j * P, 4)
        U_O = len(units)
        for j in range(KT):
            unit("wo", d["w_out"][0], 0, j * P)
        U_V = len(units)
        wa = d["a_w_in_2"][0]
        for i in range(16):
            unit("mv", wa, 0, AW + i * P)
        U_UZ = len(units)
        for i in range(16):
            unit("mu", wa, 0, i * P)
            unit("mz", wa, 0, 2 * AW + i * P)
        U_AO = len(units)
        for j in range(KT):
            unit("ao", d["a_w_out_2"][0], 0, j * P)
            unit("ao", d["a_w_out_2"][0], D, j * P)
        U_KV = len(units)
        for w in ("w_k_2", "w_v_2"):
            for j in range(2):
                unit("kv", d[w], 0, j * P)
        U_QZ = len(units)
        for i in range(QP):
            unit("q", d["b_w_in_2"][0], 0, i * P)
            unit("z", d["b_w_in_2"][0], 0, D + i * P)
        U_BO = len(units)
        for j in range(KT):
            unit("bo", d["b_w_out_2"][0], 0, j * P)
        U_END = len(units)
        outs_before, n = [], 0
        for u in range(U_END):
            outs_before.append(n)
            n += not (U_AO <= u < U_KV and (u - U_AO) % 2 == 0)
        last_unit = {0: 0, 1: U_R, 2: U_M, 3: U_V, 4: U_KV, 5: U_END}.get(stop, U_END)

        quads = [(p, g, hh, t) for p in range(PAIRS) for g in range(GROUPS) for hh in range(2) for t in range(2)]
        slot_of = {20 * p + 6 * g + 7 + 2 * hh + t: c for c, (p, g, hh, t) in enumerate(quads)}
        v_slot = {20 * p + 6 * g + 7: 3 * p + g for p in range(PAIRS) for g in range(GROUPS)}
        A_SLOTS = 20 * PAIRS
        A_END = 20 * PAIRS + 5

        def key_blocks(g, n):
            first = n == 0 if g == 0 else (n % 2 == 0 if g == 1 else True)
            return (1,) if first else (0, 1)

        def runs(g, t):
            if g == 0:
                return [(slice(0, 1), 1), (slice(1, 4), 0)] if t == 0 else [(slice(0, 4), 0)]
            return [(slice(0, 4, 2), 1), (slice(1, 4, 2), 0)] if g == 1 else [(slice(0, 4), 1)]

        def natural(ap, g, t):
            if g == 0:
                return ap[:, 512 * t:512 * t + 512]
            r = DILATION[g]
            return ap.rearrange("p (l r) -> p r l", r=r)[:, r // 2 * t:r // 2 * (t + 1), :]

        def permuted(ap, g):
            return ap if g == 0 else ap.rearrange("p (r l) -> p r l", r=DILATION[g] // 2)

        def perm_half(ap, g, h):
            if g == 0:
                return ap[:, HALF * h:HALF * h + HALF]
            r = DILATION[g]
            n = HALF // r
            return ap.rearrange("p (r l) -> p l r", r=r)[:, n * h:n * h + n, :]

        def nat_half(ap, g):
            return ap if g == 0 else ap.rearrange("p (l r) -> p l r", r=DILATION[g])

        made = {}

        def E(name):
            if name not in made:
                made[name] = sem(name)
            return made[name]

        PART = {"o": 0, "m": 8, "h2": 16, "y": 24, "hkv": 40, "h3": 48, "ys": 56}
        w_raw = [E("w_raw0"), E("w_raw1")]
        g_full = [E("gemm_full0"), E("w_used")]
        w_used = g_full[1]
        g_evac = [E("gemm_evac0"), E("gemm_evac1")]
        bias_in = [E("bias_in0"), E("bias_in1")]
        block = ctx.enter_context(nc.Block())

        def wait(eng, name, n):
            if n > 0:
                eng.wait_ge(E(name), n)

        def emptied(u, h):
            return g_evac[h], outs_before[u] + 1

        def wait_full(eng, u, h):
            eng.wait_ge(g_full[h], u + 1)

        @block.sync
        def _(sp):
            for i in range(8):
                sp.dma_start(xt[:, i, :], d["x"][0, i * P:(i + 1) * P, :]).then_inc(E(f"x_in{i}"), 16)
            for u in range(last_unit):
                name, src, nk = units[u]
                if u >= 2:
                    sp.wait_ge(E("w_split"), u - 1)
                sp.dma_start(raw[:, u % 2, 0:nk, :], src).then_inc(w_raw[u % 2], 16)
                if u < U_R and u % 10 in (2, 5, 8):
                    p, g = u // 10, u % 10 // 3
                    gi = 3 * p + g
                    b = gi % 2
                    if gi < GROUPS:
                        sp.wait_ge(E(f"lines_out{gi}"), 16)
                    if gi >= 2:
                        sp.wait_ge(E("ttr_done"), 4 * (gi - 1))
                    o = (g * 8 + 2 * p) * P * LINE
                    if g < 2:
                        sp.dma_start(bias_t[:, b, :, :], bass.AP(lines_d.tensor, o + 127, [[LINE - 1, P], [P * LINE, 2], [1, 256]])).then_inc(bias_in[b], 16)
                    else:
                        for rr in range(2):
                            for cc in range(2):
                                start, step = (o + 255, LINE - 1) if rr == cc else (o + 320, 0)
                                sp.dma_start(bias_t[64 * rr:64 * rr + 64, b, :, P + 64 * cc:P + 64 * cc + 64],
                                             bass.AP(lines_d.tensor, start, [[step, 64], [P * LINE, 2], [1, 64]])).then_inc(bias_in[b], 16)
            if stop < 99:
                sp.wait_ge(E("finished"), 1)

        bias_need, cnt = [], [0, 0]
        for gi in range(12):
            cnt[gi % 2] += 64 if gi % 3 == 2 else 16
            bias_need.append(cnt[gi % 2])

        @block.gpsimd
        def _(pool):
            Q = Own(pool, E("pool_chain"))
            Q(pool.memset(vaug[:, :, :, 64:128], 1.0), E("v_ones"))
            for u in range(last_unit):
                nk, s = units[u][2], u % 2
                pool.wait_ge(w_raw[s], 16 * (u // 2 + 1))
                if u >= 2:
                    pool.wait_ge(w_used, u - 1)
                Q(pool.tensor_copy(whi[:, s, 0:nk, :], raw[:, s, 0:nk, :]), E("w_hi"))
                Q(pool.tensor_tensor(wlo[:, s, 0:nk, :], raw[:, s, 0:nk, :], whi[:, s, 0:nk, :].bitcast(F32), ALU.subtract), E("w_split"))

        @block.tensor
        def _(pe):
            def gemm_half(u, h, hi, lo, ready=None, start=True, stop_=True):
                nk, s = units[u][2], u % 2
                if h == 0:
                    pe.wait_ge(E("w_split"), u + 1)
                if start and outs_before[u]:
                    pe.wait_ge(g_evac[h], outs_before[u])
                for k in range(nk):
                    if ready:
                        ready(k, h)
                    first, last = start and k == 0, stop_ and k == nk - 1
                    pe.matmul(G[h][:], whi[:, s, k, :], hi(k, h), start=first, stop=False)
                    pe.matmul(G[h][:], whi[:, s, k, :], lo(k, h), start=False, stop=False)
                    m = pe.matmul(G[h][:], wlo[:, s, k, :], hi(k, h), start=False, stop=last)
                m.then_inc(g_full[h], 1)

            def moving(hi, lo):
                return (lambda k, h: hi[:, k, HALF * h:HALF * h + HALF]), (lambda k, h: lo[:, k, HALF * h:HALF * h + HALF])

            H1 = moving(h1hi, h1lo)

            wait(pe, "hot_in", 32)
            wait(pe, "hot_one", 1)
            for g in range(GROUPS):
                wait(pe, "line_sb", g)
                pe.matmul(PV[0:8, 0:LINE], rb33[:, 8 * g:8 * g + 8], hot_sb[:, g, :], start=True, stop=True).then_inc(E("line_full"), 1)
            wait(pe, "c_in", 16)
            wait(pe, "prm_in", 16 * 17)
            pe.transpose(MB[:, 0:113], prm_rows[:, :], ident[0:113, 0:113])
            pe.transpose(MB[:, 113:129], prm_rows2[:, :], ident[0:16, 0:16]).then_inc(E("prm_tr"), 1)
            for f in range(16):
                kk_, hf = f // 2, f % 2
                wait(pe, "x_scaled", 4 * hf + 4)
                wait(pe, "h1_lo", f - 1)
                for i in range(4):
                    m = pe.transpose(G[f % 2][:, i * P:(i + 1) * P], xt[:, 4 * hf + i, kk_ * P:(kk_ + 1) * P], ident)
                m.then_inc(E("x_tr"), 1)
            if stop == 0:
                return

            def v_rows(gi):
                u = 10 * (gi // 3) + 3 * (gi % 3) + 2
                for h in range(2):
                    pe.wait_ge(g_evac[h], outs_before[u] + 1)
                wait(pe, "pt_done", 4 * gi)
                for t in range(2):
                    for i in range(4):
                        m = pe.transpose(PT2[:, (4 * t + i) * P:(4 * t + i + 1) * P], vT[:, (4 * t + i) * P:(4 * t + i + 1) * P], ident)
                    m.then_inc(E("v_tr"), 1)

            def scores(c):
                p, g, hh, t = quads[c]
                gi = 3 * p + g
                for h in range(2):
                    pe.wait_ge(g_evac[h], outs_before[10 * p + 3 * g + 1] + 1)
                wait(pe, "ttr_done", c)
                rows = slice(64 * hh, 64 * hh + 64)
                for i in range(4):
                    n = 4 * t + i
                    b0 = key_blocks(g, n)[0]
                    m = pe.matmul(S2[:, i * 256 + b0 * P:i * 256 + 256], qT[rows, gi % 2, n * P:n * P + P],
                                  kT[rows, gi % 2, (n - 1 + b0) * P:(n + 1) * P], start=True, stop=True)
                m.then_inc(E("s_full"), 1)

            def transposes(c):
                p, g, hh, t = quads[c]
                pe.wait_ge(E("exp_done"), c + 1)
                wait(pe, "pt_done", c)
                pe.wait_ge(E("v_rows"), 2 * (3 * p + g) + 2)
                for i in range(4):
                    for b in key_blocks(g, 4 * t + i):
                        m = pe.transpose(PT2[:, i * 256 + b * P:i * 256 + b * P + P], prob[:, i, b * P:b * P + P], ident)
                m.then_inc(E("pt_full"), 1)

            def weighted(c):
                p, g, hh, t = quads[c]
                pe.wait_ge(E("pt_done"), c + 1)
                wait(pe, "pv_free", c)
                if c == 0:
                    pe.wait_ge(E("v_ones"), 1)
                for i in range(4):
                    n = 4 * t + i
                    bs = key_blocks(g, n)
                    for b in bs:
                        pe.matmul(PV[:, i * P:i * P + P], vaug[:, (3 * p + g) % 2, n - 1 + b, 64 * hh:64 * hh + P], ptsb[:, i, b * P:b * P + P],
                                  start=b == bs[0], stop=b == 1)
                for i in range(4):
                    col = c % 4 * 4 + i
                    m = pe.matmul(MB[:, i * P:i * P + P], negm[:, col:col + 1].to_broadcast([P, P]), ident, start=True, stop=True)
                m.then_inc(E("pv_full"), 1)

            def h1_ready(k, h):
                wait(pe, "h1_lo", 2 * k + h + 1)

            for s in range(A_END):
                if s in v_slot:
                    v_rows(v_slot[s])
                if s - 1 in slot_of:
                    transposes(slot_of[s - 1])
                if s - 2 in slot_of:
                    weighted(slot_of[s - 2])
                if s in slot_of:
                    scores(slot_of[s])
                if s < A_SLOTS:
                    if s < 2:
                        wait(pe, "h1_lo", 15 + s)
                    gemm_half(s // 2, s % 2, *H1)
            if stop == 1:
                return
            def mixed_unit(u):
                for h in range(2):
                    gemm_half(u, h, *H1)

            rows2 = (slice(0, 64), slice(64, 128))
            halves = (slice(0, HALF), slice(HALF, T))
            fill_banks = (S2[:, 0:HALF], S2[:, HALF:T], PT2[:, 0:HALF], PT2[:, HALF:T])
            mixed_unit(U_R)
            for p in range(PAIRS):
                u0 = U_R + 1 + 4 * p
                mixed_unit(u0)
                wait(pe, "lora_tanh", 1)
                wait(pe, "up_in", 32)
                wait(pe, "pair_done", p)
                for h in range(2):
                    m = pe.matmul(S2[:, halves[h]], upw[0:64, p * P:p * P + P], lora[0:64, halves[h]], start=True, stop=True)
                m.then_inc(E("lw_full"), 1)
                for h in range(2):
                    m = pe.matmul(PT2[:, halves[h]], upw[64:128, p * P:p * P + P], lora[64:128, halves[h]], start=True, stop=True)
                m.then_inc(E("a_full"), 1)
                mixed_unit(u0 + 1)
                mixed_unit(u0 + 2)
                wait(pe, "k_sq", p + 1)
                wait(pe, "lw_tanh", p + 1)
                for h in range(2):
                    m = pe.matmul(S2[:, halves[h]], blocks, t0[:, halves[h]], start=True, stop=True)
                m.then_inc(E("knorm_full"), 1)
                wait(pe, "rkr", p + 1)
                wait(pe, "a_tanh", p + 1)
                for h in range(2):
                    m = pe.matmul(PT2[:, halves[h]], blocks, tb[:, halves[h]], start=True, stop=True)
                m.then_inc(E("bonus_full"), 1)
                wait(pe, "ak_ready", p + 1)
                wait(pe, "bonus_done", p + 1)
                for f in range(8):
                    hh, cq = f // 4, f % 4
                    if f >= 4:
                        wait(pe, "amat_done", 8 * p + f - 3)
                    for i in range(4):
                        c = 4 * cq + i
                        m = pe.matmul(fill_banks[f % 4][:, i * P:i * P + P], BK[rows2[hh], c, :, :], AM[rows2[hh], hh, c, 0:3:2, :], start=True, stop=True)
                    m.then_inc(E("amat_full"), 1)
                for f in range(4):
                    wait(pe, "bk_rows", 4 * p + f - 1)
                    for i in range(4):
                        m = pe.transpose(PV[:, i * P:i * P + P], BK[:, 4 * f + i, :, :], ident) if f % 2 == 0 else \
                            pe.transpose(MB[:, i * P:i * P + P], BK[:, 4 * f + i, :, :], ident)
                    m.then_inc(E("bk_tr"), 1)
                for f in range(5):
                    bank = (PV, MB)[f % 2]
                    wait(pe, "bk_rows", 4 * p + 3 + f % 2)
                    wait(pe, "vr_rows", 5 * p + f - 1)
                    for w in range(4 * f, min(4 * f + 4, 17)):
                        m = pe.transpose(bank[:, (w % 4) * P:(w % 4) * P + P], vpad[:, C * w:C * w + P], ident)
                    m.then_inc(E("vr_tr"), 1)
                wait(pe, "a_level", 6 * p + 1)
                wait(pe, "amat_done", 8 * p + 8)
                for c in range(NCH):
                    for r in rows2:
                        m = pe.matmul(PT2[r, c * C:c * C + C], AmT[r, c, :], ident2[r, :], start=True, stop=True)
                m.then_inc(E("inv_first"), 1)
                for lv in range(1, 6):
                    wait(pe, "a_level", 6 * p + lv + 1)
                    wait(pe, "inv_sb", 6 * p + lv)
                    for c in range(NCH):
                        for r in rows2:
                            m = pe.matmul(S2[r, c * C:c * C + C], AmT[r, c, :], Tm[r, c, :], start=True, stop=True)
                    m.then_inc(E("invx_full"), 1)
                    wait(pe, "invx_sb", 5 * p + lv)
                    if lv < 5:
                        for c in range(NCH):
                            for r in rows2:
                                pe.matmul(PT2[r, c * C:c * C + C], TT[r, c, :], Xs[r, c, :], start=True, stop=True)
                    for c in range(NCH):
                        for r in rows2:
                            m = pe.matmul(S2[r, c * C:c * C + C], Xs[r, c, :], TT[r, c, :], start=True, stop=True)
                    m.then_inc(E("inv_full"), 1)
                wait(pe, "vr_rows", 5 * p + 5)
                wait(pe, "inv_sb", 6 * p + 6)
                for c in range(NCH):
                    n = NCH * p + c
                    wait(pe, "state", n + 1)
                    for hh, r in enumerate(rows2):
                        m = pe.matmul(PV[r, 0:C], AM[:, hh, c, 0, :], SV[:, hh, 0, c, :], start=True, stop=True)
                    m.then_inc(E("sx_full"), 1)
                    wait(pe, "sx_sb", n + 1)
                    for hh, r in enumerate(rows2):
                        m = pe.matmul(MB[r, 0:C], TT[r, c, :], xs[r, :], start=True, stop=True)
                    m.then_inc(E("su_full"), 1)
                    wait(pe, "su_even", n + 1)
                    wait(pe, "su_odd", n + 1)
                    if c < NCH - 1:
                        for hh, r in enumerate(rows2):
                            m = pe.matmul(PT2[r, 0:C], BKt[:, c, C * hh:C * hh + C], SV[:, hh, 1, c, :], start=True, stop=True)
                        m.then_inc(E("ss_full"), 1)
                    for hh, r in enumerate(rows2):
                        o = S2[r, c * C:c * C + C]
                        pe.matmul(o, SV[:, hh, 0, c, :], AM[:, hh, c, 2, :], start=True, stop=False)
                        m = pe.matmul(o, SV[:, hh, 1, c, :], AM[:, hh, c, 1, :], start=False, stop=True)
                    if c == 3 or c == 9:
                        gemm_half(u0 + 3, c // 9, *H1)
                m.then_inc(E("y_full"), 1)
                wait(pe, "y_sb", p + 1)
                for h in range(2):
                    m = pe.matmul(PT2[:, halves[h]], blocks, yT[:, halves[h]], start=True, stop=True)
                m.then_inc(E("mean_full"), 1)
                wait(pe, "y_sq", p + 1)
                for h in range(2):
                    m = pe.matmul(S2[:, halves[h]], blocks, ysq[:, halves[h]], start=True, stop=True)
                m.then_inc(E("var_full"), 1)
            if stop == 2:
                return

            OA, OR = moving(ohi[:, 0:4, :], olo[:, 0:4, :]), moving(ohi[:, 4:8, :], olo[:, 4:8, :])
            for j in range(KT):
                for i in range(2):
                    for h in range(2):
                        gemm_half(U_M + 4 * j + i, h, *H1)
                wait(pe, "low_part", PART["o"] + 8)
                for i, src in enumerate((OA, OR)):
                    for h in range(2):
                        gemm_half(U_M + 4 * j + 2 + i, h, *src)

            def sums_of_squares(n):
                wait(pe, "sq_summed", n)
                for h in range(2):
                    m = pe.matmul(S2[:, halves[h]], ones, nsum[:, halves[h]], start=True, stop=True)
                m.then_inc(E("sumsq_full"), 1)

            MG = moving(mhi, mlo)
            for j in range(KT):
                for h in range(2):
                    gemm_half(U_O + j, h, *MG, ready=(lambda k, h: wait(pe, "low_part", PART["m"] + k + 1)) if j == 0 and h == 0 else None)
            sums_of_squares(1)
            for n in range(8):
                wait(pe, f"x_in{n}", 32)
            wait(pe, "norm_var", 1)
            for k in range(KT):
                wait(pe, "x2", k - 1)
                bank = (PT2, S2)[k % 2]
                for i in range(8):
                    m = pe.transpose(bank[:, i * P:i * P + P], xt2[:, i, k * P:k * P + P], ident)
                m.then_inc(E("xb_tr"), 1)
            wait(pe, "x2", 8)
            sums_of_squares(2)
            if stop == 3:
                return

            H2 = moving(h2hi, h2lo)

            def v_rows_of(i):
                for h in range(2):
                    pe.wait_ge(g_evac[h], outs_before[U_V + i] + 1)
                wait(pe, "vln_rows", 2 * i)
                for t in range(2):
                    for n in range(4):
                        m = pe.transpose(PT2[:, (4 * t + n) * P:(4 * t + n + 1) * P], vg[:, (4 * t + n) * P:(4 * t + n + 1) * P], ident)
                    m.then_inc(E("vg_tr"), 1)

            for i in range(16):
                rdy = (lambda k, h: wait(pe, "low_part", PART["h2"] + k + 1)) if i == 0 else None
                gemm_half(U_V + i, 0, *H2, ready=rdy)
                if i:
                    v_rows_of(i - 1)
                gemm_half(U_V + i, 1, *H2, ready=rdy)
                if i == 1:
                    wait(pe, "ws_in", 32)
                    for g in range(8):
                        m = pe.transpose(S2[:, g * P:g * P + P], wsr[:, g, :], ident)
                    m.then_inc(E("ws_tr"), 1)
                    wait(pe, "ws_t", 1)
                    for h in range(2):
                        m = pe.matmul(S2[:, halves[h]], ones, wsT[:, 4 * h:4 * h + 4, :], start=True, stop=True)
                    m.then_inc(E("rowsum_full"), 1)
            gemm_half(U_UZ, 0, *H2)
            v_rows_of(15)
            wait(pe, "rowsum", 1)
            for i in range(16):
                for h in range(2):
                    if i or h:
                        gemm_half(U_UZ + 2 * i, h, *H2)
                wait(pe, "v_normed", 8)
                wait(pe, "s_sb", i)
                for n in range(8):
                    m = pe.matmul(S2[:, n * P:n * P + P], vln[:, n, i * P:i * P + P], wsT[:, i // 2, :], start=True, stop=True)
                m.then_inc(E("sgu_full"), 1)
                for h in range(2):
                    gemm_half(U_UZ + 2 * i + 1, h, *H2)

            def y_ready(k0):
                return lambda k, h: wait(pe, "low_part", PART["y"] + k0 + k + 1)

            for j in range(KT):
                for kh in range(2):
                    u = U_AO + 2 * j + kh
                    src = (lambda k, h, kh=kh: yhi[:, 8 * kh + k, HALF * h:HALF * h + HALF],
                           lambda k, h, kh=kh: ylo[:, 4 * h:4 * h + 4, (8 * kh + k) * P:(8 * kh + k + 1) * P])
                    for h in range(2):
                        gemm_half(u, h, *src, ready=y_ready(8 * kh) if j == 0 else None, start=kh == 0, stop_=kh == 1)
            sums_of_squares(3)
            sums_of_squares(4)
            if stop == 4:
                return

            HKV = moving(kvhi, kvlo)
            H3 = moving(h3hi, h3lo)
            for j in range(4):
                for h in range(2):
                    gemm_half(U_KV + j, h, *HKV, ready=(lambda k, h: wait(pe, "low_part", PART["hkv"] + k + 1)) if j == 0 else None)
                if j >= 2:
                    for h in range(2):
                        pe.wait_ge(g_evac[h], outs_before[U_KV + j] + 1)
                    wait(pe, "v2_rows", j - 2)
                    for n in range(8):
                        m = pe.transpose(PT2[:, n * P:n * P + P], v2T[:, n * P:n * P + P], ident)
                    m.then_inc(E("v2_tr"), 1)

            def scores2(c):
                i, hh, t = c // 4, c // 2 % 2, c % 2
                for h in range(2):
                    pe.wait_ge(g_evac[h], outs_before[U_QZ + 2 * i] + 1)
                wait(pe, "ttr2_done", c)
                r = rows2[hh]
                for ti in range(4):
                    n = 4 * t + ti
                    b0 = 1 if n == 0 else 0
                    m = pe.matmul(S2[:, ti * 256 + b0 * P:ti * 256 + 256], q2[r, i % 2, n * P:n * P + P], kd[r, i // 2, (n - 1 + b0) * P:(n + 1) * P],
                                  start=True, stop=True)
                m.then_inc(E("s2_full"), 1)

            def transposes2(c):
                t = c % 2
                wait(pe, "pn_done", c + 1)
                wait(pe, "pt2_done", c)
                for ti in range(4):
                    for b in ((1,) if 4 * t + ti == 0 else (0, 1)):
                        m = pe.transpose(PT2[:, ti * 256 + b * P:ti * 256 + b * P + P], pr2[:, ti, b * P:b * P + P], ident)
                m.then_inc(E("pt2_full"), 1)

            def weighted2(c):
                i, hh, t = c // 4, c // 2 % 2, c % 2
                wait(pe, "pt2_done", c + 1)
                wait(pe, "pv2_free", c)
                for ti in range(4):
                    n = 4 * t + ti
                    bs = (1,) if n == 0 else (0, 1)
                    for b in bs:
                        m = pe.matmul(PV[rows2[hh], ti * P:ti * P + P], vt2[:, n - 1 + b, 64 * (i // 2):64 * (i // 2) + 64], pts2[:, ti, b * P:b * P + P],
                                      start=b == bs[0], stop=b == 1)
                m.then_inc(E("pv2_full"), 1)

            wait(pe, "v2_rows", 2)
            for s in range(4 * QP + 5):
                c = s - 3
                if 0 <= c - 1 < 4 * QP:
                    transposes2(c - 1)
                if 0 <= c - 2 < 4 * QP:
                    weighted2(c - 2)
                if 0 <= c < 4 * QP:
                    scores2(c)
                if s < 4 * QP:
                    gemm_half(U_QZ + s // 2, s % 2, *H3, ready=(lambda k, h: wait(pe, "low_part", PART["h3"] + k + 1)) if s == 0 else None)
            YS = moving(yshi, yslo)
            for j in range(KT):
                for h in range(2):
                    gemm_half(U_BO + j, h, *YS, ready=(lambda k, h: wait(pe, "low_part", PART["ys"] + k + 1)) if j == 0 else None)
            sums_of_squares(5)
            wait(pe, "x4", 8)
            for n in range(8):
                wait(pe, "rows_out", n - 1)
                bank = (PT2, S2)[n % 2]
                for k in range(KT):
                    m = pe.transpose(bank[:, k * P:k * P + P], y3[:, k, n * P:n * P + P], ident)
                m.then_inc(E("out_tr"), 1)

        @block.vector
        def _(dve):
            V = Own(dve, E("dve_chain"))
            v = nc.vector
            V(v.memset(rb33[32:33, :], 1.0), E("hot_one"))
            wait(dve, "squares", 8)
            V(v.tensor_scalar(stat[:, 8:16], stat[:, 0:8], 1.0 / D, EPS, ALU.mult, ALU.add), E("mean_sq0"))
            wait(dve, "sqrt0", 1)
            V(v.reciprocal(stat[:, 8:16], stat[:, 8:16]))
            for i in range(8):
                V(v.tensor_scalar(xt[:, i, :], xt[:, i, :], stat[:, 8 + i:9 + i], None, ALU.mult), E("x_scaled"))
            for f in range(16):
                kk_, hf = f // 2, f % 2
                dst = slice(HALF * hf, HALF * hf + HALF)
                wait(dve, "h1_hi", f + 1)
                wait(dve, "prm_sb", 1)
                V(v.scalar_tensor_tensor(h1lo[:, kk_, dst], G[f % 2][:], gain["pre_norm_gain"][:, kk_:kk_ + 1],
                                         h1hi[:, kk_, dst].bitcast(F32), ALU.mult, ALU.subtract), E("h1_lo"))
            if stop == 0:
                V(v.memset(stat[:, 383:384], 0.0), E("finished"))
                return

            def v_rows(gi):
                if gi >= 2:
                    dve.wait_ge(E("pv_full"), 4 * (gi - 1))
                wait(dve, "v_ones", 1)
                for t in range(2):
                    dve.wait_ge(E("v_tr"), 2 * gi + t + 1)
                    dst = vaug[:, gi % 2, 4 * t:4 * t + 4, :].rearrange("p n (a c) -> p n a c", a=3)[:, :, 0:3:2, :]
                    V(v.tensor_copy(dst, PT2[:, HALF * t:HALF * t + HALF].rearrange("p (n a c) -> p n a c", n=4, a=2)), E("v_rows"))

            def biased(c):
                p, g, hh, t = quads[c]
                gi = 3 * p + g
                dve.wait_ge(E("s_full"), c + 1)
                dve.wait_ge(bias_in[gi % 2], bias_need[gi])
                wait(dve, "exp_done", c)
                wait(dve, "pv_full", c - 3)
                for i in range(4):
                    lo = key_blocks(g, 4 * t + i)[0] * P
                    col = c % 4 * 4 + i
                    V(v.tensor_tensor_reduce(out=negl[:, i, lo:256], in0=S2[:, i * 256 + lo:i * 256 + 256], in1=bias_t[:, gi % 2, hh, lo:256],
                                             scale=-1.0, scalar=3e38, op0=ALU.add, op1=ALU.min, accum_out=negm[:, col:col + 1]),
                      E("ttr_done") if i == 3 else None)

            def merge(c):
                p, g, hh, t = quads[c]
                dve.wait_ge(E("pv_full"), c + 1)
                num, nm = natural(accu[:, hh, :], g, t), natural(nmax[:, hh, :], g, t)
                new, newm = permuted(PV[:], g), permuted(MB[:], g)
                if g == 0:
                    V(v.tensor_copy(num, new))
                    V(v.tensor_copy(nm, newm), E("pv_free"))
                    return
                k = sum(1 for q in quads[:c] if q[1]) + 1
                nn, ea, eb = (permuted(x, g) for x in (nnew[:], eab[:, 0, :], eab[:, 1, :]))
                V(v.tensor_tensor(nn, nm, newm, ALU.min))
                V(v.tensor_tensor(ea, nn, nm, ALU.subtract))
                V(v.tensor_tensor(eb, nn, newm, ALU.subtract), E("ab_ready"))
                if g == 1:
                    V(v.tensor_copy(nm, nn))
                dve.wait_ge(E("eab_done"), k)
                V(v.tensor_tensor(permuted(t1[:], g), new, eb, ALU.mult), E("pv_free"))
                V(v.tensor_tensor(num, num, ea, ALU.mult))
                V(v.tensor_tensor(num, num, permuted(t1[:], g), ALU.add))

            def finish(p):
                lo, hi = slice(0, 64), slice(64, 128)
                wait(dve, "oa_out", 16 * p)
                V(v.reciprocal(rd[lo, :], accu[hi, 0, :]))
                V(v.reciprocal(rd[hi, :], accu[lo, 1, :]))
                V(v.tensor_tensor(og[lo, :], accu[lo, 0, :], rd[lo, :], ALU.mult))
                V(v.tensor_tensor(og[hi, :], accu[hi, 1, :], rd[hi, :], ALU.mult))
                V(v.scalar_tensor_tensor(og[:], og[:], 0.5, zs[:], ALU.mult, ALU.mult), E("fin_done"))

            for s in range(A_END):
                if s in v_slot:
                    v_rows(v_slot[s])
                if s in slot_of:
                    biased(slot_of[s])
                if s - 2 in slot_of:
                    c = slot_of[s - 2]
                    merge(c)
                    if c % 12 == 11:
                        finish(c // 12)
                if s < A_SLOTS:
                    u, h = s // 2, s % 2
                    p, r = u // 10, u % 10
                    if r % 3 == 2 and r < 9:
                        gi = 3 * p + r // 3
                        wait_full(dve, u, h)
                        wait(dve, "v_tr", 2 * gi)
                        V(v.tensor_copy(perm_half(vT[:], r // 3, h), nat_half(G[h][:], r // 3)), emptied(u, h))
                    elif r == 9:
                        z = zs[:, HALF * h:HALF * h + HALF]
                        dve.wait_ge(E("z_tanh"), 2 * p + h + 1)
                        V(v.scalar_tensor_tensor(z, z, 1.0, G[h][:], ALU.add, ALU.mult), emptied(u, h))
            if stop == 1:
                wait(dve, "oa_out", 64)
                V(v.memset(stat[:, 383:384], 0.0), E("finished"))
                return
            lo_, hi_ = slice(0, 64), slice(64, 128)
            rows2 = (lo_, hi_)
            krows = (hi_, lo_)
            V(v.memset(reset[:], 1.0))
            V(v.memset(reset[:, 0:T:C], 0.0))
            half_rate = -0.5 * math.exp(-0.5)

            def mixed(n, dst, col):
                u = U_R if n == 0 else U_R + 1 + 4 * ((n - 1) // 3) + (n - 1) % 3
                for h in range(2):
                    dve.wait_ge(g_evac[h], outs_before[u] + 1)
                V(v.tensor_tensor(tb[:], rawt[:, 0:T], rawt[:, 1:1 + T], ALU.subtract))
                V(v.scalar_tensor_tensor(dst, tb[:], mix[:, col:col + 1], rawt[:, 1:1 + T], ALU.mult, ALU.add), E("mixed"))

            V(v.memset(rawt[:, 0:1], 0.0))
            mixed(0, lora[:], 12)
            for p in range(PAIRS):
                one = slice(p, p + 1)
                V(v.memset(rawt[:, 0:1], 0.0), E("raw_zero"))
                V(v.memset(vpad[:, 0:C], 0.0))
                V(v.memset(vpad[:, C + T:], 0.0))
                for hh in range(2):
                    V(v.memset(AM[krows[hh], hh, :, 1, :], 0.0))
                mixed(1 + 3 * p, rT[:], p)
                mixed(2 + 3 * p, rkT[:], 4 + p)
                mixed(3 + 3 * p, vpad[:, C:C + T], 8 + p)
                wait(dve, "lw_tanh", p + 1)
                V(v.tensor_scalar(logw[:], logw[:], half_rate, half_rate, ALU.mult, ALU.add))
                wait(dve, "a_tanh", p + 1)
                V(v.tensor_scalar(aT[:], aT[:], 0.5, 0.5, ALU.mult, ALU.add))
                V(v.tensor_tensor_scan(out=cum[:], data0=reset[:], data1=logw[:], initial=0.0, op0=ALU.mult, op1=ALU.add))
                V(v.tensor_tensor(logw[:], cum[:], logw[:], ALU.subtract), E("cum"))
                wait(dve, "knorm_full", p + 1)
                V(v.tensor_scalar(tb[:], S2[:], 1e-24, None, ALU.max), E("knorm_sb"))
                wait(dve, "k_sqrt", p + 1)
                V(v.reciprocal(tb[:], tb[:]))
                V(v.scalar_tensor_tensor(kk[:], rkT[:], chan["rwkv_k_k"][:, one], tb[:], ALU.mult, ALU.mult))
                V(v.tensor_scalar(t0[:], aT[:], -1.0, chan["rwkv_k_a"][:, one], ALU.add, ALU.mult))
                V(v.scalar_tensor_tensor(rkT[:], t0[:], 1.0, rkT[:], ALU.add, ALU.mult))
                V(v.scalar_tensor_tensor(tb[:], rT[:], chan["rwkv_r_k"][:, one], rkT[:], ALU.mult, ALU.mult), E("rkr"))
                V(v.tensor_tensor(t0[:], kk[:], aT[:], ALU.mult))
                wait(dve, "exps", p + 1)
                V(v.tensor_copy(e_end, ec[:, C - 1:T:C]))

                def chunks(ap):
                    return ap.rearrange("p (c t) -> p c t", t=C)

                for hh, r in enumerate(rows2):
                    V(v.tensor_tensor(AM[r, hh, :, 2, :], chunks(rT[r, :]), chunks(ec[r, :]), ALU.mult))
                    V(v.scalar_tensor_tensor(AM[r, hh, :, 0, :], chunks(kk[r, :]), -1.0, chunks(logw[r, :]), ALU.mult, ALU.mult))
                    V(v.tensor_tensor(BK[r, :, hh, :], chunks(t0[r, :]), chunks(cum[r, :]), ALU.mult))
                    V(v.tensor_tensor(BK[r, :, 1 - hh, :], chunks(rkT[r, :]), chunks(cum[r, :]), ALU.mult), E("ak_pre") if hh == 0 else E("ak_ready"))
                wait(dve, "bonus_full", p + 1)
                V(v.tensor_tensor(bon[:], PT2[:], vpad[:, C:C + T], ALU.mult), E("bonus_done"))
                for f in range(8):
                    hh, cq = f // 4, f % 4
                    bank = (S2[:, 0:HALF], S2[:, HALF:T], PT2[:, 0:HALF], PT2[:, HALF:T])[f % 4].rearrange("p (c x t) -> p c x t", c=4, x=2)
                    cs = slice(4 * cq, 4 * cq + 4)
                    b, k = rows2[hh], krows[hh]

                    def masked(dst, src, m, signal=None):
                        V(v.tensor_tensor(dst, src, m.unsqueeze(1).to_broadcast([64, 4, C]), ALU.mult), signal)

                    wait(dve, "amat_full", 8 * p + f + 1)
                    masked(Aab[b, cs, :], bank[b, :, 0, :], mask_a[b, 0:C])
                    masked(AM[b, hh, cs, 1, :], bank[b, :, 1, :], mask_a[b, C:2 * C])
                    masked(AM[k, hh, cs, 0, :], bank[k, :, 0, :], mask_a[k, 0:C])
                    masked(AM[k, hh, cs, 2, :], bank[k, :, 1, :], mask_a[k, C:2 * C], E("amat_done"))
                for f in range(5):
                    bank = (PV, MB)[f % 2][:].rearrange("p (w x c) -> p w x c", w=4, x=2)
                    wait(dve, "vr_tr", 5 * p + f + 1)
                    w0, w1 = 4 * f, min(4 * f + 4, 17)
                    todo = []
                    for kind in range(2):
                        if w0 < 16:
                            todo.append((SV[hi_, 0, kind, w0:min(w1, 16), :], bank[hi_, 0:min(w1, 16) - w0, 0, :]))
                        s0 = 1 if w0 == 0 else 0
                        todo.append((SV[lo_, 1, kind, w0 + s0 - 1:w1 - 1, :], bank[lo_, s0:w1 - w0, 1, :]))
                    for i, (o, s_) in enumerate(todo):
                        V(v.tensor_copy(o, s_), E("vr_rows") if i == len(todo) - 1 else None)
                wait(dve, "bk_tr", 4 * p + 4)

                def level_of(i):
                    V(v.tensor_tensor(AmT[:], Aab[:], level[i].unsqueeze(1).to_broadcast([P, NCH, C]), ALU.mult), E("a_level"))

                flat = "p c t -> p (c t)"
                eye = ident2.unsqueeze(1).to_broadcast([P, NCH, C])
                level_of(0)
                V(v.tensor_tensor(TT[:], AmT[:], eye, ALU.add))
                wait(dve, "inv_first", p + 1)
                V(v.tensor_tensor(Tm[:], PT2[:].rearrange("p (c t) -> p c t", t=C), eye, ALU.add), E("inv_sb"))
                for lv in range(1, 6):
                    level_of(lv)
                    wait(dve, "invx_full", 5 * p + lv)
                    V(v.tensor_copy(Xs[:].rearrange(flat), S2[:]), E("invx_sb"))
                    wait(dve, "inv_full", 5 * p + lv)
                    if lv < 5:
                        V(v.tensor_tensor(Tm[:].rearrange(flat), Tm[:].rearrange(flat), PT2[:], ALU.add))
                    V(v.tensor_tensor(TT[:].rearrange(flat), TT[:].rearrange(flat), S2[:], ALU.add), E("inv_sb"))
                V(v.memset(SV[lo_, 0, 0, 0, :], 0.0))
                V(v.memset(SV[hi_, 1, 0, 0, :], 0.0), E("state"))
                for c in range(NCH):
                    n = NCH * p + c
                    wait(dve, "sx_full", n + 1)
                    V(v.tensor_copy(xs[:], PV[:, 0:C]), E("sx_sb"))
                    for hh, r in enumerate(rows2):
                        V(v.tensor_scalar(se[r, :], SV[r, hh, 0, c, :], e_end[r, c:c + 1], None, ALU.mult))
                    wait(dve, "su_full", n + 1)
                    V(v.tensor_copy(SV[lo_, 0, 1, c, :], MB[lo_, 0:C]), E("su_even"))
                    if c < NCH - 1:
                        wait(dve, "ss_full", 15 * p + c + 1)
                        for hh, r in enumerate(rows2):
                            V(v.scalar_tensor_tensor(SV[r, hh, 0, c + 1, :], PT2[r, 0:C], e_end[r, c:c + 1], se[r, :], ALU.mult, ALU.add),
                              E("state") if hh else None)
                wait(dve, "mean_full", p + 1)
                V(v.scalar_tensor_tensor(yc[:], PT2[:], -1.0 / C, yT[:], ALU.mult, ALU.add), E("y_centred"))
                wait(dve, "var_full", p + 1)
                V(v.tensor_scalar(ysq[:], S2[:], 1.0 / C, GN_EPS, ALU.mult, ALU.add), E("y_var"))
                wait(dve, "y_sd", p + 1)
                V(v.reciprocal(ysq[:], ysq[:]))
                V(v.scalar_tensor_tensor(yc[:], yc[:], chan["rwkv_ln_w"][:, one], ysq[:], ALU.mult, ALU.mult))
                V(v.scalar_tensor_tensor(yc[:], yc[:], chan["rwkv_ln_b"][:, one], bon[:], ALU.add, ALU.add))
                for h in range(2):
                    wait(dve, "zr_tanh", 2 * p + h + 1)
                    z = zr[:, HALF * h:HALF * h + HALF]
                    V(v.scalar_tensor_tensor(z, z, 1.0, G[h][:], ALU.add, ALU.mult), emptied(U_R + 4 + 4 * p, h))
                V(v.scalar_tensor_tensor(oF[:, 4 + p, :], yc[:], 0.5, zr[:], ALU.mult, ALU.mult), E("pair_done"))
            if stop == 2:
                wait(dve, "dbg_out", 16)
                V(v.memset(stat[:, 383:384], 0.0), E("finished"))
                return

            for i, k in enumerate((4, 5, 6, 7, 0, 1, 2, 3)):
                wait(dve, "high_part", PART["o"] + i + 1)
                V(v.tensor_tensor(olo[:, k, :], oF[:, k, :], ohi[:, k, :].bitcast(F32), ALU.subtract), E("low_part"))
            for j in range(KT):
                u = U_M + 4 * j
                for i, (gate, dst) in enumerate(((tga, m1), (tgr, tgr))):
                    for h in range(2):
                        cs = slice(HALF * h, HALF * h + HALF)
                        dve.wait_ge(g_evac[h], outs_before[u + i] + 1)
                        wait_full(dve, u + 2 + i, h)
                        V(v.scalar_tensor_tensor(dst[:, cs], gate[:, cs], 1.0, G[h][:], ALU.add, ALU.mult), emptied(u + 2 + i, h))
                V(v.tensor_tensor(merged[:, j, :], m1[:], tgr[:], ALU.add), E("merged"))
            for j in range(KT):
                wait(dve, "high_part", PART["m"] + j + 1)
                V(v.scalar_tensor_tensor(mlo[:, j, :], merged[:, j, :], 0.5, mhi[:, j, :].bitcast(F32), ALU.mult, ALU.subtract), E("low_part"))

            sq_seen = [0, 0, 0]

            def add_square(k):
                sq_seen[0] += 1
                wait(dve, "sq", sq_seen[0])
                if k == 0:
                    V(v.tensor_copy(nsum[:], nsq[:]), E("sq_used"))
                elif k < KT - 1:
                    V(v.tensor_tensor(nsum[:], nsum[:], nsq[:], ALU.add), E("sq_used"))
                else:
                    V(v.tensor_tensor(nsum[:], nsum[:], nsq[:], ALU.add), E("sq_summed"))

            def rstd():
                sq_seen[1] += 1
                wait(dve, "sumsq_full", sq_seen[1])
                V(v.tensor_scalar(nrs[:], S2[:], 1.0 / D, EPS, ALU.mult, ALU.add), E("norm_var"))
                wait(dve, "norm_sd", sq_seen[1])
                V(v.reciprocal(nrs[:], nrs[:]))

            h_seen = [0]

            def split_h(src, g, dst_lo, first, hi_buf):
                bufs = (nsq, nsum)
                for k in range(KT):
                    h_seen[0] += 1
                    b = bufs[k % 2]
                    V(v.scalar_tensor_tensor(b[:], src[:, k, :], g[:, k:k + 1], nrs[:], ALU.mult, ALU.mult), E("h_tmp"))
                    wait(dve, "high_part", first + k + 1)
                    V(v.tensor_tensor(dst_lo[:, k, :], b[:], hi_buf[:, k, :].bitcast(F32), ALU.subtract), E("low_part"))

            for j in range(KT):
                add_square(j)
            rstd()
            g_ = gain["post_norm_gain"]
            for k in range(KT):
                V(v.scalar_tensor_tensor(y1[:, k, :], y1[:, k, :], g_[:, k:k + 1], nrs[:], ALU.mult, ALU.mult))
                wait(dve, "xb_tr", k + 1)
                V(v.tensor_tensor(y1[:, k, :], y1[:, k, :], (PT2, S2)[k % 2][:], ALU.add), E("x2"))
                if k:
                    add_square(k - 1)
            add_square(KT - 1)
            rstd()
            split_h(y1, gain["a_pre_g_2"], h2lo, PART["h2"], h2hi)
            if stop == 3:
                wait(dve, "x2_out", 16)
                V(v.memset(stat[:, 383:384], 0.0), E("finished"))
                return

            for i in range(16):
                for t in range(2):
                    wait(dve, "vg_tr", 2 * i + t + 1)
                    V(v.tensor_copy(vln[:, 4 * t:4 * t + 4, i * P:i * P + P], PT2[:, HALF * t:HALF * t + HALF].rearrange("p (n c) -> p n c", n=4)),
                      E("vln_rows"))
                if i == 0:
                    wait(dve, "ws_tr", 1)
                    V(v.tensor_tensor(wsT[:], S2[:].rearrange("p (g t) -> p g t", g=8), causal.unsqueeze(1).to_broadcast([P, 8, P]), ALU.mult), E("ws_t"))
                    wait(dve, "rowsum_full", 1)
                    V(v.tensor_copy(rowsum[:], S2[:].rearrange("p (g t) -> p g t", g=8)), E("rowsum"))
            bn = stat[:, 128:320].rearrange("p (n s x) -> p n s x", n=8, s=4)
            mv = stat[:, 320:336].rearrange("p (n x) -> p n x", n=8)
            for n in range(8):
                for s in range(4):
                    V(v.bn_stats(bn[:, n, s, :], vln[:, n, HALF * s:HALF * s + HALF]))
                V(v.bn_aggr(mv[:, n, :], bn[:, n, :, :]))
            V(v.tensor_scalar(stat[:, 336:344], mv[:, :, 1], EPS, None, ALU.add), E("ln_var"))
            wait(dve, "ln_sd", 1)
            V(v.reciprocal(stat[:, 336:344], stat[:, 336:344]))
            for n in range(8):
                V(v.tensor_scalar(vln[:, n, :], vln[:, n, :], mv[:, n, 0:1], stat[:, 336 + n:337 + n], ALU.subtract, ALU.mult), E("v_normed"))
            wait(dve, "ws_in", 32)
            for i in range(16):
                g = i // 2
                V(v.scalar_tensor_tensor(btile[:], rowsum[:, g, :], ln_b[:, i:i + 1], bsb[:, g, :], ALU.mult, ALU.add))
                wait(dve, "sgu_full", i + 1)
                V(v.scalar_tensor_tensor(sg[:].rearrange("p (n t) -> p n t", n=8), S2[:].rearrange("p (n t) -> p n t", n=8), ln_g[:, i:i + 1],
                                         btile[:].unsqueeze(1).to_broadcast([P, 8, P]), ALU.mult, ALU.add), E("s_sb"))
                for h in range(2):
                    dve.wait_ge(g_evac[h], outs_before[U_UZ + 2 * i] + 1)
                V(v.tensor_tensor(sg[:], sg[:], ug[:], ALU.mult))
                for h in range(2):
                    wait(dve, "zg_tanh", 2 * i + h + 1)
                    z = zg[:, HALF * h:HALF * h + HALF]
                    V(v.scalar_tensor_tensor(z, z, 1.0, G[h][:], ALU.add, ALU.mult), emptied(U_UZ + 2 * i + 1, h))
                V(v.scalar_tensor_tensor(vln[:, :, i * P:i * P + P], sg[:].rearrange("p (n t) -> p n t", n=8), 0.5,
                                         zg[:].rearrange("p (n t) -> p n t", n=8), ALU.mult, ALU.mult), E("y_mlp"))
            for i in range(16):
                wait(dve, "high_part", PART["y"] + i + 1)
                V(v.tensor_tensor(ylo[:, :, i * P:i * P + P], vln[:, :, i * P:i * P + P], yhi[:, i, :].bitcast(F32).rearrange("p (n t) -> p n t", n=8),
                                  ALU.subtract), E("low_part"))
            for j in range(KT):
                add_square(j)
            rstd()
            wait(dve, "res_in", 16)
            g_ = gain["a_post_g_2"]
            for k in range(KT):
                V(v.scalar_tensor_tensor(y2[:, k, :], y2[:, k, :], g_[:, k:k + 1], nrs[:], ALU.mult, ALU.mult))
                V(v.tensor_tensor(y2[:, k, :], y2[:, k, :], res[:, k, :], ALU.add), E("x3"))
                if k:
                    add_square(k - 1)
            add_square(KT - 1)
            rstd()
            split_h(y2, gain["kv_norm_g_2"], kvlo, PART["hkv"], kvhi)
            split_h(y2, gain["b_pre_g_2"], h3lo, PART["h3"], h3hi)
            if stop == 4:
                wait(dve, "x3_out", 16)
                V(v.memset(stat[:, 383:384], 0.0), E("finished"))
                return

            for j in range(2):
                wait(dve, "v2_tr", j + 1)
                V(v.tensor_copy(vt2[:, :, j * P:j * P + P], PT2[:].rearrange("p (n c) -> p n c", n=8)), E("v2_rows"))

            def biased2(c):
                i, hh, t = c // 4, c // 2 % 2, c % 2
                wait(dve, "s2_full", c + 1)
                wait(dve, "exp2_done", c)
                for ti in range(4):
                    lo = P if 4 * t + ti == 0 else 0
                    col = c % 2 * 4 + ti
                    V(v.tensor_tensor_reduce(out=neg2[:, ti, lo:256], in0=S2[:, ti * 256 + lo:ti * 256 + 256], in1=alibi[:, i % 2, hh, lo:256],
                                             scale=-1.0, scalar=3e38, op0=ALU.add, op1=ALU.min, accum_out=negm[:, col:col + 1]))
                cols = slice(c % 2 * 4, c % 2 * 4 + 4)
                V(v.tensor_scalar(negm[:, cols], negm[:, cols], neg_sink[:, 2 * i + hh:2 * i + hh + 1], None, ALU.min), E("ttr2_done"))

            def normalised2(c):
                t = c % 2
                wait(dve, "exp2_done", c + 1)
                den, es = stat[:, 352:356], stat[:, 356:360]
                V(v.tensor_tensor(den, den, es, ALU.add))
                V(v.reciprocal(den, den))
                for ti in range(4):
                    lo = P if 4 * t + ti == 0 else 0
                    V(v.tensor_scalar(pr2[:, ti, lo:256], pr2[:, ti, lo:256], stat[:, 352 + ti:353 + ti], None, ALU.mult), E("pn_done") if ti == 3 else None)

            def gated2(c):
                i, hh, t = c // 4, c // 2 % 2, c % 2
                wait(dve, "pv2_full", c + 1)
                r, cs = rows2[hh], slice(HALF * t, HALF * t + HALF)
                V(v.scalar_tensor_tensor(ys[r, i, cs], PV[r, :], 0.5, zs2[r, i % 2, cs], ALU.mult, ALU.mult), E("pv2_free"))

            for s in range(4 * QP + 5):
                c = s - 3
                if s % 4 == 0 and s // 4 < QP:
                    i = s // 4
                    for hh in range(2):
                        slope = 2.0 ** (-8.0 * (2 * i + hh + 1) / 16)
                        V(v.tensor_scalar(alibi[:, i % 2, hh, :], far, -slope, None, ALU.mult))
                if 0 <= c - 1 < 4 * QP:
                    normalised2(c - 1)
                if 0 <= c < 4 * QP:
                    biased2(c)
                if 0 <= c - 2 < 4 * QP:
                    gated2(c - 2)
                if s < 4 * QP and s % 4 >= 2:
                    i, h = s // 4, s % 2
                    wait(dve, "z2_tanh", 2 * i + h + 1)
                    z = zs2[:, i % 2, HALF * h:HALF * h + HALF]
                    V(v.scalar_tensor_tensor(z, z, 1.0, G[h][:], ALU.add, ALU.mult), emptied(U_QZ + 2 * i + 1, h))
            V(v.memset(stat[:, 382:383], 0.0), E("ys_done"))
            for k in range(QP):
                wait(dve, "high_part", PART["ys"] + k + 1)
                V(v.tensor_tensor(yslo[:, k, :], ys[:, k, :], yshi[:, k, :].bitcast(F32), ALU.subtract), E("low_part"))
            for j in range(KT):
                add_square(j)
            rstd()
            wait(dve, "x3_in", 16)
            g_ = gain["b_post_g_2"]
            for k in range(KT):
                V(v.scalar_tensor_tensor(y3[:, k, :], y3[:, k, :], g_[:, k:k + 1], nrs[:], ALU.mult, ALU.mult))
                V(v.tensor_tensor(y3[:, k, :], y3[:, k, :], x3[:, k, :], ALU.add), E("x4"))

        @block.scalar
        def _(act):
            A = Own(act, E("act_chain"))
            a = nc.scalar
            act.dma_start(cst[:], d["shape_consts"]).then_inc(E("c_in"), 16)
            act.dma_start(hot_sb[:], d["bucket_hot"]).then_inc(E("hot_in"), 16)
            act.dma_start(rb33[0:32, :], d["rel_bias"]).then_inc(E("hot_in"), 16)
            n_prm, row = 0, 0
            vectors = [*gain, "rwkv_shift_mix", *chan, "a_ln_g_2", "a_ln_b_2"]
            for n in vectors:
                src = d[n] if n == "kv_norm_g_2" else d[n][0].rearrange("h c -> (h c)") if n == "rwkv_r_k" else d[n][0]
                k = src.shape[0] // P
                dst = prm_rows2[:, :] if n == "a_ln_b_2" else prm_rows[row:row + k, :]
                act.dma_start(dst, src.rearrange("(k p) -> k p", p=P)).then_inc(E("prm_in"), 16)
                n_prm, row = n_prm + 16, row + k
            act.dma_start(sink, d["b_sinks_2"].to_broadcast([P, 16])).then_inc(E("sink_in"), 16)
            for i in range(8):
                wait(act, f"x_in{i}", 16)
                A(a.activation(sq0[:], xt[:, i, :], ACT.Square, accum_out=stat[:, i:i + 1]), E("squares"))
            wait(act, "mean_sq0", 1)
            A(a.activation(stat[:, 8:16], stat[:, 8:16], ACT.Sqrt), E("sqrt0"))
            for g in range(GROUPS):
                wait(act, "line_full", g + 1)
                A(a.activation(lines[:, g, :], PV[0:8, 0:LINE], ACT.Copy), E("line_sb"))
                act.dma_start(lines_d[g], lines[:, g, :].unsqueeze(1).to_broadcast([8, P, LINE])).then_inc(E(f"lines_out{g}"), 16)
            wait(act, "prm_tr", 1)
            A(a.activation(prm[:, 0:129], MB[:, 0:129], ACT.Copy), E("prm_sb"))
            wait(act, "sink_in", 16)
            A(a.mul(half_w0, chan["rwkv_w0"], 0.5))
            A(a.mul(half_a0, chan["rwkv_a0"], 0.5))
            A(a.mul(neg_sink, sink, -1.0))
            for f in range(16):
                kk_, hf = f // 2, f % 2
                wait(act, "x_tr", f + 1)
                A(a.activation(h1hi[:, kk_, HALF * hf:HALF * hf + HALF], G[f % 2][:], ACT.Copy, scale=gain["pre_norm_gain"][:, kk_:kk_ + 1]), E("h1_hi"))
            for g in range(GROUPS):
                wait(act, f"lines_out{g}", 16)
            if stop == 0:
                return

            def copy_back(c):
                p, g, hh, t = quads[c]
                act.wait_ge(E("pt_full"), c + 1)
                wait(act, "pv_full", c)
                todo = runs(g, t)
                src = PT2[:].rearrange("p (n k) -> p n k", n=4)
                for j, (sl, b0) in enumerate(todo):
                    A(a.activation(ptsb[:, sl, b0 * P:256], src[:, sl, b0 * P:256], ACT.Copy), E("pt_done") if j == len(todo) - 1 else None)

            def exps(c):
                p, g, hh, t = quads[c]
                act.wait_ge(E("ttr_done"), c + 1)
                wait(act, "pt_full", c)
                for i in range(4):
                    lo = key_blocks(g, 4 * t + i)[0] * P
                    col = c % 4 * 4 + i
                    A(a.activation(prob[:, i, lo:256], negl[:, i, lo:256], ACT.Exp, bias=negm[:, col:col + 1], scale=-1.0),
                      E("exp_done") if i == 3 else None)

            for s in range(A_END + 1):
                if s >= 25 and (s - 25) % 20 == 0:
                    p = (s - 25) // 20
                    act.wait_ge(E("fin_done"), p + 1)
                    act.dma_start(oA_d[p], og[:]).then_inc(E("oa_out"), 16)
                if s - 1 in slot_of:
                    copy_back(slot_of[s - 1])
                if s in slot_of:
                    exps(slot_of[s])
                if s - 2 in slot_of and quads[slot_of[s - 2]][1]:
                    c = slot_of[s - 2]
                    k = sum(1 for q in quads[:c] if q[1]) + 1
                    act.wait_ge(E("ab_ready"), k)
                    A(a.activation(eab[:], eab[:], ACT.Exp), E("eab_done"))
                if s < A_SLOTS:
                    u, h = s // 2, s % 2
                    p, r = u // 10, u % 10
                    g, gi = r // 3, 3 * p + r // 3
                    if r == 9:
                        wait_full(act, u, h)
                        wait(act, "fin_done", p)
                        A(a.activation(zs[:, HALF * h:HALF * h + HALF], G[h][:], ACT.Tanh, scale=0.5), E("z_tanh"))
                    elif r % 3 < 2:
                        wait_full(act, u, h)
                        if gi >= 2:
                            act.wait_ge(E("s_full"), 4 * (gi - 1))
                        dst = (qT, kT)[r % 3]
                        A(a.activation(perm_half(dst[:, gi % 2, :], g, h), nat_half(G[h][:], g), ACT.Copy, scale=(0.125, 1.0)[r % 3]), emptied(u, h))
            wait(act, "oa_out", 64)
            if stop == 1:
                return
            act.dma_start(upw[0:64, :], d["rwkv_w_up"][0]).then_inc(E("up_in"), 16)
            act.dma_start(upw[64:128, :], d["rwkv_a_up"][0]).then_inc(E("up_in"), 16)
            hi_ = slice(64, 128)

            def raw_half(u, n):
                wait(act, "mixed", n)
                if n % 3 == 1:
                    wait(act, "raw_zero", n // 3 + 1)
                for h in range(2):
                    wait_full(act, u, h)
                    A(a.activation(rawt[:, 1 + HALF * h:1 + HALF * h + HALF], G[h][:], ACT.Copy), emptied(u, h))

            raw_half(U_R, 0)
            wait(act, "mixed", 1)
            A(a.activation(lora[0:64, :], lora[0:64, :], ACT.Tanh), E("lora_tanh"))
            for p in range(PAIRS):
                one = slice(p, p + 1)
                u0 = U_R + 1 + 4 * p
                raw_half(u0, 1 + 3 * p)
                wait(act, "lw_full", p + 1)
                A(a.activation(logw[:], S2[:], ACT.Tanh, bias=half_w0[:, one], scale=0.5), E("lw_tanh"))
                wait(act, "a_full", p + 1)
                A(a.activation(aT[:], PT2[:], ACT.Tanh, bias=half_a0[:, one], scale=0.5), E("a_tanh"))
                raw_half(u0 + 1, 2 + 3 * p)
                raw_half(u0 + 2, 3 + 3 * p)
                A(a.activation(t0[:], rkT[:], ACT.Square, scale=chan["rwkv_k_k"][:, one]), E("k_sq"))
                wait(act, "cum", p + 1)
                A(a.activation(ec[:], cum[:], ACT.Exp))
                A(a.activation(logw[:], logw[:], ACT.Exp))
                A(a.activation(cum[:], cum[:], ACT.Exp, scale=-1.0), E("exps"))
                wait(act, "knorm_sb", p + 1)
                A(a.activation(tb[:], tb[:], ACT.Sqrt), E("k_sqrt"))
                wait(act, "bonus_done", p + 1)
                for f in range(4):
                    wait(act, "bk_tr", 4 * p + f + 1)
                    A(a.activation(BKt[:, 4 * f:4 * f + 4, :], (PV, MB)[f % 2][:].rearrange("p (n c) -> p n c", n=4), ACT.Copy), E("bk_rows"))
                for c in range(NCH):
                    wait(act, "su_full", NCH * p + c + 1)
                    if c == 0:
                        wait(act, "vr_rows", 5 * p + 5)
                    A(a.activation(SV[hi_, 1, 1, c, :], MB[hi_, 0:C], ACT.Copy), E("su_odd"))
                wait(act, "y_full", p + 1)
                A(a.activation(yT[:], S2[:], ACT.Copy), E("y_sb"))
                for h in range(2):
                    wait_full(act, u0 + 3, h)
                    A(a.activation(zr[:, HALF * h:HALF * h + HALF], G[h][:], ACT.Tanh, scale=0.5), E("zr_tanh"))
                wait(act, "y_centred", p + 1)
                A(a.activation(ysq[:], yc[:], ACT.Square), E("y_sq"))
                wait(act, "y_var", p + 1)
                A(a.activation(ysq[:], ysq[:], ACT.Sqrt), E("y_sd"))
            if stop == 2:
                o_dbg = nc.dram_tensor("o_dbg", (P, 4, T), F32).ap()
                wait(act, "pair_done", 4)
                act.dma_start(o_dbg, oF[:, 4:8, :]).then_inc(E("dbg_out"), 16)
                wait(act, "dbg_out", 16)
                return

            wait(act, "pair_done", 4)
            act.dma_start(oF[:, 0:4, :], oA_d.rearrange("k p n -> p k n")).then_inc(E("oa_in"), 16)
            for i, k in enumerate((4, 5, 6, 7, 0, 1, 2, 3)):
                if k == 0:
                    wait(act, "oa_in", 16)
                A(a.activation(ohi[:, k, :], oF[:, k, :], ACT.Copy), E("high_part"))
            for j in range(KT):
                u = U_M + 4 * j
                wait(act, "merged", j)
                for i, dst in enumerate((tga, tgr)):
                    for h in range(2):
                        wait_full(act, u + i, h)
                        A(a.activation(dst[:, HALF * h:HALF * h + HALF], G[h][:], ACT.Tanh, scale=0.5), emptied(u + i, h))
            wait(act, "merged", 8)
            act.wait_ge(w_used, U_O - 2)
            for j in range(KT):
                A(a.activation(mhi[:, j, :], merged[:, j, :], ACT.Copy, scale=0.5), E("high_part"))
            wait(act, "low_part", PART["m"] + 8)
            for n in range(8):
                act.dma_start(xt2[:, n, :], d["x"][0, n * P:(n + 1) * P, :]).then_inc(E(f"x_in{n}"), 16)

            sq_n = [0, 0]

            def square(src, k):
                i, j = divmod(sq_n[0], KT)
                wait(act, "sq_summed", i) if j == 0 else wait(act, "sq_used", 7 * i + j)
                sq_n[0] += 1
                A(a.activation(nsq[:], src[:, k, :], ACT.Square), E("sq"))

            def root():
                sq_n[1] += 1
                wait(act, "norm_var", sq_n[1])
                A(a.activation(nrs[:], nrs[:], ACT.Sqrt), E("norm_sd"))

            def product_tile(u, dst, j):
                for h in range(2):
                    wait_full(act, u, h)
                    A(a.activation(dst[:, j, HALF * h:HALF * h + HALF], G[h][:], ACT.Copy), emptied(u, h))
                square(dst, j)

            h_n = [0]

            def high_parts(dst):
                for k in range(KT):
                    h_n[0] += 1
                    wait(act, "h_tmp", h_n[0])
                    A(a.activation(dst[:, k, :], (nsq, nsum)[k % 2][:], ACT.Copy), E("high_part"))

            for j in range(KT):
                product_tile(U_O + j, y1, j)
            root()
            for k in range(KT):
                wait(act, "x2", k + 1)
                square(y1, k)
            root()
            act.dma_start(x2_d, y1[:]).then_inc(E("x2_out"), 16)
            high_parts(h2hi)
            wait(act, "x2_out", 16)
            if stop == 3:
                return

            wait(act, "low_part", PART["h2"] + 8)
            act.dma_start(wsr[:], d["a_w_s_2"][0].rearrange("g t s -> t g s")).then_inc(E("ws_in"), 16)
            act.dma_start(bsb[:], d["a_b_s_2"][0:1].to_broadcast([P, 8, P])).then_inc(E("ws_in"), 16)
            for i in range(16):
                wait(act, "vg_tr", 2 * i)
                for h in range(2):
                    wait_full(act, U_V + i, h)
                    A(a.activation(vg[:, HALF * h:HALF * h + HALF], G[h][:], ACT.Gelu_apprx_tanh), emptied(U_V + i, h))
            wait(act, "ln_var", 1)
            A(a.activation(stat[:, 336:344], stat[:, 336:344], ACT.Sqrt), E("ln_sd"))
            for i in range(16):
                wait(act, "y_mlp", i)
                for h in range(2):
                    wait_full(act, U_UZ + 2 * i, h)
                    A(a.activation(ug[:, HALF * h:HALF * h + HALF], G[h][:], ACT.Gelu_apprx_tanh), emptied(U_UZ + 2 * i, h))
                for h in range(2):
                    wait_full(act, U_UZ + 2 * i + 1, h)
                    A(a.activation(zg[:, HALF * h:HALF * h + HALF], G[h][:], ACT.Tanh, scale=0.5), E("zg_tanh"))
            act.wait_ge(w_used, U_AO)
            for i in range(16):
                wait(act, "y_mlp", i + 1)
                A(a.activation(yhi[:, i, :].rearrange("p (n t) -> p n t", n=8), vln[:, :, i * P:i * P + P], ACT.Copy), E("high_part"))
            for j in range(KT):
                product_tile(U_AO + 2 * j + 1, y2, j)
            act.dma_start(res[:], x2_d).then_inc(E("res_in"), 16)
            root()
            for k in range(KT):
                wait(act, "x3", k + 1)
                square(y2, k)
            root()
            act.dma_start(x3_d, y2[:]).then_inc(E("x3_out"), 16)
            high_parts(kvhi)
            high_parts(h3hi)
            wait(act, "x3_out", 16)
            if stop == 4:
                return

            lo_ = slice(0, 64)
            wait(act, "low_part", PART["h3"] + 8)
            for j in range(2):
                for h in range(2):
                    wait_full(act, U_KV + j, h)
                    cs = slice(HALF * h, HALF * h + HALF)
                    for m in range(2):
                        src = G[h][(lo_, hi_)[m], :]
                        A(a.activation(kd[lo_, 2 * j + m, cs], src, ACT.Copy))
                        A(a.activation(kd[hi_, 2 * j + m, cs], src, ACT.Copy), emptied(U_KV + j, h) if m else None)
            for j in range(2):
                wait(act, "v2_tr", j)
                for h in range(2):
                    wait_full(act, U_KV + 2 + j, h)
                    A(a.activation(v2T[:, HALF * h:HALF * h + HALF], G[h][:], ACT.Copy), emptied(U_KV + 2 + j, h))

            def copy_back2(c):
                wait(act, "pt2_full", c + 1)
                wait(act, "pv2_full", c)
                src = PT2[:].rearrange("p (n k) -> p n k", n=4)
                if c % 2 == 0:
                    A(a.activation(pts2[:, 0, P:256], src[:, 0, P:256], ACT.Copy))
                    A(a.activation(pts2[:, 1:4, :], src[:, 1:4, :], ACT.Copy), E("pt2_done"))
                else:
                    A(a.activation(pts2[:], src, ACT.Copy), E("pt2_done"))

            def exps2(c):
                i, hh, t = c // 4, c // 2 % 2, c % 2
                wait(act, "ttr2_done", c + 1)
                wait(act, "pt2_full", c)
                cols = slice(c % 2 * 4, c % 2 * 4 + 4)
                for ti in range(4):
                    lo = P if 4 * t + ti == 0 else 0
                    col = c % 2 * 4 + ti
                    A(a.activation(pr2[:, ti, lo:256], neg2[:, ti, lo:256], ACT.Exp, bias=negm[:, col:col + 1], scale=-1.0, accum_out=stat[:, 352 + ti:353 + ti]))
                A(a.activation(stat[:, 356:360], negm[:, cols], ACT.Exp, bias=sink[:, 2 * i + hh:2 * i + hh + 1]), E("exp2_done"))

            for s in range(4 * QP + 5):
                c = s - 3
                if 0 <= c - 1 < 4 * QP:
                    copy_back2(c - 1)
                if 0 <= c < 4 * QP:
                    exps2(c)
                if s < 4 * QP:
                    i, h = s // 4, s % 2
                    u = U_QZ + s // 2
                    wait_full(act, u, h)
                    cs = slice(HALF * h, HALF * h + HALF)
                    if s % 4 < 2:
                        wait(act, "s2_full", 4 * (i - 1))
                        A(a.activation(q2[:, i % 2, cs], G[h][:], ACT.Copy, scale=0.125), emptied(u, h))
                    else:
                        wait(act, "pv2_free", 4 * (i - 1))
                        A(a.activation(zs2[:, i % 2, cs], G[h][:], ACT.Tanh, scale=0.5), E("z2_tanh"))
            wait(act, "ys_done", 1)
            act.dma_start(x3[:], x3_d).then_inc(E("x3_in"), 16)
            act.wait_ge(w_used, U_BO)
            for k in range(QP):
                A(a.activation(yshi[:, k, :], ys[:, k, :], ACT.Copy), E("high_part"))
            for j in range(KT):
                product_tile(U_BO + j, y3, j)
            root()
            for n in range(8):
                wait(act, "out_tr", n + 1)
                A(a.activation(orow[:, n, :], (PT2, S2)[n % 2][:], ACT.Copy), E("rows_out"))
                act.dma_start(out[0, n * P:(n + 1) * P, :], orow[:, n, :]).then_inc(E("out_done"), 16)
            wait(act, "out_done", 128)


_INS = ["x", "pre_norm_gain", "w_in", "rel_bias", "rwkv_shift_mix", "rwkv_w0", "rwkv_w_up", "rwkv_a0", "rwkv_a_up", "rwkv_k_k", "rwkv_k_a",
        "rwkv_r_k", "rwkv_ln_w", "rwkv_ln_b", "w_up_attn", "w_up_rwkv", "w_out", "post_norm_gain", "a_w_in_2", "a_ln_g_2", "a_ln_b_2",
        "a_w_s_2", "a_b_s_2", "a_w_out_2", "a_pre_g_2", "a_post_g_2", "kv_norm_g_2", "w_k_2", "w_v_2", "b_w_in_2", "b_sinks_2", "b_w_out_2",
        "b_pre_g_2", "b_post_g_2"]


def kernel(**inputs):
    import numpy as _np
    import concourse.bacc as _bacc
    from concourse import mybir as _mybir
    from concourse.bass_utils import run_bass_kernel_spmd as _run

    nc = _bacc.Bacc("TRN2", target_bir_lowering=False, num_devices=1)
    packed, hot = shape_constants()
    arrays, aps = {}, {}
    for name, a in [*((n, inputs[n]) for n in _INS), ("shape_consts", packed), ("bucket_hot", hot)]:
        a = _np.ascontiguousarray(a)
        arrays[f"in_{name}"] = a
        aps[name] = nc.dram_tensor(f"in_{name}", a.shape, _mybir.dt.from_np(a.dtype), kind="ExternalInput").ap()
    out = nc.dram_tensor("out_0", (1, T, D), F32, kind="ExternalOutput").ap()
    build(nc, aps, out)
    r = _run(nc, [arrays], core_ids=[0])
    return r.results[0]["out_0"]
```

```python
from contextlib import ExitStack
import math

import numpy as np
import concourse.bass as bass
from concourse import mybir

F32 = mybir.dt.float32
F32R = mybir.dt.float32r
ALU = mybir.AluOpType
ACT = mybir.ActivationFunctionType

P = 128
T = 1024
D = 1024
HALF = 512
KT = D // P
PAIRS = 4
GROUPS = 3
DILATION = (1, 4, 16)
ATTN = 512
C = 64
NCH = T // C
LINE = 384
OFF_Q, OFF_K, OFF_V = 0, 1536, 3072
OFF_ZA, OFF_R, OFF_RK, OFF_RV, OFF_LORA, OFF_ZR = 4608, 5120, 5632, 6144, 6656, 6784
OFF_GA, OFF_GR = 7296, 8320
AW = 2048
QP = 8
FAR = 1e30
EPS = 1e-6
GN_EPS = 64e-5
KB = 1024


def shape_constants():
    r = np.arange(P)
    j = r % C
    t = np.arange(C)
    ident = np.eye(P)
    blocks = (r[:, None] // C == r[None, :] // C)
    ones = np.ones((P, P))
    centre = ident - blocks / C
    strict, incl = j[:, None] < t[None, :], j[:, None] <= t[None, :]
    levels = []
    s = 1
    while s < C:
        levels.append((t[None, :] // (2 * s) == j[:, None] // (2 * s)) & (t[None, :] // s % 2 == 1) & (j[:, None] // s % 2 == 0))
        s *= 2
    ident2 = j[:, None] == t[None, :]
    causal = r[:, None] <= r[None, :]
    q, c = r[:, None], np.arange(2 * P)[None, :]
    dist = P + q - c
    far = np.where((dist >= 0) & (dist < P), dist, FAR)
    packed = np.concatenate([np.asarray(x, np.float32) for x in (ident, blocks, ones, centre, strict, incl, *levels, ident2, causal, far)], axis=1)
    rel = 255 - np.arange(LINE)
    hot = np.zeros((33, GROUPS, LINE), np.float32)
    for g, dil in enumerate(DILATION):
        d = np.maximum(rel, 0) * dil
        ratio = np.log(np.maximum(d, 1).astype(np.float32) / 16) / np.float32(math.log(2048 / 16))
        large = np.minimum(16 + (ratio * 16).astype(np.int32), 31)
        bucket = np.where(d < 16, d, large)
        ok = (rel >= 0) & (rel <= P)
        hot[bucket, g, np.arange(LINE)] = ok
        hot[32, g] = np.where(ok, 0.0, -FAR)
    return packed, hot


NCONST = 128 * 4 + 64 * 2 + 64 * 6 + 64 + 128 + 256


class Own:

    def __init__(self, eng, chain):
        self.eng, self.chain, self.count = eng, chain, {}

    def __call__(self, ins, signal=None):
        s, n = signal if isinstance(signal, tuple) else (signal, None)
        s = self.chain if s is None else s
        ins.then_inc(s, 1)
        n = self.count.get(s.name, 0) + 1 if n is None else n
        self.count[s.name] = n
        self.eng.wait_ge(s, n)


def build(nc, d, out):
    ctx = ExitStack()
    with ctx:
        base = (nc.sbuf_base + 255) // 256 * 256

        def at(name, kb, shape, dt=F32):
            n = int(np.prod(shape[1:])) * 4
            assert kb * KB + n <= 207 * KB + 512, (name, kb, n)
            return nc.alloc_sbuf_tensor_at(name, list(shape), dt, offset=base + int(kb * KB))

        def sem(name):
            return ctx.enter_context(nc.semaphore(name))

        G = [nc.alloc_psum_tensor(f"gemm{h}", [P, HALF], F32) for h in range(2)]
        S2 = nc.alloc_psum_tensor("scores", [P, 2 * HALF], F32)
        PT2 = nc.alloc_psum_tensor("probs_t", [P, 2 * HALF], F32)
        PV = nc.alloc_psum_tensor("weighted", [P, HALF], F32)
        MB = nc.alloc_psum_tensor("max_rows", [P, HALF], F32)
        setup_bank = (S2[:, 0:HALF], S2[:, HALF:], PT2[:, 0:HALF], PT2[:, HALF:])

        raw = at("w_raw", 0, [P, 2, KT, P])
        whi = at("w_hi", 8, [P, 2, KT, P], F32R)
        wlo = at("w_lo", 16, [P, 2, KT, P], F32R)
        cst = at("consts_sb", 24, [P, NCONST])
        o_ = 0
        ident = cst[:, 0:128]
        blocks = cst[:, 128:256]
        ones = cst[:, 256:384]
        centre = cst[:, 384:512]
        mask_a = cst[:, 512:640]
        level = [cst[:, 640 + 64 * i:704 + 64 * i] for i in range(6)]
        ident2 = cst[:, 1024:1088]
        causal = cst[:, 1088:1216]
        far = cst[:, 1216:1472]
        prm = at("params", 24 + 5.75, [P, 192])
        stat = at("stats", 24 + 6.5, [P, 384])
        gain = {n: prm[:, 8 * i:8 * i + 8] for i, n in enumerate(
            ("pre_norm_gain", "post_norm_gain", "a_pre_g_2", "a_post_g_2", "kv_norm_g_2", "b_pre_g_2", "b_post_g_2"))}
        mix = prm[:, 56:69]
        chan = {n: prm[:, 69 + 4 * i:73 + 4 * i] for i, n in enumerate(
            ("rwkv_w0", "rwkv_a0", "rwkv_k_k", "rwkv_k_a", "rwkv_r_k", "rwkv_ln_w", "rwkv_ln_b"))}
        ln_g, ln_b = prm[:, 97:113], prm[:, 113:129]
        half_w0, half_a0 = prm[:, 132:136], prm[:, 136:140]
        half_k_a, less_k_a, half_ln_w = prm[:, 176:180], prm[:, 180:184], prm[:, 184:188]
        sink, neg_sink = prm[:, 144:160], prm[:, 160:176]

        h1hi, h1lo = at("h1_hi", 32, [P, KT, T], F32R), at("h1_lo", 64, [P, KT, T], F32R)
        xt = at("x_rows", 96, [P, 8, D])
        sq0 = at("x_squares", 128, [P, D])
        hot_sb = at("hot_sb", 136, [33, GROUPS, LINE])
        rb33 = at("bias_table", 142, [33, 24])
        prm_rows, prm_rows2 = at("param_rows", 176, [113, P]), at("param_rows2", 177, [16, P])
        lines = at("bias_lines", 184, [8, GROUPS, LINE])
        qT, kT = at("q_t", 128, [P, 2, T]), at("k_t", 136, [P, 2, T])
        vT = at("v_t", 144, [P, T])
        vaug = at("v_and_ones", 148, [P, 2, 8, 192])
        bias_t = at("bias_tile", 160, [P, 2, 2, 256])
        negl = at("neg_logits", 164, [P, 4, 256])
        prob = at("prob", 168, [P, 4, 256])
        ptsb = at("prob_t_sb", 172, [P, 4, 256])
        accu = at("num_den", 176, [P, 2, T])
        nmax = at("neg_max", 184, [P, 2, T])
        nnew = at("neg_max_new", 192, [P, HALF])
        eab = at("rescale", 194, [P, 2, HALF])
        zs = at("z_silu", 198, [P, T])
        og = at("o_gated", 202, [P, T])
        rd = at("recip_den", 96, [P, T])
        t1 = at("scaled_new", 100, [P, HALF])
        negm = stat[:, 64:88]
        upw = at("lora_up", 126, [P, 512])
        oF = at("o_f32", 96, [P, 8, T])
        lora = at("lora", 96, [P, T])
        rT, bon, rkT = at("r_t", 100, [P, T]), at("bonus", 104, [P, T]), at("rk_t", 108, [P, T])
        gate_out_sb, gate_out_sb2 = at("gate_out_sb", 124, [P, HALF]), at("gate_out_sb2", 96, [P, HALF])
        AM = at("a_mats", 128, [P, 2, NCH, 3, C])
        BK = at("b_k", 152, [P, NCH, 2, C])
        vpad = at("v_padded", 160, [P, C + T + C])
        raw_of = (rT[:], rkT[:], vpad[:, C:C + T])
        reset = at("chunk_reset", 201, [P, T])
        ksq, kgain = at("k_squares", 164.5, [P, T]), at("k_gain", 168.5, [P, T])
        rkr, kmod, kka = at("r_k_products", 173, [P, T]), at("k_mod", 177, [P, T]), at("kk_a", 181, [P, T])
        logw, cum = at("log_decay", 185, [P, T]), at("cum_decay", 189, [P, T])
        aT, kk = at("a_t", 193, [P, T]), at("kk_t", 197, [P, T])
        ec = at("e_cum", 201, [P, T])
        BKt = at("bk_rows", 164.5, [P, NCH, P])
        SV = at("state_and_v", 172.5, [P, 2, 2, NCH, C])
        Tm, TT = at("inv", 188.5, [P, NCH, C]), at("inv_t", 192.5, [P, NCH, C])
        Xs = at("inv_x", 196.5, [P, NCH, C])
        shift = at("token_shift", 196.5, [P, T])
        AmT = at("a_level", 152, [P, 2, NCH, C])
        Aab = at("a_ab", 200.5, [P, NCH, C])
        xs = at("scan_x", 205, [P, C])
        se = at("scan_state", 205.5, [P, C])
        e_end = stat[:, 96:112]
        yT, yc, ysq = at("y_t", 177, [P, T]), at("y_centred", 181, [P, T]), at("y_squares", 185, [P, T])
        oA = [at(f"attn_out{k}", kb, [P, T]) for k, kb in enumerate((152, 100, 156, 108))]
        ohi, olo = at("o_hi", 128, [P, 8, T], F32R), at("o_lo", 96, [P, 8, T], F32R)
        gates = at("merge_gates", 32, [P, 2 * KT, T])
        mhi, mlo = at("merged_hi", 160, [P, KT, T], F32R), at("merged_lo", 32, [P, KT, 2, T], F32R)
        y1 = at("block1_out", 96, [P, KT, T])
        xt2 = at("x_rows_again", 128, [P, 8, D])
        nsq = at("norm_squares", 192, [P, T])
        nsum = at("norm_sum", 196, [P, T])
        nrs = at("norm_rstd", 200, [P, T])
        sq_buf = (nsq, nsum)
        h2hi, h2lo = at("h2_hi", 32, [P, KT, T], F32R), at("h2_lo", 64, [P, KT, T], F32R)
        vln = at("mlp_v", 128, [P, 8, AW])
        wsT = at("ws_t", 96, [P, 8, P])
        rowsum = at("ws_rowsum", 100, [P, 8, P])
        bsb = at("bs_rows", 104, [P, 8, P])
        wsr = at("ws_raw", 108, [P, 8, P])
        btile = at("b_tile", 112, [P, P])
        zg = at("mlp_z", 116, [P, T])
        ug = at("mlp_u", 192, [P, T])
        sg = at("mlp_s", 196, [P, T])
        vg = at("mlp_vg", 200, [P, T])
        yhi, ylo = at("mlp_y_hi", 32, [P, 16, T], F32R), at("mlp_y_lo", 128, [P, 8, AW], F32R)
        y2 = at("block2a_out", 96, [P, KT, T])
        res = at("residual", 32, [P, KT, T])
        xnhi, xnlo = at("xn_hi", 128, [P, KT, T], F32R), at("xn_lo", 160, [P, KT, T], F32R)
        kd = at("k_dup", 96, [P, 4, T])
        vt2 = at("v_rows", 112, [P, 8, 256])
        q2 = at("q2_t", 120, [P, 2, T])
        v2T = at("v2_t", 192, [P, T])
        ys = at("swa_y", 32, [P, QP, T])
        zs2 = at("z2_silu", 64, [P, 2, T])
        neg2 = at("neg_logits2", 72, [P, 4, 256])
        pr2 = at("prob2", 76, [P, 4, 256])
        pts2 = at("prob2_t", 80, [P, 4, 256])
        alibi = at("alibi_tile", 84, [P, 2, 2, 256])
        yshi, yslo = at("swa_y_hi", 96, [P, QP, T], F32R), at("swa_y_lo", 128, [P, QP, T], F32R)
        y3 = at("block2b_out", 64, [P, KT, T])
        x3 = at("x3_again", 160, [P, KT, T])
        orow = at("out_rows", 96, [P, 8, D])

        lines_d = nc.dram_tensor("lines_scratch", (GROUPS, 8, P, LINE), F32).ap()
        oA_d = nc.dram_tensor("attn_out_scratch", (PAIRS, P, T), F32).ap()
        x2_d = nc.dram_tensor("x2_scratch", (P, KT, T), F32).ap()
        gates_d = nc.dram_tensor("gates_scratch", (P, 2 * KT, T), F32).ap()
        x3_d = nc.dram_tensor("x3_scratch", (P, KT, T), F32).ap()

        units = []

        def unit(name, w, rows, col, nk=KT):
            units.append((name, w[rows:rows + nk * P, col:col + P].rearrange("(k p) n -> p k n", p=P), nk))

        w_in = d["w_in"][0]
        for p in range(PAIRS):
            for g in range(GROUPS):
                for off in (OFF_Q, OFF_K, OFF_V):
                    unit("qkv", w_in, 0, off + g * ATTN + p * P)
            unit("za", w_in, 0, OFF_ZA + p * P)
        U_R = len(units)
        unit("lora", w_in, 0, OFF_LORA)
        for off in (OFF_R, OFF_RK, OFF_RV):
            unit("rwkv", w_in, 0, off)
        merge_gates = [off + j * P for j in range(KT) for off in (OFF_GA, OFF_GR)]
        U_SIDE = []
        for p in range(PAIRS):
            U_SIDE.append(len(units))
            last = p == PAIRS - 1
            for col in merge_gates[3 * p:len(merge_gates) if last else 3 * p + 3]:
                unit("gate", w_in, 0, col)
            if not last:
                for off in (OFF_R, OFF_RK, OFF_RV):
                    unit("rwkv", w_in, 0, off + (p + 1) * P)
            unit("zr", w_in, 0, OFF_ZR + p * P)
        U_M = len(units)
        U_SIDE.append(U_M)
        for j in range(KT):
            unit("ua", d["w_up_attn"][0], 0, j * P, 4)
            unit("ur", d["w_up_rwkv"][0], 0, j * P, 4)
        U_O = len(units)
        for j in range(KT):
            unit("wo", d["w_out"][0], 0, j * P)
        U_V = len(units)
        wa = d["a_w_in_2"][0]
        for i in range(16):
            unit("mv", wa, 0, AW + i * P)
        U_UZ = len(units)
        for i in range(16):
            unit("mu", wa, 0, i * P)
            unit("mz", wa, 0, 2 * AW + i * P)
        U_AO = len(units)
        for j in range(KT):
            unit("ao", d["a_w_out_2"][0], 0, j * P)
            unit("ao", d["a_w_out_2"][0], D, j * P)
        U_KV = len(units)
        for w in ("w_k_2", "w_v_2"):
            for j in range(2):
                unit("kv", d[w], 0, j * P)
        U_QZ = len(units)
        for i in range(QP):
            unit("q", d["b_w_in_2"][0], 0, i * P)
            unit("z", d["b_w_in_2"][0], 0, D + i * P)
        U_BO = len(units)
        for j in range(KT):
            unit("bo", d["b_w_out_2"][0], 0, j * P)
        U_END = len(units)
        outs_before, n = [], 0
        for u in range(U_END):
            outs_before.append(n)
            n += not (U_AO <= u < U_KV and (u - U_AO) % 2 == 0)

        def side_plan(total):
            more = (total - 112) // 2
            counts = [("in", 8), ("norm", 4), ("bonus", 16 + more), *((f"amat{f}", 3) for f in range(4)), ("rows", 8 + more),
                      *((f"inv{i}", 3) for i in range(11)), *((f"scan{i}", 1) for i in range(31)), ("scan31", 0)]
            plan, n = {}, 0
            for place, k in counts:
                plan[place] = (n, n + k)
                n += k
            assert n == total
            return plan

        SIDE = [side_plan(16 * (U_SIDE[p + 1] - U_SIDE[p])) for p in range(PAIRS)]
        MIX_AT = (1, 4, 10)

        quads = [(p, g, hh, t) for p in range(PAIRS) for g in range(GROUPS) for hh in range(2) for t in range(2)]
        slot_of = {20 * p + 6 * g + 7 + 2 * hh + t: c for c, (p, g, hh, t) in enumerate(quads)}
        v_slot = {20 * p + 6 * g + 7: 3 * p + g for p in range(PAIRS) for g in range(GROUPS)}
        A_SLOTS = 20 * PAIRS
        A_END = 20 * PAIRS + 5

        def key_blocks(g, n):
            first = n == 0 if g == 0 else (n % 2 == 0 if g == 1 else True)
            return (1,) if first else (0, 1)

        def runs(g, t):
            if g == 0:
                return [(slice(0, 1), 1), (slice(1, 4), 0)] if t == 0 else [(slice(0, 4), 0)]
            return [(slice(0, 4, 2), 1), (slice(1, 4, 2), 0)] if g == 1 else [(slice(0, 4), 1)]

        def natural(ap, g, t):
            if g == 0:
                return ap[:, 512 * t:512 * t + 512]
            r = DILATION[g]
            return ap.rearrange("p (l r) -> p r l", r=r)[:, r // 2 * t:r // 2 * (t + 1), :]

        def permuted(ap, g):
            return ap if g == 0 else ap.rearrange("p (r l) -> p r l", r=DILATION[g] // 2)

        def perm_half(ap, g, h):
            if g == 0:
                return ap[:, HALF * h:HALF * h + HALF]
            r = DILATION[g]
            n = HALF // r
            return ap.rearrange("p (r l) -> p l r", r=r)[:, n * h:n * h + n, :]

        def nat_half(ap, g):
            return ap if g == 0 else ap.rearrange("p (l r) -> p l r", r=DILATION[g])

        made = {}

        def E(name):
            if name not in made:
                made[name] = sem(name)
            return made[name]

        PART = {"o": 0, "m": 8, "h2": 16, "y": 24, "xn": 40, "ys": 48}
        w_raw = [E("w_raw0"), E("w_raw1")]
        g_full = [E("gemm_full0"), E("w_used")]
        w_used = g_full[1]
        g_evac = [E("gemm_evac0"), E("gemm_evac1")]
        bias_in = [E("bias_in0"), E("bias_in1")]
        block = ctx.enter_context(nc.Block())

        def emptied(u, h):
            return g_evac[h], outs_before[u] + 1

        def wait_full(eng, u, h):
            eng.wait_ge(g_full[h], u + 1)

        @block.sync
        def _(sp):
            for i in range(8):
                sp.dma_start(xt[:, i, :], d["x"][0, i * P:(i + 1) * P, :]).then_inc(E(f"x_in{i // 4}"), 16)
            for u in range(U_END):
                name, src, nk = units[u]
                if u >= 2:
                    sp.wait_ge(E("w_split"), u - 1)
                sp.dma_start(raw[:, u % 2, 0:nk, :], src).then_inc(w_raw[u % 2], 16)
                if u < U_R and u % 10 in (2, 5, 8):
                    p, g = u // 10, u % 10 // 3
                    gi = 3 * p + g
                    b = gi % 2
                    if gi < GROUPS:
                        sp.wait_ge(E(f"lines_out{gi}"), 16)
                    if gi >= 2:
                        sp.wait_ge(E("ttr_done"), 4 * (gi - 1))
                    o = (g * 8 + 2 * p) * P * LINE
                    if g < 2:
                        sp.dma_start(bias_t[:, b, :, :], bass.AP(lines_d.tensor, o + 127, [[LINE - 1, P], [P * LINE, 2], [1, 256]])).then_inc(bias_in[b], 16)
                    else:
                        for rr in range(2):
                            for cc in range(2):
                                start, step = (o + 255, LINE - 1) if rr == cc else (o + 320, 0)
                                sp.dma_start(bias_t[64 * rr:64 * rr + 64, b, :, P + 64 * cc:P + 64 * cc + 64],
                                             bass.AP(lines_d.tensor, start, [[step, 64], [P * LINE, 2], [1, 64]])).then_inc(bias_in[b], 16)

        bias_need, cnt = [], [0, 0]
        for gi in range(12):
            cnt[gi % 2] += 64 if gi % 3 == 2 else 16
            bias_need.append(cnt[gi % 2])

        @block.gpsimd
        def _(pool):
            Q = Own(pool, E("pool_chain"))
            Q(pool.memset(vaug[:, :, :, 64:128], 1.0), E("v_ones"))
            for u in range(U_END):
                nk, s = units[u][2], u % 2
                pool.wait_ge(w_raw[s], 16 * (u // 2 + 1))
                if U_KV <= u < U_BO:
                    g = gain["kv_norm_g_2" if u < U_QZ else "b_pre_g_2"]
                    pool.wait_ge(E("prm_sb"), 1)
                    Q(pool.tensor_tensor(raw[:, s], raw[:, s], g.unsqueeze(2).to_broadcast([P, KT, P]), ALU.mult))
                if u >= 2:
                    pool.wait_ge(w_used, u - 1)
                Q(pool.tensor_copy(whi[:, s, 0:nk, :], raw[:, s, 0:nk, :]))
                Q(pool.tensor_tensor(wlo[:, s, 0:nk, :], raw[:, s, 0:nk, :], whi[:, s, 0:nk, :].bitcast(F32), ALU.subtract), E("w_split"))

        @block.tensor
        def _(pe):
            def gemm_step(u, h, k, hi, lo, start=True, stop_=True):
                nk, s = units[u][2], u % 2
                if k == 0:
                    if h == 0:
                        pe.wait_ge(E("w_split"), u + 1)
                    if start and outs_before[u]:
                        pe.wait_ge(g_evac[h], outs_before[u])
                first, last = start and k == 0, stop_ and k == nk - 1
                pe.matmul(G[h][:], whi[:, s, k, :], hi(k, h), start=first, stop=False)
                pe.matmul(G[h][:], whi[:, s, k, :], lo(k, h), start=False, stop=False)
                m = pe.matmul(G[h][:], wlo[:, s, k, :], hi(k, h), start=False, stop=last)
                if k == nk - 1:
                    m.then_inc(g_full[h], 1)

            def gemm_half(u, h, hi, lo, ready=None, start=True, stop_=True):
                for k in range(units[u][2]):
                    if ready:
                        ready(k, h)
                    gemm_step(u, h, k, hi, lo, start, stop_)

            def moving(hi, lo):
                return (lambda k, h: hi[:, k, HALF * h:HALF * h + HALF]), (lambda k, h: lo[:, k, HALF * h:HALF * h + HALF])

            H1 = moving(h1hi, h1lo)

            pe.wait_ge(E("hot_in"), 32)
            pe.wait_ge(E("hot_one"), 1)
            for g in range(GROUPS):
                if g > 0:
                    pe.wait_ge(E("line_sb"), g)
                pe.matmul(PV[0:8, 0:LINE], rb33[:, 8 * g:8 * g + 8], hot_sb[:, g, :], start=True, stop=True).then_inc(E("line_full"), 1)
            pe.wait_ge(E("c_in"), 16)
            pe.wait_ge(E("prm_in"), 16 * 17)
            pe.transpose(MB[:, 0:113], prm_rows[:, :], ident[0:113, 0:113])
            pe.transpose(MB[:, 113:129], prm_rows2[:, :], ident[0:16, 0:16]).then_inc(E("prm_tr"), 1)
            for f in range(16):
                hf, kk_ = f // 8, f % 8
                pe.wait_ge(E("x_scaled"), 4 * hf + 4)
                if f - 3 > 0:
                    pe.wait_ge(E("h1_lo"), f - 3)
                for i in range(4):
                    m = pe.transpose(setup_bank[f % 4][:, i * P:(i + 1) * P], xt[:, 4 * hf + i, kk_ * P:(kk_ + 1) * P], ident)
                m.then_inc(E("x_tr"), 1)

            def v_rows(gi):
                u = 10 * (gi // 3) + 3 * (gi % 3) + 2
                for h in range(2):
                    pe.wait_ge(g_evac[h], outs_before[u] + 1)
                if 4 * gi > 0:
                    pe.wait_ge(E("pt_done"), 4 * gi)
                for t in range(2):
                    for i in range(4):
                        m = pe.transpose(PT2[:, (4 * t + i) * P:(4 * t + i + 1) * P], vT[:, (4 * t + i) * P:(4 * t + i + 1) * P], ident)
                    m.then_inc(E("v_tr"), 1)

            def scores(c):
                p, g, hh, t = quads[c]
                gi = 3 * p + g
                for h in range(2):
                    pe.wait_ge(g_evac[h], outs_before[10 * p + 3 * g + 1] + 1)
                if c > 0:
                    pe.wait_ge(E("ttr_done"), c)
                rows = slice(64 * hh, 64 * hh + 64)
                for i in range(4):
                    n = 4 * t + i
                    b0 = key_blocks(g, n)[0]
                    m = pe.matmul(S2[:, i * 256 + b0 * P:i * 256 + 256], qT[rows, gi % 2, n * P:n * P + P],
                                  kT[rows, gi % 2, (n - 1 + b0) * P:(n + 1) * P], start=True, stop=True)
                m.then_inc(E("s_full"), 1)

            def transposes(c):
                p, g, hh, t = quads[c]
                pe.wait_ge(E("exp_done"), c + 1)
                if c > 0:
                    pe.wait_ge(E("pt_done"), c)
                pe.wait_ge(E("v_rows"), 2 * (3 * p + g) + 2)
                for i in range(4):
                    for b in key_blocks(g, 4 * t + i):
                        m = pe.transpose(PT2[:, i * 256 + b * P:i * 256 + b * P + P], prob[:, i, b * P:b * P + P], ident)
                m.then_inc(E("pt_full"), 1)

            def weighted(c):
                p, g, hh, t = quads[c]
                pe.wait_ge(E("pt_done"), c + 1)
                if c > 0:
                    pe.wait_ge(E("pv_free"), c)
                if c == 0:
                    pe.wait_ge(E("v_ones"), 1)
                for i in range(4):
                    n = 4 * t + i
                    bs = key_blocks(g, n)
                    for b in bs:
                        pe.matmul(PV[:, i * P:i * P + P], vaug[:, (3 * p + g) % 2, n - 1 + b, 64 * hh:64 * hh + P], ptsb[:, i, b * P:b * P + P],
                                  start=b == bs[0], stop=b == 1)
                for i in range(4):
                    col = c % 4 * 4 + i
                    m = pe.matmul(MB[:, i * P:i * P + P], negm[:, col:col + 1].to_broadcast([P, P]), ident, start=True, stop=True)
                m.then_inc(E("pv_full"), 1)

            for s in range(A_END):
                if s in v_slot:
                    v_rows(v_slot[s])
                if s - 1 in slot_of:
                    transposes(slot_of[s - 1])
                if s - 2 in slot_of:
                    weighted(slot_of[s - 2])
                if s in slot_of:
                    scores(slot_of[s])
                if s < A_SLOTS:
                    if s < 2:
                        pe.wait_ge(E("h1_lo"), 8 * s + 8)
                    gemm_half(s // 2, s % 2, *H1)
            rows2 = (slice(0, 64), slice(64, 128))
            halves = (slice(0, HALF), slice(HALF, T))

            def side(p, place):
                for i in range(*SIDE[p][place]):
                    gemm_step(U_SIDE[p] + i // 16, i // 8 % 2, i % 8, *H1)

            def spread(dst, col, done):
                for n in range(8):
                    for hh, r in enumerate(rows2):
                        m = pe.matmul(dst[r, n * P:n * P + P], stat[:, col + 2 * n + hh:col + 2 * n + hh + 1].to_broadcast([P, C]), ident, start=True, stop=True)
                m.then_inc(E(done), 1)

            def head_sums(src, done):
                for n in range(8):
                    m = pe.matmul(PV[:, 2 * n:2 * n + 2], src[:, n * P:n * P + P], blocks[:, 0:P:C], start=True, stop=True)
                m.then_inc(E(done), 1)

            for u in range(U_R, U_R + 4):
                for h in range(2):
                    gemm_half(u, h, *H1)
            for p in range(PAIRS):
                pe.wait_ge(E("lora_tanh"), 1)
                pe.wait_ge(E("up_in"), 32)
                if p > 0:
                    pe.wait_ge(E("y_centred"), p)
                if p > 0:
                    pe.wait_ge(E("y_sq"), p)
                for h in range(2):
                    m = pe.matmul(PT2[:, halves[h]], upw[64:128, p * P:p * P + P], lora[64:128, halves[h]], start=True, stop=True)
                m.then_inc(E("a_full"), 1)
                if p > 0:
                    pe.wait_ge(E("y_normed"), p)
                for h in range(2):
                    m = pe.matmul(S2[:, halves[h]], upw[0:64, p * P:p * P + P], lora[0:64, halves[h]], start=True, stop=True)
                m.then_inc(E("lw_full"), 1)
                side(p, "in")
                pe.wait_ge(E("k_sq"), p + 1)
                head_sums(ksq, "knorm_full")
                side(p, "norm")
                pe.wait_ge(E("lw_tanh"), p + 1)
                pe.wait_ge(E("kinv"), p + 1)
                spread(S2, 112, "kinv_full")
                pe.wait_ge(E("rkr"), p + 1)
                pe.wait_ge(E("a_tanh"), p + 1)
                for h in range(2):
                    m = pe.matmul(PT2[:, halves[h]], blocks, rkr[:, halves[h]], start=True, stop=True)
                m.then_inc(E("bonus_full"), 1)
                side(p, "bonus")
                pe.wait_ge(E("ak_ready"), p + 1)
                pe.wait_ge(E("bonus_done"), p + 1)
                for f in range(4):
                    hh, cq = f // 2, f % 2
                    if f >= 2:
                        pe.wait_ge(E("amat_done"), 4 * p + f - 1)
                    for i in range(8):
                        c = 8 * cq + i
                        m = pe.matmul((S2, PT2)[cq][:, i * P:i * P + P], BK[rows2[hh], c, :, :], AM[rows2[hh], hh, c, 0:3:2, :], start=True, stop=True)
                    m.then_inc(E("amat_full"), 1)
                    side(p, f"amat{f}")
                for f in range(4):
                    if 4 * p + f - 1 > 0:
                        pe.wait_ge(E("bk_rows"), 4 * p + f - 1)
                    for i in range(4):
                        m = pe.transpose((PV, MB)[f % 2][:, i * P:i * P + P], BK[:, 4 * f + i, :, :], ident)
                    m.then_inc(E("bk_tr"), 1)
                for f in range(5):
                    pe.wait_ge(E("bk_rows"), 4 * p + 3 + f % 2)
                    if 4 * p + f - 1 > 0:
                        pe.wait_ge(E("vr_even"), 4 * p + f - 1)
                    if 5 * p + f - 1 > 0:
                        pe.wait_ge(E("vr_odd"), 5 * p + f - 1)
                    for w in range(4 * f, min(4 * f + 4, 17)):
                        m = pe.transpose((PV, MB)[f % 2][:, (w % 4) * P:(w % 4) * P + P], vpad[:, C * w:C * w + P], ident)
                    m.then_inc(E("vr_tr"), 1)
                side(p, "rows")
                pe.wait_ge(E("a_level"), 6 * p + 1)
                pe.wait_ge(E("amat_done"), 4 * p + 4)
                for c in range(NCH):
                    for r in rows2:
                        m = pe.matmul(PT2[r, c * C:c * C + C], AmT[r, 0, c, :], ident2[r, :], start=True, stop=True)
                m.then_inc(E("inv_first"), 1)
                side(p, "inv0")
                for lv in range(1, 6):
                    s, nh = 1 << lv, C // 2

                    def part(ap, x):
                        return ap.rearrange("p (b x s) -> p b x s", x=2, s=s)[:, :, x, :]

                    def packed_out(ap):
                        return ap.rearrange("p (b s) -> p b s", s=s)

                    pe.wait_ge(E("a_level"), 6 * p + lv + 1)
                    pe.wait_ge(E("inv_sb"), 6 * p + lv)
                    for c in range(NCH):
                        for r in rows2:
                            m = pe.matmul(S2[r, c * C:c * C + C], AmT[r, lv % 2, c, :], Tm[r, c, :], start=True, stop=True)
                    m.then_inc(E("invx_full"), 1)
                    side(p, f"inv{2 * lv - 1}")
                    pe.wait_ge(E("invx_sb"), 5 * p + lv)
                    if lv < 5:
                        for c in range(NCH):
                            for r in rows2:
                                pe.matmul(packed_out(PT2[r, c * nh:c * nh + nh]), TT[r, c, :], part(Xs[r, c, :], 0), start=True, stop=True)
                    for c in range(NCH):
                        for r in rows2:
                            m = pe.matmul(packed_out(S2[r, c * nh:c * nh + nh]), Xs[r, c, :], part(TT[r, c, :], 1), start=True, stop=True)
                    m.then_inc(E("inv_full"), 1)
                    side(p, f"inv{2 * lv}")
                pe.wait_ge(E("vr_even"), 4 * p + 4)
                pe.wait_ge(E("vr_odd"), 5 * p + 5)
                pe.wait_ge(E("inv_sb"), 6 * p + 6)
                for c in range(NCH):
                    n = NCH * p + c
                    pe.wait_ge(E("state"), n + 1)
                    for hh, r in enumerate(rows2):
                        m = pe.matmul(PV[r, 0:C], AM[:, hh, c, 0, :], SV[:, hh, 0, c, :], start=True, stop=True)
                    m.then_inc(E("sx_full"), 1)
                    side(p, f"scan{2 * c}")
                    pe.wait_ge(E("sx_sb"), n + 1)
                    for hh, r in enumerate(rows2):
                        m = pe.matmul(MB[r, 0:C], TT[r, c, :], xs[r, :], start=True, stop=True)
                    m.then_inc(E("su_full"), 1)
                    side(p, f"scan{2 * c + 1}")
                    pe.wait_ge(E("su_even"), n + 1)
                    pe.wait_ge(E("su_odd"), n + 1)
                    if c < NCH - 1:
                        for hh, r in enumerate(rows2):
                            m = pe.matmul(PT2[r, 0:C], BKt[:, c, C * hh:C * hh + C], SV[:, hh, 1, c, :], start=True, stop=True)
                        m.then_inc(E("ss_full"), 1)
                    for hh, r in enumerate(rows2):
                        o = S2[r, c * C:c * C + C]
                        pe.matmul(o, SV[:, hh, 0, c, :], AM[:, hh, c, 2, :], start=True, stop=False)
                        m = pe.matmul(o, SV[:, hh, 1, c, :], AM[:, hh, c, 1, :], start=False, stop=True)
                m.then_inc(E("y_full"), 1)
                pe.wait_ge(E("y_sb"), p + 1)
                for h in range(2):
                    m = pe.matmul(PT2[:, halves[h]], centre, yT[:, halves[h]], start=True, stop=True)
                m.then_inc(E("centred_full"), 1)
                pe.wait_ge(E("y_sq"), p + 1)
                head_sums(ysq, "var_full")
                pe.wait_ge(E("y_rstd"), p + 1)
                spread(S2, 128, "y_rstd_full")

            OA, OR = moving(ohi[:, 0:4, :], olo[:, 0:4, :]), moving(ohi[:, 4:8, :], olo[:, 4:8, :])
            pe.wait_ge(E("low_part"), PART["o"] + 8)
            for j in range(KT):
                for i, src in enumerate((OA, OR)):
                    for h in range(2):
                        gemm_half(U_M + 2 * j + i, h, *src)

            sums = [0, 0]

            def sum_squares(k):
                sums[0] += 1
                pe.wait_ge(E("sq"), sums[0])
                for i in range(8):
                    m = pe.matmul(PV[:, i:i + 1], sq_buf[k % 2][:, i * P:i * P + P], ones[:, 0:1], start=k == 0 and i == 0, stop=k == KT - 1 and i == 7)
                m.then_inc(E("sq_used"), 1)

            def spread_rstd():
                sums[1] += 1
                pe.wait_ge(E("rstd"), sums[1])
                for i in range(8):
                    m = pe.matmul(S2[:, i * P:i * P + P], stat[:, 344 + i:345 + i].to_broadcast([P, P]), ident, start=True, stop=True)
                m.then_inc(E("rstd_full"), 1)

            MG = moving(mhi, mlo[:, :, 0, :])
            for j in range(KT):
                for h in range(2):
                    gemm_half(U_O + j, h, *MG, ready=(lambda k, h: pe.wait_ge(E("low_part"), PART["m"] + k + 1)) if j == 0 and h == 0 else None)
                if j:
                    sum_squares(j - 1)
            sum_squares(KT - 1)
            spread_rstd()
            for n in range(2):
                pe.wait_ge(E(f"x_in{n}"), 128)
            pe.wait_ge(E("nrs"), 1)
            for k in range(KT):
                if k - 1 > 0:
                    pe.wait_ge(E("x2"), k - 1)
                bank = (PT2, S2)[k % 2]
                for i in range(8):
                    m = pe.transpose(bank[:, i * P:i * P + P], xt2[:, i, k * P:k * P + P], ident)
                m.then_inc(E("xb_tr"), 1)
                if k >= 2:
                    sum_squares(k - 2)
            sum_squares(KT - 2)
            sum_squares(KT - 1)
            spread_rstd()

            H2 = moving(h2hi, h2lo)

            def v_rows_of(i):
                for h in range(2):
                    pe.wait_ge(g_evac[h], outs_before[U_V + i] + 1)
                if 2 * i > 0:
                    pe.wait_ge(E("vln_rows"), 2 * i)
                for t in range(2):
                    for n in range(4):
                        m = pe.transpose(PT2[:, (4 * t + n) * P:(4 * t + n + 1) * P], vg[:, (4 * t + n) * P:(4 * t + n + 1) * P], ident)
                    m.then_inc(E("vg_tr"), 1)

            for i in range(16):
                rdy = (lambda k, h: pe.wait_ge(E("low_part"), PART["h2"] + k + 1)) if i == 0 else None
                gemm_half(U_V + i, 0, *H2, ready=rdy)
                if i:
                    v_rows_of(i - 1)
                gemm_half(U_V + i, 1, *H2, ready=rdy)
                if i == 1:
                    pe.wait_ge(E("ws_in"), 32)
                    for g in range(8):
                        m = pe.transpose(S2[:, g * P:g * P + P], wsr[:, g, :], ident)
                    m.then_inc(E("ws_tr"), 1)
                    pe.wait_ge(E("ws_t"), 1)
                    for h in range(2):
                        m = pe.matmul(S2[:, halves[h]], ones, wsT[:, 4 * h:4 * h + 4, :], start=True, stop=True)
                    m.then_inc(E("rowsum_full"), 1)
            gemm_half(U_UZ, 0, *H2)
            v_rows_of(15)
            pe.wait_ge(E("rowsum"), 1)
            for i in range(16):
                for h in range(2):
                    if i or h:
                        gemm_half(U_UZ + 2 * i, h, *H2)
                for h in range(2):
                    gemm_half(U_UZ + 2 * i + 1, h, *H2)
                pe.wait_ge(E("v_normed"), 4)
                pe.wait_ge(E("v_normed_act"), 4)
                if i > 0:
                    pe.wait_ge(E("s_sb"), i)
                for n in range(8):
                    m = pe.matmul(S2[:, n * P:n * P + P], vln[:, n, i * P:i * P + P], wsT[:, i // 2, :], start=True, stop=True)
                m.then_inc(E("sgu_full"), 1)

            def y_ready(k0):
                return lambda k, h: pe.wait_ge(E("low_part"), PART["y"] + k0 + k + 1)

            for j in range(KT):
                for kh in range(2):
                    u = U_AO + 2 * j + kh
                    src = (lambda k, h, kh=kh: yhi[:, 8 * kh + k, HALF * h:HALF * h + HALF],
                           lambda k, h, kh=kh: ylo[:, 4 * h:4 * h + 4, (8 * kh + k) * P:(8 * kh + k + 1) * P])
                    for h in range(2):
                        gemm_half(u, h, *src, ready=y_ready(8 * kh) if j == 0 else None, start=kh == 0, stop_=kh == 1)
                if j:
                    sum_squares(j - 1)
            sum_squares(KT - 1)
            spread_rstd()
            for k in range(KT):
                sum_squares(k)
            spread_rstd()

            XN = moving(xnhi, xnlo)
            for j in range(4):
                for h in range(2):
                    gemm_half(U_KV + j, h, *XN, ready=(lambda k, h: pe.wait_ge(E("low_part"), PART["xn"] + k + 1)) if j == 0 else None)
                if j >= 2:
                    for h in range(2):
                        pe.wait_ge(g_evac[h], outs_before[U_KV + j] + 1)
                    if j - 2 > 0:
                        pe.wait_ge(E("v2_rows"), j - 2)
                    for n in range(8):
                        m = pe.transpose(PT2[:, n * P:n * P + P], v2T[:, n * P:n * P + P], ident)
                    m.then_inc(E("v2_tr"), 1)

            def scores2(c):
                i, hh, t = c // 4, c // 2 % 2, c % 2
                for h in range(2):
                    pe.wait_ge(g_evac[h], outs_before[U_QZ + 2 * i] + 1)
                pe.wait_ge(E("ttr_done"), len(quads) + c)
                r = rows2[hh]
                for ti in range(4):
                    n = 4 * t + ti
                    b0 = 1 if n == 0 else 0
                    m = pe.matmul(S2[:, ti * 256 + b0 * P:ti * 256 + 256], q2[r, i % 2, n * P:n * P + P], kd[r, i // 2, (n - 1 + b0) * P:(n + 1) * P],
                                  start=True, stop=True)
                m.then_inc(E("s_full"), 1)

            def transposes2(c):
                t = c % 2
                pe.wait_ge(E("pn_done"), c + 1)
                pe.wait_ge(E("pt_done"), len(quads) + c)
                for ti in range(4):
                    for b in ((1,) if 4 * t + ti == 0 else (0, 1)):
                        m = pe.transpose(PT2[:, ti * 256 + b * P:ti * 256 + b * P + P], pr2[:, ti, b * P:b * P + P], ident)
                m.then_inc(E("pt_full"), 1)

            def weighted2(c):
                i, hh, t = c // 4, c // 2 % 2, c % 2
                pe.wait_ge(E("pt_done"), len(quads) + c + 1)
                pe.wait_ge(E("pv_free"), len(quads) + c)
                for ti in range(4):
                    n = 4 * t + ti
                    bs = (1,) if n == 0 else (0, 1)
                    for b in bs:
                        m = pe.matmul(PV[rows2[hh], ti * P:ti * P + P], vt2[:, n - 1 + b, 64 * (i // 2):64 * (i // 2) + 64], pts2[:, ti, b * P:b * P + P],
                                      start=b == bs[0], stop=b == 1)
                m.then_inc(E("pv_full"), 1)

            pe.wait_ge(E("v2_rows"), 2)
            for s in range(4 * QP + 5):
                c = s - 3
                if 0 <= c - 1 < 4 * QP:
                    transposes2(c - 1)
                if 0 <= c - 2 < 4 * QP:
                    weighted2(c - 2)
                if 0 <= c < 4 * QP:
                    scores2(c)
                if s < 4 * QP:
                    gemm_half(U_QZ + s // 2, s % 2, *XN)
            YS = moving(yshi, yslo)
            for j in range(KT):
                for h in range(2):
                    gemm_half(U_BO + j, h, *YS, ready=(lambda k, h: pe.wait_ge(E("low_part"), PART["ys"] + k + 1)) if j == 0 else None)
                if j:
                    sum_squares(j - 1)
            sum_squares(KT - 1)
            spread_rstd()
            pe.wait_ge(E("x4"), 8)
            for n in range(8):
                if n - 1 > 0:
                    pe.wait_ge(E("rows_out"), n - 1)
                bank = (PT2, S2)[n % 2]
                for k in range(KT):
                    m = pe.transpose(bank[:, k * P:k * P + P], y3[:, k, n * P:n * P + P], ident)
                m.then_inc(E("out_tr"), 1)

        @block.vector
        def _(dve):
            V = Own(dve, E("dve_chain"))
            v = nc.vector
            V(v.memset(rb33[32:33, :], 1.0), E("hot_one"))
            for hf in range(2):
                cols = slice(8 + 4 * hf, 12 + 4 * hf)
                dve.wait_ge(E("squares"), 4 * hf + 4)
                V(v.tensor_scalar(stat[:, cols], stat[:, 4 * hf:4 * hf + 4], 1.0 / D, EPS, ALU.mult, ALU.add), E("mean_sq0"))
                dve.wait_ge(E("sqrt0"), hf + 1)
                V(v.reciprocal(stat[:, cols], stat[:, cols]))
                for i in range(4 * hf, 4 * hf + 4):
                    V(v.tensor_scalar(xt[:, i, :], xt[:, i, :], stat[:, 8 + i:9 + i], None, ALU.mult), E("x_scaled"))
            for f in range(16):
                hf, kk_ = f // 8, f % 8
                dst = slice(HALF * hf, HALF * hf + HALF)
                dve.wait_ge(E("h1_hi"), f + 1)
                dve.wait_ge(E("prm_sb"), 1)
                V(v.scalar_tensor_tensor(h1lo[:, kk_, dst], setup_bank[f % 4], gain["pre_norm_gain"][:, kk_:kk_ + 1],
                                         h1hi[:, kk_, dst].bitcast(F32), ALU.mult, ALU.subtract), E("h1_lo"))

            def v_rows(gi):
                if gi >= 2:
                    dve.wait_ge(E("pv_full"), 4 * (gi - 1))
                dve.wait_ge(E("v_ones"), 1)
                for t in range(2):
                    dve.wait_ge(E("v_tr"), 2 * gi + t + 1)
                    dst = vaug[:, gi % 2, 4 * t:4 * t + 4, :].rearrange("p n (a c) -> p n a c", a=3)[:, :, 0:3:2, :]
                    V(v.tensor_copy(dst, PT2[:, HALF * t:HALF * t + HALF].rearrange("p (n a c) -> p n a c", n=4, a=2)), E("v_rows"))

            def biased(c):
                p, g, hh, t = quads[c]
                gi = 3 * p + g
                dve.wait_ge(E("s_full"), c + 1)
                dve.wait_ge(bias_in[gi % 2], bias_need[gi])
                if c > 0:
                    dve.wait_ge(E("exp_done"), c)
                if c - 3 > 0:
                    dve.wait_ge(E("pv_full"), c - 3)
                for i in range(4):
                    lo = key_blocks(g, 4 * t + i)[0] * P
                    col = c % 4 * 4 + i
                    V(v.tensor_tensor_reduce(out=negl[:, i, lo:256], in0=S2[:, i * 256 + lo:i * 256 + 256], in1=bias_t[:, gi % 2, hh, lo:256],
                                             scale=-1.0, scalar=3e38, op0=ALU.add, op1=ALU.min, accum_out=negm[:, col:col + 1]),
                      E("ttr_done") if i == 3 else None)

            def merge(c):
                p, g, hh, t = quads[c]
                dve.wait_ge(E("pv_full"), c + 1)
                num, nm = natural(accu[:, hh, :], g, t), natural(nmax[:, hh, :], g, t)
                new, newm = permuted(PV[:], g), permuted(MB[:], g)
                if g == 0:
                    V(v.tensor_copy(num, new))
                    V(v.tensor_copy(nm, newm), E("pv_free"))
                    return
                k = sum(1 for q in quads[:c] if q[1]) + 1
                nn, ea, eb = (permuted(x, g) for x in (nnew[:], eab[:, 0, :], eab[:, 1, :]))
                V(v.tensor_tensor(nn, nm, newm, ALU.min))
                V(v.tensor_tensor(ea, nn, nm, ALU.subtract))
                V(v.tensor_tensor(eb, nn, newm, ALU.subtract), E("ab_ready"))
                if g == 1:
                    V(v.tensor_copy(nm, nn))
                dve.wait_ge(E("eab_done"), k)
                V(v.tensor_tensor(permuted(t1[:], g), new, eb, ALU.mult), E("pv_free"))
                V(v.tensor_tensor(num, num, ea, ALU.mult))
                V(v.tensor_tensor(num, num, permuted(t1[:], g), ALU.add))
                if g == GROUPS - 1:
                    own, other = (slice(0, 64), slice(64, 128))[::1 - 2 * hh]
                    rden = natural(rd[own, :], g, t)
                    V(v.reciprocal(rden, natural(accu[other, hh, :], g, t)))
                    if c % 12 == 8:
                        if 16 * p > 0:
                            dve.wait_ge(E("oa_out"), 16 * p)
                    V(v.tensor_tensor(natural(og[own, :], g, t), natural(accu[own, hh, :], g, t), rden, ALU.mult))

            for s in range(A_END):
                if s in v_slot:
                    v_rows(v_slot[s])
                if s in slot_of:
                    biased(slot_of[s])
                if s - 2 in slot_of:
                    c = slot_of[s - 2]
                    merge(c)
                    if c % 12 == 11:
                        V(v.scalar_tensor_tensor(og[:], og[:], 0.5, zs[:], ALU.mult, ALU.mult), E("fin_done"))
                if s < A_SLOTS:
                    u, h = s // 2, s % 2
                    p, r = u // 10, u % 10
                    if r % 3 == 2 and r < 9:
                        gi = 3 * p + r // 3
                        wait_full(dve, u, h)
                        if 2 * gi > 0:
                            dve.wait_ge(E("v_tr"), 2 * gi)
                        V(v.tensor_copy(perm_half(vT[:], r // 3, h), nat_half(G[h][:], r // 3)), emptied(u, h))
                    elif r == 9:
                        z = zs[:, HALF * h:HALF * h + HALF]
                        dve.wait_ge(E("z_tanh"), 2 * p + h + 1)
                        V(v.scalar_tensor_tensor(z, z, 1.0, G[h][:], ALU.add, ALU.mult), emptied(u, h))
            lo_, hi_ = slice(0, 64), slice(64, 128)
            rows2 = (lo_, hi_)
            krows = (hi_, lo_)
            V(v.memset(vpad[:, 0:C], 0.0))
            V(v.memset(vpad[:, C + T:], 0.0))
            for hh in range(2):
                V(v.memset(AM[krows[hh], hh, :, 1, :], 0.0))

            def mixed(u, raw_, col):
                for h in range(2):
                    dve.wait_ge(g_evac[h], outs_before[u] + 1)
                V(v.tensor_scalar(shift[:, 0:1], raw_[:, 0:1], -1.0, None, ALU.mult))
                V(v.tensor_tensor(shift[:, 1:T], raw_[:, 0:T - 1], raw_[:, 1:T], ALU.subtract))
                V(v.scalar_tensor_tensor(raw_, shift[:], mix[:, col:col + 1], raw_, ALU.mult, ALU.add), E("mixed"))

            mixed(U_R, lora[:], 12)
            for i in range(3):
                mixed(U_R + 1 + i, raw_of[i], 4 * i)
            for p in range(PAIRS):
                one = slice(p, p + 1)
                V(v.memset(reset[:], 1.0))
                V(v.memset(reset[:, 0:T:C], 0.0))
                dve.wait_ge(E("k_gain"), p + 1)
                V(v.tensor_tensor(kmod[:], kgain[:], rkT[:], ALU.mult))
                V(v.scalar_tensor_tensor(rkr[:], rT[:], chan["rwkv_r_k"][:, one], kmod[:], ALU.mult, ALU.mult), E("rkr"))
                dve.wait_ge(E("logw"), p + 1)
                V(v.tensor_tensor_scan(out=cum[:], data0=reset[:], data1=logw[:], initial=0.0, op0=ALU.mult, op1=ALU.add))
                V(v.tensor_tensor(logw[:], cum[:], logw[:], ALU.subtract), E("cum"))
                dve.wait_ge(E("knorm_full"), p + 1)
                V(v.tensor_scalar(stat[:, 112:128], PV[:, 0:16], 1e-24, None, ALU.max), E("knorm_sb"))
                dve.wait_ge(E("k_sqrt"), p + 1)
                V(v.reciprocal(stat[:, 112:128], stat[:, 112:128]), E("kinv"))
                dve.wait_ge(E("kinv_full"), p + 1)
                V(v.scalar_tensor_tensor(kk[:], rkT[:], chan["rwkv_k_k"][:, one], S2[:], ALU.mult, ALU.mult))
                dve.wait_ge(E("a_sig"), p + 1)
                V(v.tensor_tensor(kka[:], kk[:], aT[:], ALU.mult))
                dve.wait_ge(E("bonus_full"), p + 1)
                V(v.tensor_tensor(bon[:], PT2[:], vpad[:, C:C + T], ALU.mult), E("bonus_done"))
                dve.wait_ge(E("exps"), p + 1)
                V(v.tensor_copy(e_end, ec[:, C - 1:T:C]))

                def chunks(ap):
                    return ap.rearrange("p (c t) -> p c t", t=C)

                for hh, r in enumerate(rows2):
                    V(v.tensor_tensor(AM[r, hh, :, 2, :], chunks(rT[r, :]), chunks(ec[r, :]), ALU.mult))
                    V(v.scalar_tensor_tensor(AM[r, hh, :, 0, :], chunks(kk[r, :]), -1.0, chunks(logw[r, :]), ALU.mult, ALU.mult))
                    V(v.tensor_tensor(BK[r, :, hh, :], chunks(kka[r, :]), chunks(cum[r, :]), ALU.mult))
                    V(v.tensor_tensor(BK[r, :, 1 - hh, :], chunks(kmod[r, :]), chunks(cum[r, :]), ALU.mult), E("ak_ready") if hh else None)
                for f in range(4):
                    hh, cq = f // 2, f % 2
                    bank = (S2, PT2)[cq][:].rearrange("p (c x t) -> p c x t", c=8, x=2)
                    cs = slice(8 * cq, 8 * cq + 8)
                    b, k = rows2[hh], krows[hh]

                    def masked(dst, src, m, signal=None):
                        V(v.tensor_tensor(dst, src, m.unsqueeze(1).to_broadcast([64, 8, C]), ALU.mult), signal)

                    dve.wait_ge(E("amat_full"), 4 * p + f + 1)
                    masked(Aab[b, cs, :], bank[b, :, 0, :], mask_a[b, 0:C])
                    masked(AM[b, hh, cs, 1, :], bank[b, :, 1, :], mask_a[b, C:2 * C])
                    masked(AM[k, hh, cs, 0, :], bank[k, :, 0, :], mask_a[k, 0:C])
                    masked(AM[k, hh, cs, 2, :], bank[k, :, 1, :], mask_a[k, C:2 * C], E("amat_done"))
                for f in range(4):
                    bank = (PV, MB)[f % 2][:].rearrange("p (w x c) -> p w x c", w=4, x=2)
                    dve.wait_ge(E("vr_tr"), 5 * p + f + 1)
                    for kind in range(2):
                        V(v.tensor_copy(SV[hi_, 0, kind, 4 * f:4 * f + 4, :], bank[hi_, :, 0, :]), E("vr_even") if kind else None)
                dve.wait_ge(E("bk_tr"), 4 * p + 4)

                def level_of(i):
                    V(v.tensor_tensor(AmT[:, i % 2], Aab[:], level[i].unsqueeze(1).to_broadcast([P, NCH, C]), ALU.mult), E("a_level"))

                flat = "p c t -> p (c t)"
                eye = ident2.unsqueeze(1).to_broadcast([P, NCH, C])
                level_of(0)
                V(v.tensor_tensor(TT[:], AmT[:, 0], eye, ALU.add))
                level_of(1)
                dve.wait_ge(E("inv_first"), p + 1)
                V(v.tensor_tensor(Tm[:], PT2[:].rearrange("p (c t) -> p c t", t=C), eye, ALU.add), E("inv_sb"))
                for lv in range(1, 6):
                    s = 1 << lv

                    def part(ap, x):
                        return ap.rearrange("p c (b x s) -> p (c b) x s", x=2, s=s)[:, :, x, :]

                    def packed_in(ap):
                        return ap.rearrange("p (q s) -> p q s", s=s)

                    dve.wait_ge(E("invx_full"), 5 * p + lv)
                    V(v.tensor_copy(Xs[:].rearrange(flat), S2[:]), E("invx_sb"))
                    if lv < 5:
                        level_of(lv + 1)
                    dve.wait_ge(E("inv_full"), 5 * p + lv)
                    if lv < 5:
                        V(v.tensor_tensor(part(Tm[:], 0), part(Tm[:], 0), packed_in(PT2[:, 0:HALF]), ALU.add))
                    V(v.tensor_tensor(part(TT[:], 1), part(TT[:], 1), packed_in(S2[:, 0:HALF]), ALU.add), E("inv_sb"))
                V(v.memset(SV[lo_, 0, 0, 0, :], 0.0))
                V(v.memset(SV[hi_, 1, 0, 0, :], 0.0), E("state"))
                for c in range(NCH):
                    n = NCH * p + c
                    dve.wait_ge(E("sx_full"), n + 1)
                    V(v.tensor_copy(xs[:], PV[:, 0:C]), E("sx_sb"))
                    for hh, r in enumerate(rows2):
                        V(v.tensor_scalar(se[r, :], SV[r, hh, 0, c, :], e_end[r, c:c + 1], None, ALU.mult))
                    dve.wait_ge(E("su_full"), n + 1)
                    V(v.tensor_copy(SV[lo_, 0, 1, c, :], MB[lo_, 0:C]), E("su_even"))
                    if c < NCH - 1:
                        dve.wait_ge(E("ss_full"), 15 * p + c + 1)
                        for hh, r in enumerate(rows2):
                            V(v.scalar_tensor_tensor(SV[r, hh, 0, c + 1, :], PT2[r, 0:C], e_end[r, c:c + 1], se[r, :], ALU.mult, ALU.add),
                              E("state") if hh else None)
                    if p < PAIRS - 1 and c in MIX_AT:
                        i = MIX_AT.index(c)
                        mixed(U_SIDE[p] + 3 + i, raw_of[i], 4 * i + p + 1)
                z = oF[:, 4 + p, :]
                u = U_SIDE[p + 1] - 1
                for h in range(2):
                    dve.wait_ge(E("zr_tanh"), 2 * p + h + 1)
                    cs = slice(HALF * h, HALF * h + HALF)
                    V(v.scalar_tensor_tensor(z[:, cs], z[:, cs], 1.0, G[h][:], ALU.add, ALU.mult), emptied(u, h))
                dve.wait_ge(E("centred_full"), p + 1)
                dve.wait_ge(E("y_sq"), p + 1)
                V(v.tensor_scalar(yc[:], PT2[:], half_ln_w[:, one], None, ALU.mult), E("y_centred"))
                dve.wait_ge(E("var_full"), p + 1)
                V(v.tensor_scalar(stat[:, 128:144], PV[:, 0:16], 1.0 / C, GN_EPS, ALU.mult, ALU.add), E("y_var"))
                V(v.tensor_tensor(yc[:], yc[:], z, ALU.mult))
                dve.wait_ge(E("y_sd"), p + 1)
                V(v.reciprocal(stat[:, 128:144], stat[:, 128:144]), E("y_rstd"))
                V(v.scalar_tensor_tensor(bon[:], bon[:], chan["rwkv_ln_b"][:, one], z, ALU.add, ALU.mult))
                dve.wait_ge(E("y_rstd_full"), p + 1)
                V(v.tensor_tensor(yc[:], yc[:], S2[:], ALU.mult), E("y_normed"))
                V(v.scalar_tensor_tensor(z, bon[:], 0.5, yc[:], ALU.mult, ALU.add), E("pair_done"))

            dve.wait_ge(E("gate_out"), 16 * 32)
            for k in range(8):
                dve.wait_ge(E("high_part"), PART["o"] + k + 1)
                V(v.tensor_tensor(olo[:, k, :], oF[:, k, :] if k >= 4 else oA[k][:], ohi[:, k, :].bitcast(F32), ALU.subtract), E("low_part"))

            def merged_low(j):
                dve.wait_ge(E("high_part"), PART["m"] + j + 1)
                V(v.scalar_tensor_tensor(mlo[:, j, 0, :], gates[:, 2 * j + 1, :], 0.5, mhi[:, j, :].bitcast(F32), ALU.mult, ALU.subtract), E("low_part"))

            dve.wait_ge(E("gates_in"), 64)
            for j in range(KT):
                u = U_M + 2 * j
                for i in range(2):
                    for h in range(2):
                        cs = slice(HALF * h, HALF * h + HALF)
                        wait_full(dve, u + i, h)
                        V(v.scalar_tensor_tensor(gates[:, 2 * j + i, cs], gates[:, 2 * j + i, cs], 1.0, G[h][:], ALU.add, ALU.mult), emptied(u + i, h))
                V(v.tensor_tensor(gates[:, 2 * j + 1, :], gates[:, 2 * j, :], gates[:, 2 * j + 1, :], ALU.add), E("merged"))
                if j:
                    merged_low(j - 1)
            merged_low(KT - 1)

            norms = [0]

            def rstd():
                norms[0] += 1
                col = stat[:, 344:352]
                dve.wait_ge(E("sq_used"), KT * norms[0])
                V(v.tensor_scalar(col, PV[:, 0:8], 1.0 / D, EPS, ALU.mult, ALU.add), E("norm_var"))
                dve.wait_ge(E("norm_sd"), norms[0])
                V(v.reciprocal(col, col), E("rstd"))
                dve.wait_ge(E("nrs"), norms[0])

            h_seen = [0]

            def split_h(scaled, dst_lo, first, hi_buf):
                bufs = (nsq, nsum)
                for k in range(KT + 1):
                    if k < KT:
                        h_seen[0] += 1
                        V(scaled(k, bufs[k % 2][:]), E("h_tmp"))
                    if k:
                        dve.wait_ge(E("high_part"), first + k)
                        V(v.tensor_tensor(dst_lo[:, k - 1, :], bufs[(k - 1) % 2][:], hi_buf[:, k - 1, :].bitcast(F32), ALU.subtract), E("low_part"))

            rstd()
            g_ = gain["post_norm_gain"]
            for k in range(KT):
                V(v.scalar_tensor_tensor(y1[:, k, :], y1[:, k, :], g_[:, k:k + 1], nrs[:], ALU.mult, ALU.mult))
                dve.wait_ge(E("xb_tr"), k + 1)
                V(v.tensor_tensor(y1[:, k, :], y1[:, k, :], (PT2, S2)[k % 2][:], ALU.add), E("x2"))
            rstd()
            g2 = gain["a_pre_g_2"]
            split_h(lambda k, b: v.scalar_tensor_tensor(b, y1[:, k, :], g2[:, k:k + 1], nrs[:], ALU.mult, ALU.mult), h2lo, PART["h2"], h2hi)

            bn = stat[:, 128:320].rearrange("p (n s x) -> p n s x", n=8, s=4)
            mv = stat[:, 320:336].rearrange("p (n x) -> p n x", n=8)

            def gate_z(i):
                for h in range(2):
                    dve.wait_ge(E("zg_tanh"), 2 * i + h + 1)
                    z = zg[:, HALF * h:HALF * h + HALF]
                    V(v.scalar_tensor_tensor(z, z, 1.0, G[h][:], ALU.add, ALU.mult), emptied(U_UZ + 2 * i + 1, h))

            for i in range(16):
                for t in range(2):
                    dve.wait_ge(E("vg_tr"), 2 * i + t + 1)
                    V(v.tensor_copy(vln[:, 4 * t:4 * t + 4, i * P:i * P + P], PT2[:, HALF * t:HALF * t + HALF].rearrange("p (n c) -> p n c", n=4)),
                      E("vln_rows"))
                if i % 4 == 3:
                    for n in range(8):
                        V(v.bn_stats(bn[:, n, i // 4, :], vln[:, n, HALF * (i // 4):HALF * (i // 4) + HALF]))
                if i == 0:
                    dve.wait_ge(E("ws_tr"), 1)
                    V(v.tensor_tensor(wsT[:], S2[:].rearrange("p (g t) -> p g t", g=8), causal.unsqueeze(1).to_broadcast([P, 8, P]), ALU.mult), E("ws_t"))
                    dve.wait_ge(E("rowsum_full"), 1)
                    V(v.tensor_copy(rowsum[:], S2[:].rearrange("p (g t) -> p g t", g=8)), E("rowsum"))
            for n in range(8):
                V(v.bn_aggr(mv[:, n, :], bn[:, n, :, :]))
            V(v.tensor_scalar(stat[:, 336:344], mv[:, :, 1], EPS, None, ALU.add), E("ln_var"))
            dve.wait_ge(E("ln_sd"), 1)
            V(v.reciprocal(stat[:, 336:344], stat[:, 336:344]))
            V(v.scalar_tensor_tensor(stat[:, 344:352], mv[:, :, 0], -1.0, stat[:, 336:344], ALU.mult, ALU.mult), E("ln_stats"))
            gate_z(0)
            for n in range(4):
                V(v.tensor_scalar(vln[:, n, :], vln[:, n, :], mv[:, n, 0:1], stat[:, 336 + n:337 + n], ALU.subtract, ALU.mult), E("v_normed"))
            dve.wait_ge(E("ws_in"), 32)
            for i in range(16):
                g = i // 2
                V(v.scalar_tensor_tensor(btile[:], rowsum[:, g, :], ln_b[:, i:i + 1], bsb[:, g, :], ALU.mult, ALU.add))
                if i:
                    gate_z(i)
                dve.wait_ge(E("sgu_full"), i + 1)
                V(v.scalar_tensor_tensor(sg[:].rearrange("p (n t) -> p n t", n=8), S2[:].rearrange("p (n t) -> p n t", n=8), ln_g[:, i:i + 1],
                                         btile[:].unsqueeze(1).to_broadcast([P, 8, P]), ALU.mult, ALU.add), E("s_sb"))
                for h in range(2):
                    dve.wait_ge(g_evac[h], outs_before[U_UZ + 2 * i] + 1)
                V(v.tensor_tensor(sg[:], sg[:], ug[:], ALU.mult), E("u_used"))
                V(v.scalar_tensor_tensor(vln[:, :, i * P:i * P + P], sg[:].rearrange("p (n t) -> p n t", n=8), 0.5,
                                         zg[:].rearrange("p (n t) -> p n t", n=8), ALU.mult, ALU.mult), E("y_mlp"))
            for i in range(16):
                dve.wait_ge(E("high_part"), PART["y"] + i + 1)
                V(v.tensor_tensor(ylo[:, :, i * P:i * P + P], vln[:, :, i * P:i * P + P], yhi[:, i, :].bitcast(F32).rearrange("p (n t) -> p n t", n=8),
                                  ALU.subtract), E("low_part"))
            rstd()
            dve.wait_ge(E("res_in"), 16)
            g_ = gain["a_post_g_2"]
            for k in range(KT):
                V(v.scalar_tensor_tensor(y2[:, k, :], y2[:, k, :], g_[:, k:k + 1], nrs[:], ALU.mult, ALU.mult))
                V(v.tensor_tensor(y2[:, k, :], y2[:, k, :], res[:, k, :], ALU.add), E("x3"))
            rstd()
            split_h(lambda k, b: v.tensor_tensor(b, y2[:, k, :], nrs[:], ALU.mult), xnlo, PART["xn"], xnhi)

            for j in range(2):
                dve.wait_ge(E("v2_tr"), j + 1)
                V(v.tensor_copy(vt2[:, :, j * P:j * P + P], PT2[:].rearrange("p (n c) -> p n c", n=8)), E("v2_rows"))

            def biased2(c):
                i, hh, t = c // 4, c // 2 % 2, c % 2
                dve.wait_ge(E("s_full"), len(quads) + c + 1)
                dve.wait_ge(E("exp_done"), len(quads) + c)
                for ti in range(4):
                    lo = P if 4 * t + ti == 0 else 0
                    col = c % 2 * 4 + ti
                    V(v.tensor_tensor_reduce(out=neg2[:, ti, lo:256], in0=S2[:, ti * 256 + lo:ti * 256 + 256], in1=alibi[:, i % 2, hh, lo:256],
                                             scale=-1.0, scalar=3e38, op0=ALU.add, op1=ALU.min, accum_out=negm[:, col:col + 1]))
                cols = slice(c % 2 * 4, c % 2 * 4 + 4)
                V(v.tensor_scalar(negm[:, cols], negm[:, cols], neg_sink[:, 2 * i + hh:2 * i + hh + 1], None, ALU.min), E("ttr_done"))

            def normalised2(c):
                t = c % 2
                dve.wait_ge(E("exp_done"), len(quads) + c + 1)
                den, es = stat[:, 352:356], stat[:, 356:360]
                V(v.tensor_tensor(den, den, es, ALU.add))
                V(v.reciprocal(den, den))
                for ti in range(4):
                    lo = P if 4 * t + ti == 0 else 0
                    V(v.tensor_scalar(pr2[:, ti, lo:256], pr2[:, ti, lo:256], stat[:, 352 + ti:353 + ti], None, ALU.mult), E("pn_done") if ti == 3 else None)

            def gated2(c):
                i, hh, t = c // 4, c // 2 % 2, c % 2
                dve.wait_ge(E("pv_full"), len(quads) + c + 1)
                r, cs = rows2[hh], slice(HALF * t, HALF * t + HALF)
                V(v.scalar_tensor_tensor(ys[r, i, cs], PV[r, :], 0.5, zs2[r, i % 2, cs], ALU.mult, ALU.mult), E("pv_free"))

            for s in range(4 * QP + 5):
                c = s - 3
                if s % 4 == 0 and s // 4 < QP:
                    i = s // 4
                    for hh in range(2):
                        slope = 2.0 ** (-8.0 * (2 * i + hh + 1) / 16)
                        V(v.tensor_scalar(alibi[:, i % 2, hh, :], far, -slope, None, ALU.mult))
                if 0 <= c - 1 < 4 * QP:
                    normalised2(c - 1)
                if 0 <= c < 4 * QP:
                    biased2(c)
                if 0 <= c - 2 < 4 * QP:
                    gated2(c - 2)
                if s < 4 * QP and s % 4 >= 2:
                    i, h = s // 4, s % 2
                    dve.wait_ge(E("z2_tanh"), 2 * i + h + 1)
                    z = zs2[:, i % 2, HALF * h:HALF * h + HALF]
                    V(v.scalar_tensor_tensor(z, z, 1.0, G[h][:], ALU.add, ALU.mult), emptied(U_QZ + 2 * i + 1, h))
            V(v.memset(stat[:, 382:383], 0.0), E("ys_done"))
            for k in range(QP):
                dve.wait_ge(E("high_part"), PART["ys"] + k + 1)
                V(v.tensor_tensor(yslo[:, k, :], ys[:, k, :], yshi[:, k, :].bitcast(F32), ALU.subtract), E("low_part"))
            rstd()
            dve.wait_ge(E("x3_in"), 16)
            g_ = gain["b_post_g_2"]
            for k in range(KT):
                V(v.scalar_tensor_tensor(y3[:, k, :], y3[:, k, :], g_[:, k:k + 1], nrs[:], ALU.mult, ALU.mult))
                V(v.tensor_tensor(y3[:, k, :], y3[:, k, :], x3[:, k, :], ALU.add), E("x4"))

        @block.scalar
        def _(act):
            A = Own(act, E("act_chain"))
            a = nc.scalar
            act.dma_start(cst[:], d["shape_consts"]).then_inc(E("c_in"), 16)
            act.dma_start(hot_sb[:], d["bucket_hot"]).then_inc(E("hot_in"), 16)
            act.dma_start(rb33[0:32, :], d["rel_bias"]).then_inc(E("hot_in"), 16)
            n_prm, row = 0, 0
            vectors = [*gain, "rwkv_shift_mix", *chan, "a_ln_g_2", "a_ln_b_2"]
            for n in vectors:
                src = d[n] if n == "kv_norm_g_2" else d[n][0].rearrange("h c -> (h c)") if n == "rwkv_r_k" else d[n][0]
                k = src.shape[0] // P
                dst = prm_rows2[:, :] if n == "a_ln_b_2" else prm_rows[row:row + k, :]
                act.dma_start(dst, src.rearrange("(k p) -> k p", p=P)).then_inc(E("prm_in"), 16)
                n_prm, row = n_prm + 16, row + k
            act.dma_start(sink, d["b_sinks_2"].to_broadcast([P, 16])).then_inc(E("sink_in"), 16)
            for hf in range(2):
                for i in range(4 * hf, 4 * hf + 4):
                    act.wait_ge(E(f"x_in{hf}"), 64)
                    A(a.activation(sq0[:], xt[:, i, :], ACT.Square, accum_out=stat[:, i:i + 1]), E("squares"))
                act.wait_ge(E("mean_sq0"), hf + 1)
                A(a.activation(stat[:, 8 + 4 * hf:12 + 4 * hf], stat[:, 8 + 4 * hf:12 + 4 * hf], ACT.Sqrt), E("sqrt0"))
            for g in range(GROUPS):
                act.wait_ge(E("line_full"), g + 1)
                A(a.activation(lines[:, g, :], PV[0:8, 0:LINE], ACT.Copy), E("line_sb"))
                act.dma_start(lines_d[g], lines[:, g, :].unsqueeze(1).to_broadcast([8, P, LINE])).then_inc(E(f"lines_out{g}"), 16)
            act.wait_ge(E("prm_tr"), 1)
            A(a.activation(prm[:, 0:129], MB[:, 0:129], ACT.Copy), E("prm_sb"))
            act.wait_ge(E("sink_in"), 16)
            A(a.mul(half_w0, chan["rwkv_w0"], 0.5))
            A(a.mul(half_a0, chan["rwkv_a0"], 0.5))
            A(a.mul(neg_sink, sink, -1.0))
            A(a.mul(half_k_a, chan["rwkv_k_a"], 0.5))
            A(a.activation(less_k_a, half_k_a, ACT.Copy, bias=1.0, scale=-1.0))
            A(a.mul(half_ln_w, chan["rwkv_ln_w"], 0.5), E("prm_derived"))
            for f in range(16):
                hf, kk_ = f // 8, f % 8
                act.wait_ge(E("x_tr"), f + 1)
                A(a.activation(h1hi[:, kk_, HALF * hf:HALF * hf + HALF], setup_bank[f % 4], ACT.Copy, scale=gain["pre_norm_gain"][:, kk_:kk_ + 1]), E("h1_hi"))
            for g in range(GROUPS):
                act.wait_ge(E(f"lines_out{g}"), 16)

            def copy_back(c):
                p, g, hh, t = quads[c]
                act.wait_ge(E("pt_full"), c + 1)
                if c > 0:
                    act.wait_ge(E("pv_full"), c)
                todo = runs(g, t)
                src = PT2[:].rearrange("p (n k) -> p n k", n=4)
                for j, (sl, b0) in enumerate(todo):
                    A(a.activation(ptsb[:, sl, b0 * P:256], src[:, sl, b0 * P:256], ACT.Copy), E("pt_done") if j == len(todo) - 1 else None)

            def exps(c):
                p, g, hh, t = quads[c]
                act.wait_ge(E("ttr_done"), c + 1)
                if c > 0:
                    act.wait_ge(E("pt_full"), c)
                for i in range(4):
                    lo = key_blocks(g, 4 * t + i)[0] * P
                    col = c % 4 * 4 + i
                    A(a.activation(prob[:, i, lo:256], negl[:, i, lo:256], ACT.Exp, bias=negm[:, col:col + 1], scale=-1.0),
                      E("exp_done") if i == 3 else None)

            for s in range(A_END + 1):
                if s >= 25 and (s - 25) % 20 == 0:
                    p = (s - 25) // 20
                    act.wait_ge(E("fin_done"), p + 1)
                    act.dma_start(oA_d[p], og[:]).then_inc(E("oa_out"), 16)
                if s - 1 in slot_of:
                    copy_back(slot_of[s - 1])
                if s in slot_of:
                    exps(slot_of[s])
                if s - 2 in slot_of and quads[slot_of[s - 2]][1]:
                    c = slot_of[s - 2]
                    k = sum(1 for q in quads[:c] if q[1]) + 1
                    act.wait_ge(E("ab_ready"), k)
                    A(a.activation(eab[:], eab[:], ACT.Exp), E("eab_done"))
                if s < A_SLOTS:
                    u, h = s // 2, s % 2
                    p, r = u // 10, u % 10
                    g, gi = r // 3, 3 * p + r // 3
                    if r == 9:
                        wait_full(act, u, h)
                        if p > 0:
                            act.wait_ge(E("fin_done"), p)
                        A(a.activation(zs[:, HALF * h:HALF * h + HALF], G[h][:], ACT.Tanh, scale=0.5), E("z_tanh"))
                    elif r % 3 < 2:
                        wait_full(act, u, h)
                        if gi >= 2:
                            act.wait_ge(E("s_full"), 4 * (gi - 1))
                        dst = (qT, kT)[r % 3]
                        A(a.activation(perm_half(dst[:, gi % 2, :], g, h), nat_half(G[h][:], g), ACT.Copy, scale=(0.125, 1.0)[r % 3]), emptied(u, h))
            act.wait_ge(E("oa_out"), 64)
            act.dma_start(upw[0:64, :], d["rwkv_w_up"][0]).then_inc(E("up_in"), 16)
            act.dma_start(upw[64:128, :], d["rwkv_a_up"][0]).then_inc(E("up_in"), 16)
            lo_, hi_ = slice(0, 64), slice(64, 128)

            def raw_half(u, h, dst):
                wait_full(act, u, h)
                A(a.activation(dst[:, HALF * h:HALF * h + HALF], G[h][:], ACT.Copy), emptied(u, h))

            def side_out(p, place):
                i0, i1 = SIDE[p][place]
                for e in range(i0 // 8, i1 // 8):
                    ui, h = e // 2, e % 2
                    u = U_SIDE[p] + ui
                    if u == U_SIDE[p + 1] - 1:
                        wait_full(act, u, h)
                        A(a.activation(oF[:, 4 + p, HALF * h:HALF * h + HALF], G[h][:], ACT.Tanh, scale=0.5), E("zr_tanh"))
                    elif p < PAIRS - 1 and ui >= 3:
                        act.wait_ge(E("ak_ready"), p + 1)
                        if ui == 5:
                            act.wait_ge(E("vr_tr"), 5 * p + 5)
                        raw_half(u, h, raw_of[ui - 3])
                    else:
                        n = 2 * (3 * p + ui) + h
                        buf = gate_out_sb if p < PAIRS - 1 else gate_out_sb2
                        wait_full(act, u, h)
                        if 16 * n > 0:
                            act.wait_ge(E("gate_out"), 16 * n)
                        A(a.activation(buf[:], G[h][:], ACT.Tanh, scale=0.5), emptied(u, h))
                        act.dma_start(gates_d[:, 3 * p + ui, HALF * h:HALF * h + HALF], buf[:]).then_inc(E("gate_out"), 16)

            for h in range(2):
                raw_half(U_R, h, lora)
            for i in range(3):
                for h in range(2):
                    raw_half(U_R + 1 + i, h, raw_of[i])
                if i == 0:
                    act.wait_ge(E("mixed"), 1)
                    A(a.activation(lora[0:64, :], lora[0:64, :], ACT.Tanh), E("lora_tanh"))
            half_rate = -0.5 * math.exp(-0.5)
            for p in range(PAIRS):
                one = slice(p, p + 1)
                act.wait_ge(E("mixed"), 3 * p + 3)
                A(a.activation(ksq[:], rkT[:], ACT.Square, scale=chan["rwkv_k_k"][:, one]), E("k_sq"))
                act.wait_ge(E("a_full"), p + 1)
                act.wait_ge(E("mixed"), 3 * p + 4)
                A(a.activation(aT[:], PT2[:], ACT.Tanh, bias=half_a0[:, one], scale=0.5), E("a_tanh"))
                A(a.activation(kgain[:], aT[:], ACT.Identity, bias=less_k_a[:, one], scale=half_k_a[:, one]), E("k_gain"))
                act.wait_ge(E("lw_full"), p + 1)
                A(a.activation(logw[:], S2[:], ACT.Tanh, bias=half_w0[:, one], scale=0.5), E("lw_tanh"))
                A(a.activation(logw[:], logw[:], ACT.Copy, bias=half_rate, scale=half_rate), E("logw"))
                A(a.activation(aT[:], aT[:], ACT.Copy, bias=0.5, scale=0.5), E("a_sig"))
                side_out(p, "in")
                act.wait_ge(E("knorm_sb"), p + 1)
                A(a.activation(stat[:, 112:128], stat[:, 112:128], ACT.Sqrt), E("k_sqrt"))
                act.wait_ge(E("cum"), p + 1)
                A(a.activation(ec[:], cum[:], ACT.Exp))
                A(a.activation(logw[:], logw[:], ACT.Exp))
                A(a.activation(cum[:], cum[:], ACT.Exp, scale=-1.0), E("exps"))
                side_out(p, "norm")
                side_out(p, "bonus")
                for f in range(4):
                    side_out(p, f"amat{f}")
                for f in range(4):
                    act.wait_ge(E("bk_tr"), 4 * p + f + 1)
                    A(a.activation(BKt[:, 4 * f:4 * f + 4, :], (PV, MB)[f % 2][:].rearrange("p (n c) -> p n c", n=4), ACT.Copy), E("bk_rows"))
                for f in range(5):
                    bank = (PV, MB)[f % 2][:].rearrange("p (w x c) -> p w x c", w=4, x=2)
                    act.wait_ge(E("vr_tr"), 5 * p + f + 1)
                    w0, w1 = 4 * f, min(4 * f + 4, 17)
                    s0 = 1 if w0 == 0 else 0
                    for kind in range(2):
                        A(a.activation(SV[lo_, 1, kind, w0 + s0 - 1:w1 - 1, :], bank[lo_, s0:w1 - w0, 1, :], ACT.Copy), E("vr_odd") if kind else None)
                side_out(p, "rows")
                for i in range(11):
                    side_out(p, f"inv{i}")
                if p == PAIRS - 1:
                    act.wait_ge(E("inv_sb"), 6 * PAIRS)
                    for k in range(4):
                        act.dma_start(oA[k][:], oA_d[k]).then_inc(E("oa_in"), 16)
                for c in range(NCH):
                    side_out(p, f"scan{2 * c}")
                    act.wait_ge(E("su_full"), NCH * p + c + 1)
                    A(a.activation(SV[hi_, 1, 1, c, :], MB[hi_, 0:C], ACT.Copy), E("su_odd"))
                    side_out(p, f"scan{2 * c + 1}")
                act.wait_ge(E("y_full"), p + 1)
                A(a.activation(yT[:], S2[:], ACT.Copy), E("y_sb"))
                if p == PAIRS - 1:
                    act.wait_ge(E("oa_in"), 64)
                    for k in range(3):
                        A(a.activation(ohi[:, k, :], oA[k][:], ACT.Copy), E("high_part"))
                act.wait_ge(E("centred_full"), p + 1)
                A(a.activation(ysq[:], PT2[:], ACT.Square), E("y_sq"))
                act.wait_ge(E("y_var"), p + 1)
                A(a.activation(stat[:, 128:144], stat[:, 128:144], ACT.Sqrt), E("y_sd"))

            act.wait_ge(E("gate_out"), 16 * 32)
            act.wait_ge(w_used, U_M)
            for j in range(4):
                act.dma_start(gates[:, 4 * j:4 * j + 4, :], gates_d[:, 4 * j:4 * j + 4, :]).then_inc(E("gates_in"), 16)
            act.wait_ge(E("pair_done"), 4)
            for k in range(3, 8):
                if k >= 6:
                    act.wait_ge(E("low_part"), PART["o"] + 2 * (k - 6) + 1)
                A(a.activation(ohi[:, k, :], oF[:, k, :] if k >= 4 else oA[k][:], ACT.Copy), E("high_part"))
            for j in range(KT):
                act.wait_ge(E("merged"), j + 1)
                A(a.activation(mhi[:, j, :], gates[:, 2 * j + 1, :], ACT.Copy, scale=0.5), E("high_part"))
            act.wait_ge(w_used, U_O)
            for n in range(8):
                act.dma_start(xt2[:, n, :], d["x"][0, n * P:(n + 1) * P, :]).then_inc(E(f"x_in{n // 4}"), 16)

            sq_n = [0, 0]

            def square(src, k):
                sq_n[0] += 1
                if sq_n[0] - 2 > 0:
                    act.wait_ge(E("sq_used"), sq_n[0] - 2)
                A(a.activation(sq_buf[k % 2][:], src[:, k, :], ACT.Square), E("sq"))

            def root():
                sq_n[1] += 1
                act.wait_ge(E("norm_var"), sq_n[1])
                A(a.activation(stat[:, 344:352], stat[:, 344:352], ACT.Sqrt), E("norm_sd"))
                act.wait_ge(E("rstd_full"), sq_n[1])
                A(a.activation(nrs[:], S2[:], ACT.Copy), E("nrs"))

            def product_tile(u, dst, j):
                for h in range(2):
                    wait_full(act, u, h)
                    A(a.activation(dst[:, j, HALF * h:HALF * h + HALF], G[h][:], ACT.Copy), emptied(u, h))
                square(dst, j)

            h_n = [0]

            def high_parts(dst):
                for k in range(KT):
                    h_n[0] += 1
                    act.wait_ge(E("h_tmp"), h_n[0])
                    A(a.activation(dst[:, k, :], (nsq, nsum)[k % 2][:], ACT.Copy), E("high_part"))

            for j in range(KT):
                product_tile(U_O + j, y1, j)
            root()
            for k in range(KT):
                act.wait_ge(E("x2"), k + 1)
                if k == KT - 1:
                    act.dma_start(x2_d, y1[:]).then_inc(E("x2_out"), 16)
                square(y1, k)
            root()
            high_parts(h2hi)
            act.wait_ge(E("x2_out"), 16)

            act.wait_ge(E("low_part"), PART["h2"] + 8)
            act.dma_start(wsr[:], d["a_w_s_2"][0].rearrange("g t s -> t g s")).then_inc(E("ws_in"), 16)
            act.dma_start(bsb[:], d["a_b_s_2"][0:1].to_broadcast([P, 8, P])).then_inc(E("ws_in"), 16)
            for i in range(16):
                if 2 * i > 0:
                    act.wait_ge(E("vg_tr"), 2 * i)
                for h in range(2):
                    wait_full(act, U_V + i, h)
                    A(a.activation(vg[:, HALF * h:HALF * h + HALF], G[h][:], ACT.Gelu_apprx_tanh), emptied(U_V + i, h))
            act.wait_ge(E("ln_var"), 1)
            A(a.activation(stat[:, 336:344], stat[:, 336:344], ACT.Sqrt), E("ln_sd"))
            for i in range(16):
                if i > 0:
                    act.wait_ge(E("u_used"), i)
                for h in range(2):
                    wait_full(act, U_UZ + 2 * i, h)
                    A(a.activation(ug[:, HALF * h:HALF * h + HALF], G[h][:], ACT.Gelu_apprx_tanh), emptied(U_UZ + 2 * i, h))
                if i == 0:
                    act.wait_ge(E("ln_stats"), 1)
                    for n in range(4, 8):
                        A(a.activation(vln[:, n, :], vln[:, n, :], ACT.Identity, bias=stat[:, 344 + n:345 + n], scale=stat[:, 336 + n:337 + n]), E("v_normed_act"))
                if i > 0:
                    act.wait_ge(E("y_mlp"), i)
                for h in range(2):
                    wait_full(act, U_UZ + 2 * i + 1, h)
                    A(a.activation(zg[:, HALF * h:HALF * h + HALF], G[h][:], ACT.Tanh, scale=0.5), E("zg_tanh"))
            act.wait_ge(w_used, U_AO)
            for i in range(16):
                act.wait_ge(E("y_mlp"), i + 1)
                A(a.activation(yhi[:, i, :].rearrange("p (n t) -> p n t", n=8), vln[:, :, i * P:i * P + P], ACT.Copy), E("high_part"))
            for j in range(KT):
                if j == KT - 1:
                    act.wait_ge(w_used, U_KV - 1)
                    act.dma_start(res[:], x2_d).then_inc(E("res_in"), 16)
                product_tile(U_AO + 2 * j + 1, y2, j)
            root()
            for k in range(KT):
                act.wait_ge(E("x3"), k + 1)
                if k == KT - 1:
                    act.dma_start(x3_d, y2[:]).then_inc(E("x3_out"), 16)
                square(y2, k)
            root()
            high_parts(xnhi)
            act.wait_ge(E("x3_out"), 16)

            lo_ = slice(0, 64)
            act.wait_ge(E("low_part"), PART["xn"] + 8)
            for j in range(2):
                for h in range(2):
                    wait_full(act, U_KV + j, h)
                    cs = slice(HALF * h, HALF * h + HALF)
                    for m in range(2):
                        src = G[h][(lo_, hi_)[m], :]
                        A(a.activation(kd[lo_, 2 * j + m, cs], src, ACT.Copy))
                        A(a.activation(kd[hi_, 2 * j + m, cs], src, ACT.Copy), emptied(U_KV + j, h) if m else None)
            for j in range(2):
                if j > 0:
                    act.wait_ge(E("v2_tr"), j)
                for h in range(2):
                    wait_full(act, U_KV + 2 + j, h)
                    A(a.activation(v2T[:, HALF * h:HALF * h + HALF], G[h][:], ACT.Copy), emptied(U_KV + 2 + j, h))

            def copy_back2(c):
                act.wait_ge(E("pt_full"), len(quads) + c + 1)
                act.wait_ge(E("pv_full"), len(quads) + c)
                src = PT2[:].rearrange("p (n k) -> p n k", n=4)
                if c % 2 == 0:
                    A(a.activation(pts2[:, 0, P:256], src[:, 0, P:256], ACT.Copy))
                    A(a.activation(pts2[:, 1:4, :], src[:, 1:4, :], ACT.Copy), E("pt_done"))
                else:
                    A(a.activation(pts2[:], src, ACT.Copy), E("pt_done"))

            def exps2(c):
                i, hh, t = c // 4, c // 2 % 2, c % 2
                act.wait_ge(E("ttr_done"), len(quads) + c + 1)
                act.wait_ge(E("pt_full"), len(quads) + c)
                cols = slice(c % 2 * 4, c % 2 * 4 + 4)
                for ti in range(4):
                    lo = P if 4 * t + ti == 0 else 0
                    col = c % 2 * 4 + ti
                    A(a.activation(pr2[:, ti, lo:256], neg2[:, ti, lo:256], ACT.Exp, bias=negm[:, col:col + 1], scale=-1.0, accum_out=stat[:, 352 + ti:353 + ti]))
                A(a.activation(stat[:, 356:360], negm[:, cols], ACT.Exp, bias=sink[:, 2 * i + hh:2 * i + hh + 1]), E("exp_done"))

            for s in range(4 * QP + 5):
                c = s - 3
                if 0 <= c - 1 < 4 * QP:
                    copy_back2(c - 1)
                if 0 <= c < 4 * QP:
                    exps2(c)
                if s < 4 * QP:
                    i, h = s // 4, s % 2
                    u = U_QZ + s // 2
                    wait_full(act, u, h)
                    cs = slice(HALF * h, HALF * h + HALF)
                    if s % 4 < 2:
                        act.wait_ge(E("s_full"), len(quads) + 4 * (i - 1))
                        A(a.activation(q2[:, i % 2, cs], G[h][:], ACT.Copy, scale=0.125), emptied(u, h))
                    else:
                        act.wait_ge(E("pv_free"), len(quads) + 4 * (i - 1))
                        A(a.activation(zs2[:, i % 2, cs], G[h][:], ACT.Tanh, scale=0.5), E("z2_tanh"))
            act.wait_ge(E("ys_done"), 1)
            act.dma_start(x3[:], x3_d).then_inc(E("x3_in"), 16)
            act.wait_ge(w_used, U_BO)
            for k in range(QP):
                A(a.activation(yshi[:, k, :], ys[:, k, :], ACT.Copy), E("high_part"))
            for j in range(KT):
                product_tile(U_BO + j, y3, j)
            root()
            for n in range(8):
                act.wait_ge(E("out_tr"), n + 1)
                A(a.activation(orow[:, n, :], (PT2, S2)[n % 2][:], ACT.Copy), E("rows_out"))
                act.dma_start(out[0, n * P:(n + 1) * P, :], orow[:, n, :]).then_inc(E("out_done"), 16)
            act.wait_ge(E("out_done"), 128)


_INS = ["x", "pre_norm_gain", "w_in", "rel_bias", "rwkv_shift_mix", "rwkv_w0", "rwkv_w_up", "rwkv_a0", "rwkv_a_up", "rwkv_k_k", "rwkv_k_a",
        "rwkv_r_k", "rwkv_ln_w", "rwkv_ln_b", "w_up_attn", "w_up_rwkv", "w_out", "post_norm_gain", "a_w_in_2", "a_ln_g_2", "a_ln_b_2",
        "a_w_s_2", "a_b_s_2", "a_w_out_2", "a_pre_g_2", "a_post_g_2", "kv_norm_g_2", "w_k_2", "w_v_2", "b_w_in_2", "b_sinks_2", "b_w_out_2",
        "b_pre_g_2", "b_post_g_2"]


def kernel(**inputs):
    import numpy as _np
    import concourse.bacc as _bacc
    from concourse import mybir as _mybir
    from concourse.bass_utils import run_bass_kernel_spmd as _run

    nc = _bacc.Bacc("TRN2", target_bir_lowering=False, num_devices=1)
    packed, hot = shape_constants()
    arrays, aps = {}, {}
    for name, a in [*((n, inputs[n]) for n in _INS), ("shape_consts", packed), ("bucket_hot", hot)]:
        a = _np.ascontiguousarray(a)
        arrays[f"in_{name}"] = a
        aps[name] = nc.dram_tensor(f"in_{name}", a.shape, _mybir.dt.from_np(a.dtype), kind="ExternalInput").ap()
    out = nc.dram_tensor("out_0", (1, T, D), F32, kind="ExternalOutput").ap()
    build(nc, aps, out)
    r = _run(nc, [arrays], core_ids=[0])
    return r.results[0]["out_0"]
```

```python
from contextlib import ExitStack
import math

import numpy as np
import concourse.bass as bass
from concourse import mybir

F32 = mybir.dt.float32
F32R = mybir.dt.float32r
ALU = mybir.AluOpType
ACT = mybir.ActivationFunctionType

P = 128
T = 1024
D = 1024
HALF = 512
KT = D // P
PAIRS = 4
GROUPS = 3
DILATION = (1, 4, 16)
ATTN = 512
C = 64
NCH = T // C
LINE = 384
OFF_Q, OFF_K, OFF_V = 0, 1536, 3072
OFF_ZA, OFF_R, OFF_RK, OFF_RV, OFF_LORA, OFF_ZR = 4608, 5120, 5632, 6144, 6656, 6784
OFF_GA, OFF_GR = 7296, 8320
AW = 2048
QP = 8
GATES_BEFORE = (0, 2, 6, 10, 16)
SIDE_PRE = (3, 2, 3, 2)
SIDE_IN, SIDE_NORM, SIDE_BONUS = 8, 4, 20
SIDE_AMAT, SIDE_ROWS, SIDE_INV = (2, 2, 2, 3), (3, 2, 2, 2, 2), 22 * (1,)
FAR = 1e30
EPS = 1e-6
GN_EPS = 64e-5
KB = 1024


def shape_constants():
    r = np.arange(P)
    j = r % C
    t = np.arange(C)
    ident = np.eye(P)
    blocks = (r[:, None] // C == r[None, :] // C)
    ones = np.ones((P, P))
    centre = ident - blocks / C
    strict, incl = j[:, None] < t[None, :], j[:, None] <= t[None, :]
    levels = []
    s = 1
    while s < C:
        levels.append((t[None, :] // (2 * s) == j[:, None] // (2 * s)) & (t[None, :] // s % 2 == 1) & (j[:, None] // s % 2 == 0))
        s *= 2
    ident2 = j[:, None] == t[None, :]
    causal = r[:, None] <= r[None, :]
    q, c = r[:, None], np.arange(2 * P)[None, :]
    dist = P + q - c
    far = np.where((dist >= 0) & (dist < P), dist, FAR)
    packed = np.concatenate([np.asarray(x, np.float32) for x in (ident, blocks, ones, centre, strict, incl, *levels, ident2, causal, far)], axis=1)
    rel = 255 - np.arange(LINE)
    hot = np.zeros((33, GROUPS, LINE), np.float32)
    for g, dil in enumerate(DILATION):
        d = np.maximum(rel, 0) * dil
        ratio = np.log(np.maximum(d, 1).astype(np.float32) / 16) / np.float32(math.log(2048 / 16))
        large = np.minimum(16 + (ratio * 16).astype(np.int32), 31)
        bucket = np.where(d < 16, d, large)
        ok = (rel >= 0) & (rel <= P)
        hot[bucket, g, np.arange(LINE)] = ok
        hot[32, g] = np.where(ok, 0.0, -FAR)
    return packed, hot


NCONST = 128 * 4 + 64 * 2 + 64 * 6 + 64 + 128 + 256


class Own:

    def __init__(self, eng, chain):
        self.eng, self.chain, self.count = eng, chain, {}

    def __call__(self, ins, signal=None):
        s, n = signal if isinstance(signal, tuple) else (signal, None)
        s = self.chain if s is None else s
        ins.then_inc(s, 1)
        n = self.count.get(s.name, 0) + 1 if n is None else n
        self.count[s.name] = n
        self.eng.wait_ge(s, n)


def build(nc, d, out):
    ctx = ExitStack()
    with ctx:
        base = (nc.sbuf_base + 255) // 256 * 256

        def at(name, kb, shape, dt=F32):
            n = int(np.prod(shape[1:])) * 4
            assert kb * KB + n <= 207 * KB + 512, (name, kb, n)
            return nc.alloc_sbuf_tensor_at(name, list(shape), dt, offset=base + int(kb * KB))

        def sem(name):
            return ctx.enter_context(nc.semaphore(name))

        G = [nc.alloc_psum_tensor(f"gemm{h}", [P, HALF], F32) for h in range(2)]
        S2 = nc.alloc_psum_tensor("scores", [P, 2 * HALF], F32)
        PT2 = nc.alloc_psum_tensor("probs_t", [P, 2 * HALF], F32)
        PV = nc.alloc_psum_tensor("weighted", [P, HALF], F32)
        MB = nc.alloc_psum_tensor("max_rows", [P, HALF], F32)
        setup_bank = (S2[:, 0:HALF], S2[:, HALF:], PT2[:, 0:HALF], PT2[:, HALF:])

        raw = at("w_raw", 0, [P, 2, KT, P])
        whi = at("w_hi", 8, [P, 2, KT, P], F32R)
        wlo = at("w_lo", 16, [P, 2, KT, P], F32R)
        cst = at("consts_sb", 24, [P, NCONST])
        ident = cst[:, 0:128]
        blocks = cst[:, 128:256]
        ones = cst[:, 256:384]
        centre = cst[:, 384:512]
        mask_a = cst[:, 512:640]
        level = [cst[:, 640 + 64 * i:704 + 64 * i] for i in range(6)]
        ident2 = cst[:, 1024:1088]
        causal = cst[:, 1088:1216]
        far = cst[:, 1216:1472]
        prm = at("params", 24 + 5.75, [P, 192])
        stat = at("stats", 24 + 6.5, [P, 384])
        gain = {n: prm[:, 8 * i:8 * i + 8] for i, n in enumerate(
            ("pre_norm_gain", "post_norm_gain", "a_pre_g_2", "a_post_g_2", "kv_norm_g_2", "b_pre_g_2", "b_post_g_2"))}
        mix = prm[:, 56:69]
        chan = {n: prm[:, 69 + 4 * i:73 + 4 * i] for i, n in enumerate(
            ("rwkv_w0", "rwkv_a0", "rwkv_k_k", "rwkv_k_a", "rwkv_r_k", "rwkv_ln_w", "rwkv_ln_b"))}
        ln_g, ln_b = prm[:, 97:113], prm[:, 113:129]
        half_w0, half_a0 = prm[:, 132:136], prm[:, 136:140]
        less_mix = stat[:, 16:29]
        half_k_a, less_k_a, half_ln_w = prm[:, 176:180], prm[:, 180:184], prm[:, 184:188]
        sink, neg_sink = prm[:, 144:160], prm[:, 160:176]

        h1hi, h1lo = at("h1_hi", 32, [P, KT, T], F32R), at("h1_lo", 64, [P, KT, T], F32R)
        xt = at("x_rows", 96, [P, 8, D])
        sq0 = at("x_squares", 128, [P, D])
        sq1 = at("x_squares_2", 132, [P, D])
        line_bank = (PV, G[0], G[1])
        hot_sb = at("hot_sb", 136, [33, GROUPS, LINE])
        rb33 = at("bias_table", 142, [33, 24])
        lines = at("bias_lines", 184, [8, GROUPS, LINE])
        qT, kT = at("q_t", 128, [P, 2, T]), at("k_t", 136, [P, 2, T])
        vT = at("v_t", 144, [P, T])
        vrows = at("v_rows_1", 148, [P, 2, 8, P])
        bias_t = at("bias_tile", 160, [P, 2, 2, 256])
        negl = at("neg_logits", 164, [P, 4, 256])
        prob = at("prob", 168, [P, 4, 256])
        ptsb = at("prob_t_sb", 172, [P, 4, 256])
        accu = at("num_den", 176, [P, 2, T])
        nmax = at("neg_max", 184, [P, 1, T])
        nnew = at("neg_max_new", 192, [P, 1, 256])
        eab = at("rescale", 194, [P, 2, 256])
        zs = at("z_silu", 198, [P, T])
        wide = at("den_max_wide", 124, [P, 2, 2, 2, 2, 64])
        og = at("o_gated", 202, [P, T])
        rd = at("recip_den", 108, [P, 1, T])
        rescaled = at("scaled_new", 156, [P, 2, 256])
        negm, den1 = stat[:, 64:80], stat[:, 80:96]
        upw = at("lora_up", 205.5, [P, 512])
        oF = at("o_f32", 96, [P, 8, T])
        lora = at("lora", 96, [P, T])
        rT, rkT, bon = at("r_t", 100, [P, T]), at("rk_t", 104, [P, T]), at("bonus", 108, [P, T])
        AM = at("a_mats", 128, [P, 2, NCH, 3, C])
        BK = at("b_k", 152, [P, NCH, 2, C])
        vpad = at("v_padded", 160, [P, C + T + C])
        raw_of = (rT[:], rkT[:], vpad[:, C:C + T])
        reset = at("chunk_reset", 201, [P, T])
        ksq, kgain = at("k_squares", 164.5, [P, T]), at("k_gain", 168.5, [P, T])
        rkr, kmod, kka = at("r_k_products", 173, [P, T]), at("k_mod", 177, [P, T]), at("kk_a", 181, [P, T])
        logw, cum = at("log_decay", 185, [P, T]), at("cum_decay", 189, [P, T])
        aT, kk = at("a_t", 193, [P, T]), at("kk_t", 197, [P, T])
        ec = at("e_cum", 201, [P, T])
        BKt = at("bk_rows", 164.5, [P, NCH, P])
        SV = at("state_and_v", 172.5, [P, 2, 2, NCH, C])
        Tm, TT = at("inv", 188.5, [P, NCH, C]), at("inv_t", 192.5, [P, NCH, C])
        Xs = at("inv_x", 196.5, [P, NCH, C])
        AmT = at("a_level", 152, [P, 2, NCH, C])
        Aab = at("a_ab", 200.5, [P, NCH, C])
        xs = at("scan_x", 205, [P, C])
        se = at("scan_state", 205.25, [P, C])
        e_end = stat[:, 96:112]
        yT, yc, ysq = at("y_t", 177, [P, T]), at("y_centred", 181, [P, T]), at("y_squares", 185, [P, T])
        oA = [at(f"attn_out{k}", kb, [P, T]) for k, kb in enumerate((152, 100, 104, 156))]
        ohi, olo = at("o_hi", 128, [P, 8, T], F32R), at("o_lo", 96, [P, 8, T], F32R)
        gates = at("merge_gates", 32, [P, 2 * KT, T])
        mhi, mlo = at("merged_hi", 160, [P, KT, T], F32R), at("merged_lo", 32, [P, KT, 2, T], F32R)
        y1 = at("block1_out", 96, [P, KT, T])
        xt2 = at("x_rows_again", 128, [P, 8, D])
        nsq = at("norm_squares", 192, [P, T])
        nsum = at("norm_sum", 196, [P, T])
        nrs = at("norm_rstd", 200, [P, T])
        sq_buf = (nsq, nsum)
        h2hi, h2lo = at("h2_hi", 32, [P, KT, T], F32R), at("h2_lo", 64, [P, KT, T], F32R)
        vln = at("mlp_v", 128, [P, 8, AW])
        wsT = at("ws_t", 96, [P, 8, P])
        rowsum = at("ws_rowsum", 100, [P, 8, P])
        bsb = at("bs_rows", 104, [P, 8, P])
        wsr = at("ws_raw", 108, [P, 8, P])
        btile = at("b_tile", 112, [P, P])
        zg = at("mlp_z", 116, [P, T])
        ug = at("mlp_u", 192, [P, T])
        sg = at("mlp_s", 196, [P, T])
        vg = at("mlp_vg", 124, [P, T])
        scaled_g = at("scaled_product", 120, [P, 2, HALF])
        yhi, ylo = at("mlp_y_hi", 32, [P, 16, T], F32R), at("mlp_y_lo", 128, [P, 8, AW], F32R)
        y2 = at("block2a_out", 96, [P, KT, T])
        res = at("residual", 32, [P, KT, T])
        xnhi, xnlo = at("xn_hi", 128, [P, KT, T], F32R), at("xn_lo", 160, [P, KT, T], F32R)
        kd = at("k_dup", 96, [P, 4, T])
        vt2 = at("v_rows", 112, [P, 8, 256])
        q2 = at("q2_t", 120, [P, 2, T])
        v2T = at("v2_t", 192, [P, T])
        ys = at("swa_y", 32, [P, QP, T])
        zs2 = at("z2_silu", 64, [P, 2, T])
        neg2 = at("neg_logits2", 72, [P, 4, 256])
        pr2 = at("prob2", 76, [P, 2, 4, 256])
        pts2 = at("prob2_t", 84, [P, 4, 256])
        scaled_s = at("scaled_product2", 92, [P, 2, HALF])
        den2 = stat[:, 352:368].rearrange("p (b x) -> p b x", b=2)
        alibi = at("alibi_tile", 88, [P, 2, 2, 256])
        yshi, yslo = at("swa_y_hi", 128, [P, QP, T], F32R), at("swa_y_lo", 160, [P, QP, T], F32R)
        y3 = at("block2b_out", 64, [P, KT, T])
        x3 = at("x3_again", 96, [P, KT, T])
        orow = at("out_rows", 160, [P, 8, D])

        lines_d = nc.dram_tensor("lines_scratch", (GROUPS, 8, P, LINE), F32).ap()
        oA_d = nc.dram_tensor("attn_out_scratch", (PAIRS, P, T), F32).ap()
        x2_d = nc.dram_tensor("x2_scratch", (P, KT, T), F32).ap()
        gates_d = nc.dram_tensor("gates_scratch", (P, 2 * KT, T), F32).ap()
        x3_d = nc.dram_tensor("x3_scratch", (P, KT, T), F32).ap()

        units = []

        def unit(name, w, rows, col, nk=KT):
            units.append((name, w[rows:rows + nk * P, col:col + P].rearrange("(k p) n -> p k n", p=P), nk))

        w_in = d["w_in"][0]
        for p in range(PAIRS):
            for g in range(GROUPS):
                for off in (OFF_Q, OFF_K, OFF_V):
                    unit("qkv", w_in, 0, off + g * ATTN + p * P)
            unit("za", w_in, 0, OFF_ZA + p * P)
        U_R = len(units)
        unit("lora", w_in, 0, OFF_LORA)
        for off in (OFF_R, OFF_RK, OFF_RV):
            unit("rwkv", w_in, 0, off)
        merge_gates = [off + j * P for j in range(KT) for off in (OFF_GA, OFF_GR)]
        U_SIDE = []
        for p in range(PAIRS):
            U_SIDE.append(len(units))
            last = p == PAIRS - 1
            for col in merge_gates[GATES_BEFORE[p]:GATES_BEFORE[p + 1]]:
                unit("gate", w_in, 0, col)
            if not last:
                for off in (OFF_R, OFF_RK, OFF_RV):
                    unit("rwkv", w_in, 0, off + (p + 1) * P)
            unit("zr", w_in, 0, OFF_ZR + p * P)
        U_M = len(units)
        U_SIDE.append(U_M)
        for j in range(KT):
            unit("ua", d["w_up_attn"][0], 0, j * P, 4)
            unit("ur", d["w_up_rwkv"][0], 0, j * P, 4)
        U_O = len(units)
        for j in range(KT):
            unit("wo", d["w_out"][0], 0, j * P)
        U_V = len(units)
        wa = d["a_w_in_2"][0]
        for i in range(16):
            unit("mv", wa, 0, AW + i * P)
        U_UZ = len(units)
        for i in range(16):
            unit("mu", wa, 0, i * P)
            unit("mz", wa, 0, 2 * AW + i * P)
        U_AO = len(units)
        for j in range(KT):
            unit("ao", d["a_w_out_2"][0], 0, j * P)
            unit("ao", d["a_w_out_2"][0], D, j * P)
        U_KV = len(units)
        for w in ("w_k_2", "w_v_2"):
            for j in range(2):
                unit("kv", d[w], 0, j * P)
        U_QZ = len(units)
        for i in range(QP):
            unit("q", d["b_w_in_2"][0], 0, i * P)
            unit("z", d["b_w_in_2"][0], 0, D + i * P)
        U_BO = len(units)
        for j in range(KT):
            unit("bo", d["b_w_out_2"][0], 0, j * P)
        U_END = len(units)
        outs_before, n = [], 0
        for u in range(U_END):
            outs_before.append(n)
            n += not (U_AO <= u < U_KV and (u - U_AO) % 2 == 0)
        BY_POOL = (True, False, True, False, True)
        SUMS_BEFORE = [sum(1 if b else KT for b in BY_POOL[:n]) for n in range(len(BY_POOL) + 1)]
        ADDS = KT - 2
        sq_add = {}
        for m, (u0, per) in enumerate(((U_O, 1), (U_AO, 2), (U_BO, 1))):
            for k in range(1, KT - 1):
                sq_add.setdefault(min(u0 + per * k + per + 1, U_END - 1), []).append((m, k))

        def side_plan(p):
            total = 16 * (U_SIDE[p + 1] - U_SIDE[p])
            counts = {f"pre{f}": SIDE_PRE[f] * (p > 0) for f in range(4)}
            counts.update({"in": SIDE_IN, "norm": SIDE_NORM, "bonus": SIDE_BONUS})
            counts.update({f"amat{f}": SIDE_AMAT[f] for f in range(4)})
            counts.update({f"rows{f}": SIDE_ROWS[f] for f in range(5)})
            counts.update({f"inv{i}": SIDE_INV[i] for i in range(22)})
            rest = total - sum(counts.values())
            first = sorted(range(3 * NCH), key=lambda i: (i % 3 == 0, i))
            counts.update({f"scan{i}": rest // len(first) + (first.index(i) < rest % len(first)) for i in range(3 * NCH)})
            plan, n = {}, 0
            for place, k in counts.items():
                plan[place] = (n, n + k)
                n += k
            assert n == total
            return plan

        chunk_half = (range(NCH // 2), range(NCH // 2, NCH))
        SIDE = [side_plan(p) for p in range(PAIRS)]

        quads = [(p, g, t) for p in range(PAIRS) for g in range(GROUPS) for t in range(4)]
        slot_of = {20 * p + 6 * g + 7 + t: c for c, (p, g, t) in enumerate(quads)}
        quad = [(i, i // 2, i % 2) for i in range(4)]
        pairwise = (quad[0], quad[2], quad[1], quad[3])
        v_slot = {20 * p + 6 * g + 7: 3 * p + g for p in range(PAIRS) for g in range(GROUPS)}
        A_SLOTS = 20 * PAIRS
        A_END = 20 * PAIRS + 5

        def key_blocks(g, n):
            first = n == 0 if g == 0 else (n % 2 == 0 if g == 1 else True)
            return (1,) if first else (0, 1)

        def runs(first):
            if first[0] == first[1]:
                return [(slice(0, 4), first[0])]
            return [(slice(i, 4, 2), b0) for i, b0 in enumerate(first)]

        def natural(ap, g, t):
            if g == 0:
                return ap[:, :, 256 * t:256 * t + 256]
            r = DILATION[g]
            return ap.rearrange("p x (l r) -> p x r l", r=r)[:, :, r // 4 * t:r // 4 * (t + 1), :]

        def permuted(ap, g):
            return ap if g == 0 else ap.rearrange("p x (r l) -> p x r l", r=DILATION[g] // 4)

        def perm_half(ap, g, h):
            if g == 0:
                return ap[:, HALF * h:HALF * h + HALF]
            r = DILATION[g]
            n = HALF // r
            return ap.rearrange("p (r l) -> p l r", r=r)[:, n * h:n * h + n, :]

        def nat_half(ap, g):
            return ap if g == 0 else ap.rearrange("p (l r) -> p l r", r=DILATION[g])

        made = {}

        def E(name):
            if name not in made:
                made[name] = sem(name)
            return made[name]

        PART = {"o": 0, "m": 8, "h2": 16, "y": 24, "xn": 40, "ys": 48}
        w_raw = [E("w_raw0"), E("w_raw1")]
        g_full = [E("gemm_full0"), E("w_used")]
        w_used = g_full[1]
        g_evac = [E("gemm_evac0"), E("gemm_evac1")]
        bias_in = [E("bias_in0"), E("bias_in1")]
        block = ctx.enter_context(nc.Block())

        def emptied(u, h):
            return g_evac[h], outs_before[u] + 1

        def wait_full(eng, u, h):
            eng.wait_ge(g_full[h], u + 1)

        @block.sync
        def _(sp):
            for i in range(8):
                sp.dma_start(xt[:, i, :], d["x"][0, i * P:(i + 1) * P, :]).then_inc(E(f"x_in{i // 4}"), 16)
            for u in range(U_END):
                name, src, nk = units[u]
                if u >= 2:
                    sp.wait_ge(E("w_split"), u - 1)
                sp.dma_start(raw[:, u % 2, 0:nk, :], src).then_inc(w_raw[u % 2], 16)
                if u < U_R and u % 10 in (2, 5, 8):
                    p, g = u // 10, u % 10 // 3
                    gi = 3 * p + g
                    b = gi % 2
                    if gi < GROUPS:
                        sp.wait_ge(E(f"lines_out{gi}"), 16)
                    if gi >= 2:
                        sp.wait_ge(E("ttr_done"), 4 * (gi - 1))
                    o = (g * 8 + 2 * p) * P * LINE
                    if g < 2:
                        sp.dma_start(bias_t[:, b, :, :], bass.AP(lines_d.tensor, o + 127, [[LINE - 1, P], [P * LINE, 2], [1, 256]])).then_inc(bias_in[b], 16)
                    else:
                        for rr in range(2):
                            for cc in range(2):
                                start, step = (o + 255, LINE - 1) if rr == cc else (o + 320, 0)
                                sp.dma_start(bias_t[64 * rr:64 * rr + 64, b, :, P + 64 * cc:P + 64 * cc + 64],
                                             bass.AP(lines_d.tensor, start, [[step, 64], [P * LINE, 2], [1, 64]])).then_inc(bias_in[b], 16)

        bias_need, cnt = [], [0, 0]
        for gi in range(12):
            cnt[gi % 2] += 64 if gi % 3 == 2 else 16
            bias_need.append(cnt[gi % 2])

        @block.gpsimd
        def _(pool):
            Q = Own(pool, E("pool_chain"))
            for u in range(U_END):
                nk, s = units[u][2], u % 2
                pool.wait_ge(w_raw[s], 16 * (u // 2 + 1))
                if U_KV <= u < U_BO:
                    g = gain["kv_norm_g_2" if u < U_QZ else "b_pre_g_2"]
                    pool.wait_ge(E("prm_in"), 32)
                    Q(pool.tensor_tensor(raw[:, s], raw[:, s], g.unsqueeze(2).to_broadcast([P, KT, P]), ALU.mult))
                if u >= 2:
                    pool.wait_ge(w_used, u - 1)
                Q(pool.tensor_copy(whi[:, s, 0:nk, :], raw[:, s, 0:nk, :]))
                Q(pool.tensor_tensor(wlo[:, s, 0:nk, :], raw[:, s, 0:nk, :], whi[:, s, 0:nk, :].bitcast(F32), ALU.subtract), E("w_split"))
                if u == U_BO + 1:
                    for k in range(QP):
                        pool.wait_ge(E("high_part"), PART["ys"] + k + 1)
                        Q(pool.tensor_tensor(yslo[:, k, :], ys[:, k, :], yshi[:, k, :].bitcast(F32), ALU.subtract), E("low_by_pool"))
                if u == U_KV + 1:
                    for k in range(KT):
                        pool.wait_ge(E("high_part"), PART["xn"] + k + 1)
                        Q(pool.tensor_tensor(xnlo[:, k, :], y2[:, k, :], xnhi[:, k, :].bitcast(F32), ALU.subtract), E("low_by_pool"))
                for m, k in sq_add.get(u, ()):
                    pool.wait_ge(E("sq"), 2 * KT * m + k + 1)
                    Q(pool.tensor_tensor(sq_buf[0][:], sq_buf[0][:], sq_buf[1][:], ALU.add), E("sq_added"))
                for p in range(PAIRS - 1):
                    i = u - 2 - (U_SIDE[p + 1] - 4)
                    if 0 <= i < 3:
                        for h in range(2):
                            pool.wait_ge(g_evac[h], outs_before[u - 2] + 1)
                        Q(pool.tensor_tensor(raw_of[i][:, 1:T], raw_of[i][:, 1:T], oF[:, 5 + p, 0:T - 1], ALU.add), E("mixed_next"))
            pool.wait_ge(E("x3_in"), 16)
            for h in range(2):
                cs = slice(HALF * h, HALF * h + HALF)
                for n in range(4):
                    pool.wait_ge(E("y3_normed"), 4 * h + n + 1)
                    Q(pool.tensor_tensor(y3[:, 2 * n + 1, cs], y3[:, 2 * n + 1, cs], x3[:, 2 * n + 1, cs], ALU.add), E("x4_pool"))

        @block.tensor
        def _(pe):
            def gemm_step(u, h, k, hi, lo, start=True, stop_=True):
                nk, s = units[u][2], u % 2
                if k == 0:
                    if h == 0:
                        pe.wait_ge(E("w_split"), u + 1)
                    if start and outs_before[u]:
                        pe.wait_ge(g_evac[h], outs_before[u])
                first, last = start and k == 0, stop_ and k == nk - 1
                pe.matmul(G[h][:], whi[:, s, k, :], hi(k, h), start=first, stop=False)
                pe.matmul(G[h][:], whi[:, s, k, :], lo(k, h), start=False, stop=False)
                m = pe.matmul(G[h][:], wlo[:, s, k, :], hi(k, h), start=False, stop=last)
                if k == nk - 1:
                    m.then_inc(g_full[h], 1)

            def gemm_half(u, h, hi, lo, ready=None, start=True, stop_=True):
                for k in range(units[u][2]):
                    if ready:
                        ready(k, h)
                    gemm_step(u, h, k, hi, lo, start, stop_)

            def moving(hi, lo):
                return (lambda k, h: hi[:, k, HALF * h:HALF * h + HALF]), (lambda k, h: lo[:, k, HALF * h:HALF * h + HALF])

            H1 = moving(h1hi, h1lo)

            pe.wait_ge(E("hot_in"), 32)
            pe.wait_ge(E("hot_one"), 1)
            for g in range(GROUPS):
                pe.matmul(line_bank[g][0:8, 0:LINE], rb33[:, 8 * g:8 * g + 8], hot_sb[:, g, :], start=True, stop=True).then_inc(E("line_full"), 1)
            pe.wait_ge(E("c_in"), 16)

            def h_tiles(hf):
                pe.wait_ge(E("x_scaled"), 4 * hf + 4)
                for f in range(8 * hf, 8 * hf + 8):
                    if f - 3 > 0:
                        pe.wait_ge(E("h1_lo"), f - 3)
                    for i in range(4):
                        m = pe.transpose(setup_bank[f % 4][:, i * P:(i + 1) * P], xt[:, 4 * hf + i, f % 8 * P:(f % 8 + 1) * P], ident)
                    m.then_inc(E("x_tr"), 1)


            def v_rows(gi):
                u = 10 * (gi // 3) + 3 * (gi % 3) + 2
                for h in range(2):
                    pe.wait_ge(g_evac[h], outs_before[u] + 1)
                if 4 * gi > 0:
                    pe.wait_ge(E("pt_done"), 4 * gi)
                for t in range(2):
                    for i in range(4):
                        m = pe.transpose(PT2[:, (4 * t + i) * P:(4 * t + i + 1) * P], vT[:, (4 * t + i) * P:(4 * t + i + 1) * P], ident)
                    m.then_inc(E("v_tr"), 1)

            def scores(c):
                p, g, t = quads[c]
                gi = 3 * p + g
                for h in range(2):
                    pe.wait_ge(g_evac[h], outs_before[10 * p + 3 * g + 1] + 1)
                if c > 0:
                    pe.wait_ge(E("ttr_done"), c)
                for i, hh, ti in pairwise:
                    n = 2 * t + ti
                    rows = slice(64 * hh, 64 * hh + 64)
                    b0 = key_blocks(g, n)[0]
                    m = pe.matmul(S2[:, i * 256 + b0 * P:i * 256 + 256], qT[rows, gi % 2, n * P:n * P + P],
                                  kT[rows, gi % 2, (n - 1 + b0) * P:(n + 1) * P], start=True, stop=True)
                m.then_inc(E("s_full"), 1)

            def transposes(c):
                p, g, t = quads[c]
                pe.wait_ge(E("exp_done"), c + 1)
                if c > 0:
                    pe.wait_ge(E("pt_done"), c)
                pe.wait_ge(E("v_rows"), 2 * (3 * p + g) + 2)
                for i, hh, ti in quad:
                    for b in key_blocks(g, 2 * t + ti):
                        m = pe.transpose(PT2[:, i * 256 + b * P:i * 256 + b * P + P], prob[:, i, b * P:b * P + P], ident)
                m.then_inc(E("pt_full"), 1)

            def weighted(c):
                p, g, t = quads[c]
                pe.wait_ge(E("pt_done"), c + 1)
                if c > 0:
                    pe.wait_ge(E("pv_free"), c)
                for ti in range(2):
                    n = 2 * t + ti
                    bs = key_blocks(g, n)
                    for b in bs:
                        for hh in range(2):
                            rows = slice(64 * hh, 64 * hh + 64)
                            i = 2 * hh + ti
                            pe.matmul(PV[rows, ti * P:ti * P + P], vrows[:, (3 * p + g) % 2, n - 1 + b, rows], ptsb[:, i, b * P:b * P + P],
                                      start=b == bs[0], stop=b == 1)
                for x, rows in enumerate((PV[:, 256:512], MB[:, 0:256])):
                    for ti in range(2):
                        m = pe.transpose(rows[:, ti * P:ti * P + P], wide[:, c % 2, x, ti, :, :].rearrange("p h c -> p (h c)"), ident)
                m.then_inc(E("pv_full"), 1)

            for s in range(A_END):
                if s in v_slot:
                    v_rows(v_slot[s])
                if s - 1 in slot_of:
                    transposes(slot_of[s - 1])
                if s - 2 in slot_of:
                    weighted(slot_of[s - 2])
                if s in slot_of:
                    scores(slot_of[s])
                if s < A_SLOTS:
                    if s < 2:
                        h_tiles(s)
                    gemm_half(s // 2, s % 2, *H1, ready=(lambda k, h: pe.wait_ge(E("h1_lo"), 8 * h + k + 1)) if s < 2 else None)
                else:
                    gemm_half(U_R + (s - A_SLOTS) // 2, s % 2, *H1)
            rows2 = (slice(0, 64), slice(64, 128))
            halves = (slice(0, HALF), slice(HALF, T))

            def side(p, place):
                for i in range(*SIDE[p][place]):
                    gemm_step(U_SIDE[p] + i // 16, i // 8 % 2, i % 8, *H1)

            def spread(dst, col, done):
                for n in range(8):
                    for hh, r in enumerate(rows2):
                        m = pe.matmul(dst[r, n * P:n * P + P], stat[:, col + 2 * n + hh:col + 2 * n + hh + 1].to_broadcast([P, C]), ident, start=True, stop=True)
                m.then_inc(E(done), 1)

            def head_sums(src, done):
                for n in range(8):
                    m = pe.matmul(PV[:, 2 * n:2 * n + 2], src[:, n * P:n * P + P], blocks[:, 0:P:C], start=True, stop=True)
                m.then_inc(E(done), 1)

            for i in range(A_END - A_SLOTS, 8):
                gemm_half(U_R + i // 2, i % 2, *H1)
            for p in range(PAIRS):
                pe.wait_ge(E("lora_tanh"), 1)
                pe.wait_ge(E("up_in"), 32)
                if p > 0:
                    pe.wait_ge(E("y_centred"), p)
                if p > 0:
                    pe.wait_ge(E("y_sq"), p)
                if p > 0:
                    pe.wait_ge(E("y_normed"), p)
                for h in range(2):
                    ma = pe.matmul(PT2[:, halves[h]], upw[64:128, p * P:p * P + P], lora[64:128, halves[h]], start=True, stop=True)
                    mw = pe.matmul(S2[:, halves[h]], upw[0:64, p * P:p * P + P], lora[0:64, halves[h]], start=True, stop=True)
                ma.then_inc(E("a_full"), 1)
                mw.then_inc(E("lw_full"), 1)
                side(p, "in")
                pe.wait_ge(E("k_sq"), p + 1)
                head_sums(ksq, "knorm_full")
                side(p, "norm")
                pe.wait_ge(E("lw_tanh"), p + 1)
                pe.wait_ge(E("kinv"), p + 1)
                spread(S2, 112, "kinv_full")
                pe.wait_ge(E("rkr"), p + 1)
                pe.wait_ge(E("a_tanh"), p + 1)
                for h in range(2):
                    m = pe.matmul(PT2[:, halves[h]], blocks, rkr[:, halves[h]], start=True, stop=True)
                m.then_inc(E("bonus_full"), 1)
                side(p, "bonus")
                pe.wait_ge(E("ak_ready"), p + 1)
                pe.wait_ge(E("bonus_done"), p + 1)
                def products(cq):
                    for i in range(8):
                        for hh, r in enumerate(rows2):
                            c = 8 * cq + i
                            m = pe.matmul((S2, PT2)[hh][:, i * P:i * P + P], BK[r, c, :, :], AM[r, hh, c, 0:3:2, :], start=True, stop=True)
                    m.then_inc(E("amat_full"), 1)

                products(0)
                side(p, "amat0")
                for f in range(4):
                    if 4 * p + f - 1 > 0:
                        pe.wait_ge(E("bk_rows"), 4 * p + f - 1)
                    for i in range(4):
                        m = pe.transpose((PV, MB)[f % 2][:, i * P:i * P + P], BK[:, 4 * f + i, :, :], ident)
                    m.then_inc(E("bk_tr"), 1)
                    if f == 1:
                        side(p, "amat1")
                side(p, "amat2")
                pe.wait_ge(E("amat_done"), 2 * p + 1)
                products(1)
                side(p, "amat3")
                for f in range(5):
                    pe.wait_ge(E("bk_rows"), 4 * p + 3 + f % 2)
                    if 4 * p + f - 1 > 0:
                        pe.wait_ge(E("vr_even"), 4 * p + f - 1)
                    if 5 * p + f - 1 > 0:
                        pe.wait_ge(E("vr_odd"), 5 * p + f - 1)
                    for w in range(4 * f, min(4 * f + 4, 17)):
                        m = pe.transpose((PV, MB)[f % 2][:, (w % 4) * P:(w % 4) * P + P], vpad[:, C * w:C * w + P], ident)
                    m.then_inc(E("vr_tr"), 1)
                    side(p, f"rows{f}")
                pe.wait_ge(E("a_level"), 6 * p + 1)
                pe.wait_ge(E("amat_done"), 2 * p + 2)
                for hf in range(2):
                    for c in chunk_half[hf]:
                        for r in rows2:
                            m = pe.matmul(PT2[r, c * C:c * C + C], AmT[r, 0, c, :], ident2[r, :], start=True, stop=True)
                    m.then_inc(E("inv_first"), 1)
                    side(p, f"inv{hf}")
                for lv in range(1, 6):
                    pe.wait_ge(E("a_level"), 6 * p + lv + 1)
                    for hf in range(2):
                        pe.wait_ge(E("inv_sb"), 12 * p + 2 * lv - 1 + hf)
                        for c in chunk_half[hf]:
                            for r in rows2:
                                m = pe.matmul(S2[r, c * C:c * C + C], AmT[r, lv % 2, c, :], Tm[r, c, :], start=True, stop=True)
                        m.then_inc(E("invx_full"), 1)
                        side(p, f"inv{4 * lv - 2 + hf}")
                    for hf in range(2):
                        pe.wait_ge(E("invx_sb"), 10 * p + 2 * lv - 1 + hf)
                        if lv < 5:
                            for c in chunk_half[hf]:
                                for r in rows2:
                                    pe.matmul(PT2[r, c * C:c * C + C], TT[r, c, :], Xs[r, c, :], start=True, stop=True)
                        for c in chunk_half[hf]:
                            for r in rows2:
                                m = pe.matmul(S2[r, c * C:c * C + C], Xs[r, c, :], TT[r, c, :], start=True, stop=True)
                        m.then_inc(E("inv_full"), 1)
                        side(p, f"inv{4 * lv + hf}")
                pe.wait_ge(E("vr_even"), 4 * p + 4)
                pe.wait_ge(E("vr_odd"), 5 * p + 5)
                pe.wait_ge(E("inv_sb"), 12 * p + 12)
                for c in range(NCH):
                    n = NCH * p + c
                    pe.wait_ge(E("state"), n + 1)
                    for hh, r in enumerate(rows2):
                        m = pe.matmul(PV[r, 0:C], AM[:, hh, c, 0, :], SV[:, hh, 0, c, :], start=True, stop=True)
                    m.then_inc(E("sx_full"), 1)
                    side(p, f"scan{3 * c}")
                    pe.wait_ge(E("sx_sb"), n + 1)
                    for hh, r in enumerate(rows2):
                        m = pe.matmul(MB[r, 0:C], TT[r, c, :], xs[r, :], start=True, stop=True)
                    m.then_inc(E("su_full"), 1)
                    side(p, f"scan{3 * c + 1}")
                    pe.wait_ge(E("su_even"), n + 1)
                    pe.wait_ge(E("su_odd"), n + 1)
                    if c < NCH - 1:
                        for hh, r in enumerate(rows2):
                            m = pe.matmul(PT2[r, 0:C], BKt[:, c, C * hh:C * hh + C], SV[:, hh, 1, c, :], start=True, stop=True)
                        m.then_inc(E("ss_full"), 1)
                    for hh, r in enumerate(rows2):
                        o = S2[r, c * C:c * C + C]
                        pe.matmul(o, SV[:, hh, 0, c, :], AM[:, hh, c, 2, :], start=True, stop=False)
                        m = pe.matmul(o, SV[:, hh, 1, c, :], AM[:, hh, c, 1, :], start=False, stop=True)
                    if c == NCH - 1:
                        m.then_inc(E("y_full"), 1)
                    side(p, f"scan{3 * c + 2}")
                if p < PAIRS - 1:
                    side(p + 1, "pre0")
                pe.wait_ge(E("y_sb"), p + 1)
                for h in range(2):
                    m = pe.matmul(PT2[:, halves[h]], centre, yT[:, halves[h]], start=True, stop=True)
                m.then_inc(E("centred_full"), 1)
                if p < PAIRS - 1:
                    side(p + 1, "pre1")
                pe.wait_ge(E("y_sq"), p + 1)
                head_sums(ysq, "var_full")
                if p < PAIRS - 1:
                    side(p + 1, "pre2")
                pe.wait_ge(E("y_rstd"), p + 1)
                spread(S2, 128, "y_rstd_full")
                if p < PAIRS - 1:
                    side(p + 1, "pre3")

            OA, OR = moving(ohi[:, 0:4, :], olo[:, 0:4, :]), moving(ohi[:, 4:8, :], olo[:, 4:8, :])
            for j in range(KT):
                for i, src in enumerate((OA, OR)):
                    for h in range(2):
                        gemm_half(U_M + 2 * j + i, h, *src, ready=(lambda k, h: pe.wait_ge(E("low_part"), PART["o"] + 4 * i + k + 1)) if j + h == 0 else None)

            sums = [0, 0]

            def sum_tile(buf, start, stop_):
                for i in range(8):
                    m = pe.matmul(PV[:, i:i + 1], buf[:, i * P:i * P + P], ones[:, 0:1], start=start and i == 0, stop=stop_ and i == 7)
                return m

            def sum_squares(k):
                pe.wait_ge(E("sq"), KT * sums[1] + k + 1)
                sum_tile(sq_buf[k % 2], k == 0, k == KT - 1).then_inc(E("sq_used"), 1)

            def sum_product():
                pe.wait_ge(E("sq_added"), ADDS * (sums[1] // 2 + 1))
                sum_tile(sq_buf[0], True, False)
                pe.wait_ge(E("sq"), KT * (sums[1] + 1))
                sum_tile(sq_buf[1], False, True).then_inc(E("sq_used"), 1)

            def spread_rstd():
                sums[1] += 1
                pe.wait_ge(E("rstd"), sums[1])
                for i in range(8):
                    m = pe.transpose(S2[:, i * P:i * P + P], stat[:, 344 + i:345 + i].to_broadcast([P, P]), ident)
                m.then_inc(E("rstd_full"), 1)

            MG = moving(mhi, mlo[:, :, 0, :])
            for j in range(KT):
                for h in range(2):
                    gemm_half(U_O + j, h, *MG, ready=(lambda k, h: pe.wait_ge(E("low_part"), PART["m"] + k + 1)) if j == 0 and h == 0 else None)
            sum_product()
            spread_rstd()
            for n in range(2):
                pe.wait_ge(E(f"x_in{n}"), 128)
            pe.wait_ge(E("nrs"), 1)
            H2 = moving(h2hi, h2lo)
            for k in range(KT + 2):
                if k < KT:
                    if k - 1 > 0:
                        pe.wait_ge(E("x2"), k - 1)
                    bank = (PT2, S2)[k % 2]
                    for i in range(8):
                        m = pe.transpose(bank[:, i * P:i * P + P], xt2[:, i, k * P:k * P + P], ident)
                    m.then_inc(E("xb_tr"), 1)
                if k >= 2:
                    sum_squares(k - 2)
                    pe.wait_ge(E("low_part"), PART["h2"] + k - 1)
                    for h in range(2):
                        gemm_step(U_V, h, k - 2, *H2)
            spread_rstd()

            def v_rows_of(i):
                pe.wait_ge(E("scaled_used"), 2 * i + 2)
                if 2 * i > 0:
                    pe.wait_ge(E("vln_rows"), 2 * i)
                for t in range(2):
                    for n in range(4):
                        m = pe.transpose(PT2[:, (4 * t + n) * P:(4 * t + n + 1) * P], vg[:, (4 * t + n) * P:(4 * t + n + 1) * P], ident)
                    m.then_inc(E("vg_tr"), 1)

            for i in range(16):
                if i:
                    gemm_half(U_V + i, 0, *H2)
                    v_rows_of(i - 1)
                    gemm_half(U_V + i, 1, *H2)
                if i == 1:
                    pe.wait_ge(E("ws_in"), 32)
                    for g in range(8):
                        m = pe.transpose(S2[:, g * P:g * P + P], wsr[:, g, :], ident)
                    m.then_inc(E("ws_tr"), 1)
                    pe.wait_ge(E("ws_t"), 1)
                    for h in range(2):
                        m = pe.matmul(S2[:, halves[h]], ones, wsT[:, 4 * h:4 * h + 4, :], start=True, stop=True)
                    m.then_inc(E("rowsum_full"), 1)
            gemm_half(U_UZ, 0, *H2)
            v_rows_of(15)
            pe.wait_ge(E("rowsum"), 1)
            for i in range(16):
                for h in range(2):
                    if i or h:
                        gemm_half(U_UZ + 2 * i, h, *H2)
                for h in range(2):
                    gemm_half(U_UZ + 2 * i + 1, h, *H2)
                pe.wait_ge(E("v_normed"), 4)
                pe.wait_ge(E("v_normed_act"), 4)
                if i > 0:
                    pe.wait_ge(E("s_sb"), i)
                for n in range(8):
                    m = pe.matmul(S2[:, n * P:n * P + P], vln[:, n, i * P:i * P + P], wsT[:, i // 2, :], start=True, stop=True)
                m.then_inc(E("sgu_full"), 1)

            def y_ready(k0):
                return lambda k, h: pe.wait_ge(E("low_part"), PART["y"] + k0 + k + 1)

            for j in range(KT):
                for kh in range(2):
                    u = U_AO + 2 * j + kh
                    src = (lambda k, h, kh=kh: yhi[:, 8 * kh + k, HALF * h:HALF * h + HALF],
                           lambda k, h, kh=kh: ylo[:, 4 * h:4 * h + 4, (8 * kh + k) * P:(8 * kh + k + 1) * P])
                    for h in range(2):
                        gemm_half(u, h, *src, ready=y_ready(8 * kh) if j == 0 else None, start=kh == 0, stop_=kh == 1)
            sum_product()
            spread_rstd()
            XN = moving(xnhi, xnlo)
            for k in range(KT):
                sum_squares(k)
                pe.wait_ge(E("low_by_pool"), k + 1)
                for h in range(2):
                    gemm_step(U_KV, h, k, *XN)
            spread_rstd()

            for j in range(4):
                if j:
                    for h in range(2):
                        gemm_half(U_KV + j, h, *XN)
                if j >= 2:
                    for h in range(2):
                        pe.wait_ge(g_evac[h], outs_before[U_KV + j] + 1)
                    if j - 2 > 0:
                        pe.wait_ge(E("v2_rows"), j - 2)
                    for n in range(8):
                        m = pe.transpose(PT2[:, n * P:n * P + P], v2T[:, n * P:n * P + P], ident)
                    m.then_inc(E("v2_tr"), 1)

            def key_blocks2(n):
                return (1,) if n == 0 else (0, 1)

            def scores2(c):
                i, t = c // 4, c % 4
                for h in range(2):
                    pe.wait_ge(g_evac[h], outs_before[U_QZ + 2 * i] + 1)
                pe.wait_ge(E("ttr_done"), len(quads) + c)
                for x, hh, ti in pairwise:
                    n = 2 * t + ti
                    b0 = key_blocks2(n)[0]
                    r = rows2[hh]
                    m = pe.matmul(S2[:, x * 256 + b0 * P:x * 256 + 256], q2[r, i % 2, n * P:n * P + P], kd[r, i // 2, (n - 1 + b0) * P:(n + 1) * P],
                                  start=True, stop=True)
                m.then_inc(E("s_full"), 1)

            def transposes2(c):
                t = c % 4
                pe.wait_ge(E("pn_done"), c + 1)
                pe.wait_ge(E("pt_done"), len(quads) + c)
                for x, hh, ti in quad:
                    for b in key_blocks2(2 * t + ti):
                        m = pe.transpose(PT2[:, x * 256 + b * P:x * 256 + b * P + P], pr2[:, c % 2, x, b * P:b * P + P], ident)
                m.then_inc(E("pt_full"), 1)

            def weighted2(c):
                i, t = c // 4, c % 4
                pe.wait_ge(E("pt_done"), len(quads) + c + 1)
                pe.wait_ge(E("pv_free"), len(quads) + c)
                for ti in range(2):
                    n = 2 * t + ti
                    bs = key_blocks2(n)
                    for b in bs:
                        for hh in range(2):
                            m = pe.matmul(PV[rows2[hh], ti * P:ti * P + P], vt2[:, n - 1 + b, 64 * (i // 2):64 * (i // 2) + 64], pts2[:, 2 * hh + ti, b * P:b * P + P],
                                          start=b == bs[0], stop=b == 1)
                m.then_inc(E("pv_full"), 1)

            pe.wait_ge(E("v2_rows"), 2)
            pe.wait_ge(E("scaled_used"), 100)
            for s in range(4 * QP + 6):
                c = s - 3
                if 0 <= c - 2 < 4 * QP:
                    transposes2(c - 2)
                if 0 <= c - 3 < 4 * QP:
                    weighted2(c - 3)
                if 0 <= c < 4 * QP:
                    scores2(c)
                if s < 4 * QP:
                    gemm_half(U_QZ + s // 2, s % 2, *XN)
            YS = moving(yshi, yslo)
            for j in range(KT):
                for h in range(2):
                    gemm_half(U_BO + j, h, *YS, ready=(lambda k, h: pe.wait_ge(E("low_by_pool"), KT + k + 1)) if j == 0 else None)
            sum_product()
            spread_rstd()
            for n in range(8):
                pe.wait_ge(E("x4"), 4 * (n // 4) + 4)
                pe.wait_ge(E("x4_pool"), 4 * (n // 4) + 4)
                if n - 1 > 0:
                    pe.wait_ge(E("rows_out"), n - 1)
                bank = (PT2, S2)[n % 2]
                for k in range(KT):
                    m = pe.transpose(bank[:, k * P:k * P + P], y3[:, k, n * P:n * P + P], ident)
                m.then_inc(E("out_tr"), 1)

        @block.vector
        def _(dve):
            V = Own(dve, E("dve_chain"))
            v = nc.vector
            V(v.memset(rb33[32:33, :], 1.0), E("hot_one"))

            def mean_squares(hf):
                for i in (4 * hf + 2, 4 * hf + 3):
                    dve.wait_ge(E(f"x_in{hf}"), 64)
                    V(v.tensor_tensor_reduce(out=sq1[:], in0=xt[:, i, :], in1=xt[:, i, :], scale=1.0, scalar=0.0, op0=ALU.mult, op1=ALU.add,
                                             accum_out=stat[:, i:i + 1]))
                dve.wait_ge(E("squares"), 2 * hf + 2)
                V(v.tensor_scalar(stat[:, 8 + 4 * hf:12 + 4 * hf], stat[:, 4 * hf:4 * hf + 4], 1.0 / D, EPS, ALU.mult, ALU.add), E("mean_sq0"))

            def scale_rows(hf):
                cols = stat[:, 8 + 4 * hf:12 + 4 * hf]
                dve.wait_ge(E("sqrt0"), hf + 1)
                V(v.reciprocal(cols, cols))
                for i in range(4):
                    V(v.tensor_scalar(xt[:, 4 * hf + i, :], xt[:, 4 * hf + i, :], cols[:, i:i + 1], None, ALU.mult), E("x_scaled"))

            def h_low(hf):
                dst = slice(HALF * hf, HALF * hf + HALF)
                for k in range(8):
                    dve.wait_ge(E("h1_hi"), 8 * hf + k + 1)
                    dve.wait_ge(E("prm_in"), 32)
                    V(v.scalar_tensor_tensor(h1lo[:, k, dst], setup_bank[k % 4], gain["pre_norm_gain"][:, k:k + 1],
                                             h1hi[:, k, dst].bitcast(F32), ALU.mult, ALU.subtract), E("h1_lo"))

            mean_squares(0)
            scale_rows(0)
            mean_squares(1)
            h_low(0)
            scale_rows(1)
            h_low(1)

            def v_rows(gi):
                if gi >= 2:
                    dve.wait_ge(E("pv_full"), 4 * (gi - 1))
                for t in range(2):
                    dve.wait_ge(E("v_tr"), 2 * gi + t + 1)
                    V(v.tensor_copy(vrows[:, gi % 2, 4 * t:4 * t + 4, :], PT2[:, HALF * t:HALF * t + HALF].rearrange("p (n c) -> p n c", n=4)), E("v_rows"))

            def biased(c):
                p, g, t = quads[c]
                gi = 3 * p + g
                dve.wait_ge(E("s_full"), c + 1)
                dve.wait_ge(bias_in[gi % 2], bias_need[gi])
                if c > 0:
                    dve.wait_ge(E("exp_done"), c)
                if c - 3 > 0:
                    dve.wait_ge(E("pv_full"), c - 3)
                for i, hh, ti in quad:
                    lo = key_blocks(g, 2 * t + ti)[0] * P
                    col = c % 4 * 4 + i
                    V(v.tensor_tensor_reduce(out=negl[:, i, lo:256], in0=S2[:, i * 256 + lo:i * 256 + 256], in1=bias_t[:, gi % 2, hh, lo:256],
                                             scale=-1.0, scalar=3e38, op0=ALU.add, op1=ALU.min, accum_out=negm[:, col:col + 1]),
                      E("ttr_done") if i == 3 else None)

            def merge(c):
                p, g, t = quads[c]
                dve.wait_ge(E("pv_full"), c + 1)
                sums, nm = natural(accu[:], g, t), natural(nmax[:], g, t)
                new, newm = permuted(PV[:].rearrange("p (x n) -> p x n", x=2), g), permuted(MB[:, 0:256].unsqueeze(1), g)
                if g == 0:
                    V(v.tensor_copy(sums, new))
                    V(v.tensor_copy(nm, newm), E("pv_free"))
                    return
                k = sum(1 for q in quads[:c] if q[1]) + 1
                nn, ea, eb, scaled = (permuted(x, g) for x in (nnew[:], eab[:, 0:1, :], eab[:, 1:2, :], rescaled[:]))
                V(v.tensor_tensor(nn, nm, newm, ALU.min))
                V(v.tensor_tensor(ea, nn, nm, ALU.subtract))
                V(v.tensor_tensor(eb, nn, newm, ALU.subtract), E("ab_ready"))
                if g == 1:
                    V(v.tensor_copy(nm, nn))
                dve.wait_ge(E("eab_done"), k)
                for x in range(2):
                    one = slice(x, x + 1)
                    V(v.tensor_tensor(scaled[:, one], new[:, one], eb, ALU.mult), E("pv_free") if x else None)
                for x in range(2):
                    one = slice(x, x + 1)
                    V(v.tensor_tensor(sums[:, one], sums[:, one], ea, ALU.mult))
                V(v.tensor_tensor(sums, sums, scaled, ALU.add))
                if g == GROUPS - 1:
                    rden = natural(rd[:], g, t)
                    V(v.reciprocal(rden, sums[:, 1:2]))
                    if t == 0:
                        if 16 * p > 0:
                            dve.wait_ge(E("oa_out"), 16 * p)
                    V(v.tensor_tensor(natural(og[:].unsqueeze(1), g, t), sums[:, 0:1], rden, ALU.mult))

            for s in range(A_END):
                if s in v_slot:
                    v_rows(v_slot[s])
                if s in slot_of:
                    biased(slot_of[s])
                if s - 2 in slot_of:
                    c = slot_of[s - 2]
                    merge(c)
                    if c % 12 == 11:
                        V(v.scalar_tensor_tensor(og[:], og[:], 0.5, zs[:], ALU.mult, ALU.mult), E("fin_done"))
                if s < A_SLOTS:
                    u, h = s // 2, s % 2
                    p, r = u // 10, u % 10
                    if r % 3 == 2 and r < 9:
                        gi = 3 * p + r // 3
                        wait_full(dve, u, h)
                        if 2 * gi > 0:
                            dve.wait_ge(E("v_tr"), 2 * gi)
                        V(v.tensor_copy(perm_half(vT[:], r // 3, h), nat_half(G[h][:], r // 3)), emptied(u, h))
                    elif r == 9:
                        z = zs[:, HALF * h:HALF * h + HALF]
                        dve.wait_ge(E("z_tanh"), 2 * p + h + 1)
                        V(v.scalar_tensor_tensor(z, z, 1.0, G[h][:], ALU.add, ALU.mult), emptied(u, h))
            lo_, hi_ = slice(0, 64), slice(64, 128)
            rows2 = (lo_, hi_)
            krows = (hi_, lo_)
            V(v.memset(vpad[:, 0:C], 0.0))
            V(v.memset(vpad[:, C + T:], 0.0))
            for hh in range(2):
                V(v.memset(AM[krows[hh], hh, :, 1, :], 0.0))

            for i, dst in enumerate((lora[:], *raw_of)):
                for h in range(2):
                    dve.wait_ge(g_evac[h], outs_before[U_R + i] + 1)
                V(v.tensor_tensor(dst[:, 1:T], dst[:, 1:T], oF[:, 4 + i, 0:T - 1], ALU.add), E("mixed"))
            def low_of_o(k):
                dve.wait_ge(E("high_part"), PART["o"] + k + 1)
                V(v.tensor_tensor(olo[:, k, :], oF[:, k, :] if k >= 4 else oA[k][:], ohi[:, k, :].bitcast(F32), ALU.subtract), E("low_part"))

            for p in range(PAIRS):
                one = slice(p, p + 1)
                V(v.memset(reset[:], 1.0))
                V(v.memset(reset[:, 0:T:C], 0.0))
                dve.wait_ge(E("k_gain"), p + 1)
                V(v.tensor_tensor(kmod[:], kgain[:], rkT[:], ALU.mult))
                V(v.scalar_tensor_tensor(rkr[:], rT[:], chan["rwkv_r_k"][:, one], kmod[:], ALU.mult, ALU.mult), E("rkr"))
                dve.wait_ge(E("logw"), p + 1)
                V(v.tensor_tensor_scan(out=cum[:], data0=reset[:], data1=logw[:], initial=0.0, op0=ALU.mult, op1=ALU.add))
                V(v.tensor_tensor(logw[:], cum[:], logw[:], ALU.subtract), E("cum"))
                dve.wait_ge(E("knorm_full"), p + 1)
                V(v.tensor_scalar(stat[:, 112:128], PV[:, 0:16], 1e-24, None, ALU.max), E("knorm_sb"))
                dve.wait_ge(E("k_sqrt"), p + 1)
                V(v.reciprocal(stat[:, 112:128], stat[:, 112:128]), E("kinv"))
                dve.wait_ge(E("kinv_full"), p + 1)
                V(v.scalar_tensor_tensor(kk[:], rkT[:], chan["rwkv_k_k"][:, one], S2[:], ALU.mult, ALU.mult))
                dve.wait_ge(E("a_sig"), p + 1)
                V(v.tensor_tensor(kka[:], kk[:], aT[:], ALU.mult))
                dve.wait_ge(E("bonus_full"), p + 1)
                V(v.tensor_tensor(bon[:], PT2[:], vpad[:, C:C + T], ALU.mult), E("bonus_done"))
                dve.wait_ge(E("exps"), p + 1)
                V(v.tensor_copy(e_end, ec[:, C - 1:T:C]))

                def chunks(ap):
                    return ap.rearrange("p (c t) -> p c t", t=C)

                for hh, r in enumerate(rows2):
                    V(v.tensor_tensor(AM[r, hh, :, 2, :], chunks(rT[r, :]), chunks(ec[r, :]), ALU.mult))
                    V(v.scalar_tensor_tensor(AM[r, hh, :, 0, :], chunks(kk[r, :]), -1.0, chunks(logw[r, :]), ALU.mult, ALU.mult))
                    V(v.tensor_tensor(BK[r, :, hh, :], chunks(kka[r, :]), chunks(cum[r, :]), ALU.mult))
                    V(v.tensor_tensor(BK[r, :, 1 - hh, :], chunks(kmod[r, :]), chunks(cum[r, :]), ALU.mult), E("ak_ready") if hh else None)
                def masked(dst, src, m, signal=None):
                    V(v.tensor_tensor(dst, src, m.unsqueeze(1).to_broadcast([64, 8, C]), ALU.mult), signal)

                for cq in range(2):
                    cs = slice(8 * cq, 8 * cq + 8)
                    dve.wait_ge(E("amat_full"), 2 * p + cq + 1)
                    for hh in range(2):
                        bank = (S2, PT2)[hh][:].rearrange("p (c x t) -> p c x t", c=8, x=2)
                        b, k = rows2[hh], krows[hh]
                        masked(Aab[b, cs, :], bank[b, :, 0, :], mask_a[b, 0:C])
                        masked(AM[b, hh, cs, 1, :], bank[b, :, 1, :], mask_a[b, C:2 * C])
                        masked(AM[k, hh, cs, 0, :], bank[k, :, 0, :], mask_a[k, 0:C])
                        masked(AM[k, hh, cs, 2, :], bank[k, :, 1, :], mask_a[k, C:2 * C], E("amat_done") if hh else None)
                for f in range(4):
                    bank = (PV, MB)[f % 2][:].rearrange("p (w x c) -> p w x c", w=4, x=2)
                    dve.wait_ge(E("vr_tr"), 5 * p + f + 1)
                    for kind in range(2):
                        V(v.tensor_copy(SV[hi_, 0, kind, 4 * f:4 * f + 4, :], bank[hi_, :, 0, :]), E("vr_even") if kind else None)
                dve.wait_ge(E("bk_tr"), 4 * p + 4)

                def level_of(i):
                    V(v.tensor_tensor(AmT[:, i % 2], Aab[:], level[i].unsqueeze(1).to_broadcast([P, NCH, C]), ALU.mult), E("a_level"))

                eye = ident2.unsqueeze(1).to_broadcast([P, NCH, C])
                level_of(0)
                V(v.tensor_tensor(TT[:], AmT[:, 0], eye, ALU.add))
                level_of(1)
                ch = [slice(8 * hf, 8 * hf + 8) for hf in range(2)]
                bank = [slice(HALF * hf, HALF * hf + HALF) for hf in range(2)]

                def rows(ap, hf):
                    return ap[:, ch[hf]].rearrange("p c t -> p (c t)")

                for hf in range(2):
                    dve.wait_ge(E("inv_first"), 2 * p + hf + 1)
                    V(v.tensor_tensor(Tm[:, ch[hf]], PT2[:, bank[hf]].rearrange("p (c t) -> p c t", t=C), ident2.unsqueeze(1).to_broadcast([P, 8, C]), ALU.add), E("inv_sb"))
                for lv in range(1, 6):
                    for hf in range(2):
                        dve.wait_ge(E("invx_full"), 10 * p + 2 * lv - 1 + hf)
                        V(v.tensor_copy(rows(Xs, hf), S2[:, bank[hf]]), E("invx_sb"))
                    if lv < 5:
                        level_of(lv + 1)
                    for hf in range(2):
                        dve.wait_ge(E("inv_full"), 10 * p + 2 * lv - 1 + hf)
                        if lv < 5:
                            V(v.tensor_tensor(rows(Tm, hf), rows(Tm, hf), PT2[:, bank[hf]], ALU.add))
                        V(v.tensor_tensor(rows(TT, hf), rows(TT, hf), S2[:, bank[hf]], ALU.add), E("inv_sb"))
                V(v.memset(SV[lo_, 0, 0, 0, :], 0.0))
                V(v.memset(SV[hi_, 1, 0, 0, :], 0.0), E("state"))
                for c in range(NCH):
                    n = NCH * p + c
                    dve.wait_ge(E("sx_full"), n + 1)
                    V(v.tensor_copy(xs[:], PV[:, 0:C]), E("sx_sb"))
                    for hh, r in enumerate(rows2):
                        V(v.tensor_scalar(se[r, :], SV[r, hh, 0, c, :], e_end[r, c:c + 1], None, ALU.mult))
                    dve.wait_ge(E("su_full"), n + 1)
                    V(v.tensor_copy(SV[lo_, 0, 1, c, :], MB[lo_, 0:C]), E("su_even"))
                    if c < NCH - 1:
                        dve.wait_ge(E("ss_full"), 15 * p + c + 1)
                        for hh, r in enumerate(rows2):
                            V(v.scalar_tensor_tensor(SV[r, hh, 0, c + 1, :], PT2[r, 0:C], e_end[r, c:c + 1], se[r, :], ALU.mult, ALU.add),
                              E("state") if hh else None)
                z = oF[:, 4 + p, :]
                u = U_SIDE[p + 1] - 1
                for h in range(2):
                    dve.wait_ge(E("zr_tanh"), 2 * p + h + 1)
                    cs = slice(HALF * h, HALF * h + HALF)
                    V(v.scalar_tensor_tensor(z[:, cs], z[:, cs], 1.0, G[h][:], ALU.add, ALU.mult), emptied(u, h))
                if p == PAIRS - 1:
                    low_of_o(0)
                dve.wait_ge(E("centred_full"), p + 1)
                dve.wait_ge(E("y_sq"), p + 1)
                V(v.tensor_scalar(yc[:], PT2[:], half_ln_w[:, one], None, ALU.mult), E("y_centred"))
                dve.wait_ge(E("var_full"), p + 1)
                V(v.tensor_scalar(stat[:, 128:144], PV[:, 0:16], 1.0 / C, GN_EPS, ALU.mult, ALU.add), E("y_var"))
                V(v.tensor_tensor(yc[:], yc[:], z, ALU.mult))
                dve.wait_ge(E("y_sd"), p + 1)
                V(v.reciprocal(stat[:, 128:144], stat[:, 128:144]), E("y_rstd"))
                V(v.scalar_tensor_tensor(bon[:], bon[:], chan["rwkv_ln_b"][:, one], z, ALU.add, ALU.mult))
                if p == PAIRS - 1:
                    low_of_o(1)
                    low_of_o(2)
                dve.wait_ge(E("y_rstd_full"), p + 1)
                V(v.tensor_tensor(yc[:], yc[:], S2[:], ALU.mult), E("y_normed"))
                V(v.scalar_tensor_tensor(z, bon[:], 0.5, yc[:], ALU.mult, ALU.add), E("pair_done"))

            for k in range(3, 8):
                low_of_o(k)

            def merged_low(j):
                dve.wait_ge(E("high_part"), PART["m"] + j + 1)
                V(v.scalar_tensor_tensor(mlo[:, j, 0, :], gates[:, 2 * j + 1, :], 0.5, mhi[:, j, :].bitcast(F32), ALU.mult, ALU.subtract), E("low_part"))

            for j in range(KT):
                u = U_M + 2 * j
                dve.wait_ge(E(f"gates_in{j // 2}"), 16)
                for i in range(2):
                    for h in range(2):
                        cs = slice(HALF * h, HALF * h + HALF)
                        wait_full(dve, u + i, h)
                        V(v.scalar_tensor_tensor(gates[:, 2 * j + i, cs], gates[:, 2 * j + i, cs], 1.0, G[h][:], ALU.add, ALU.mult), emptied(u + i, h))
                V(v.tensor_tensor(gates[:, 2 * j + 1, :], gates[:, 2 * j, :], gates[:, 2 * j + 1, :], ALU.add), E("merged"))
                if j:
                    merged_low(j - 1)
            merged_low(KT - 1)

            norms = [0]

            def rstd():
                norms[0] += 1
                col = stat[:, 344:352]
                dve.wait_ge(E("sq_used"), SUMS_BEFORE[norms[0]])
                V(v.tensor_scalar(col, PV[:, 0:8], 1.0 / D, EPS, ALU.mult, ALU.add), E("norm_var"))
                dve.wait_ge(E("norm_sd"), norms[0])
                V(v.reciprocal(col, col), E("rstd"))
                dve.wait_ge(E("nrs"), norms[0])

            half_n = [0]

            def scaled(u, h, buf):
                n = half_n[0]
                half_n[0] += 1
                wait_full(dve, u, h)
                if n - 1 > 0:
                    dve.wait_ge(E("scaled_used"), n - 1)
                V(v.tensor_tensor(buf[:, h, :], G[h][:], nrs[:, HALF * h:HALF * h + HALF], ALU.mult), emptied(u, h))

            rstd()
            g_, g2 = gain["post_norm_gain"], gain["a_pre_g_2"]
            for k in range(KT + 1):
                if k < KT:
                    V(v.scalar_tensor_tensor(y1[:, k, :], y1[:, k, :], g_[:, k:k + 1], nrs[:], ALU.mult, ALU.mult))
                    dve.wait_ge(E("xb_tr"), k + 1)
                    V(v.tensor_tensor(y1[:, k, :], y1[:, k, :], (PT2, S2)[k % 2][:], ALU.add), E("x2"))
                if k:
                    dve.wait_ge(E("high_part"), PART["h2"] + k)
                    V(v.scalar_tensor_tensor(h2lo[:, k - 1, :], y1[:, k - 1, :], g2[:, k - 1:k], h2hi[:, k - 1, :].bitcast(F32), ALU.mult, ALU.subtract), E("low_part"))
            rstd()

            bn = stat[:, 128:320].rearrange("p (n s x) -> p n s x", n=8, s=4)
            mv = stat[:, 320:336].rearrange("p (n x) -> p n x", n=8)

            def gate_z(i):
                u = U_UZ + 2 * i + 1
                for h in range(2):
                    scaled(u, h, scaled_g)
                for h in range(2):
                    dve.wait_ge(E("scaled_used"), 32 + 4 * i + 3 + h)
                    z = zg[:, HALF * h:HALF * h + HALF]
                    V(v.scalar_tensor_tensor(z, z, 1.0, scaled_g[:, h, :], ALU.add, ALU.mult))

            def v_rows_in(i):
                for t in range(2):
                    dve.wait_ge(E("vg_tr"), 2 * i + t + 1)
                    V(v.tensor_copy(vln[:, 4 * t:4 * t + 4, i * P:i * P + P], PT2[:, HALF * t:HALF * t + HALF].rearrange("p (n c) -> p n c", n=4)),
                      E("vln_rows"))
                if i % 4 == 3:
                    for n in range(8):
                        V(v.bn_stats(bn[:, n, i // 4, :], vln[:, n, HALF * (i // 4):HALF * (i // 4) + HALF]))
                if i == 0:
                    dve.wait_ge(E("ws_tr"), 1)
                    V(v.tensor_tensor(wsT[:], S2[:].rearrange("p (g t) -> p g t", g=8), causal.unsqueeze(1).to_broadcast([P, 8, P]), ALU.mult), E("ws_t"))
                    dve.wait_ge(E("rowsum_full"), 1)
                    V(v.tensor_copy(rowsum[:], S2[:].rearrange("p (g t) -> p g t", g=8)), E("rowsum"))

            dve.wait_ge(E("x2_out"), 16 * KT)
            for i in range(17):
                scaled(U_V + i, 0, scaled_g)
                if i:
                    v_rows_in(i - 1)
                scaled(U_V + i, 1, scaled_g)
            for n in range(8):
                V(v.bn_aggr(mv[:, n, :], bn[:, n, :, :]))
            V(v.tensor_scalar(stat[:, 336:344], mv[:, :, 1], EPS, None, ALU.add), E("ln_var"))
            dve.wait_ge(E("ln_sd"), 1)
            V(v.reciprocal(stat[:, 336:344], stat[:, 336:344]))
            V(v.scalar_tensor_tensor(stat[:, 344:352], mv[:, :, 0], -1.0, stat[:, 336:344], ALU.mult, ALU.mult), E("ln_stats"))
            for n in range(4):
                V(v.tensor_scalar(vln[:, n, :], vln[:, n, :], mv[:, n, 0:1], stat[:, 336 + n:337 + n], ALU.subtract, ALU.mult), E("v_normed"))
            gate_z(0)
            dve.wait_ge(E("ws_in"), 32)
            for i in range(16):
                g = i // 2
                if i:
                    for h in range(2):
                        scaled(U_UZ + 2 * i, h, scaled_g)
                V(v.scalar_tensor_tensor(btile[:], rowsum[:, g, :], ln_b[:, i:i + 1], bsb[:, g, :], ALU.mult, ALU.add))
                if i:
                    gate_z(i)
                dve.wait_ge(E("sgu_full"), i + 1)
                V(v.scalar_tensor_tensor(sg[:].rearrange("p (n t) -> p n t", n=8), S2[:].rearrange("p (n t) -> p n t", n=8), ln_g[:, i:i + 1],
                                         btile[:].unsqueeze(1).to_broadcast([P, 8, P]), ALU.mult, ALU.add), E("s_sb"))
                dve.wait_ge(E("scaled_used"), 32 + 4 * i + 2)
                V(v.tensor_tensor(sg[:], sg[:], ug[:], ALU.mult), E("u_used"))
                V(v.scalar_tensor_tensor(vln[:, :, i * P:i * P + P], sg[:].rearrange("p (n t) -> p n t", n=8), 0.5,
                                         zg[:].rearrange("p (n t) -> p n t", n=8), ALU.mult, ALU.mult), E("y_mlp"))
            for i in range(16):
                dve.wait_ge(E("high_part"), PART["y"] + i + 1)
                V(v.tensor_tensor(ylo[:, :, i * P:i * P + P], vln[:, :, i * P:i * P + P], yhi[:, i, :].bitcast(F32).rearrange("p (n t) -> p n t", n=8),
                                  ALU.subtract), E("low_part"))
            rstd()
            dve.wait_ge(E("res_in"), 16)
            g_ = gain["a_post_g_2"]
            for k in range(KT):
                V(v.scalar_tensor_tensor(y2[:, k, :], y2[:, k, :], g_[:, k:k + 1], nrs[:], ALU.mult, ALU.mult))
                V(v.tensor_tensor(y2[:, k, :], y2[:, k, :], res[:, k, :], ALU.add), E("x3"))
            rstd()

            for j in range(2):
                for h in range(2):
                    scaled(U_KV + j, h, scaled_s)
            for j in range(2):
                u = U_KV + 2 + j
                for h in range(2):
                    cs = slice(HALF * h, HALF * h + HALF)
                    wait_full(dve, u, h)
                    if j > 0:
                        dve.wait_ge(E("v2_tr"), j)
                    V(v.tensor_tensor(v2T[:, cs], G[h][:], nrs[:, cs], ALU.mult), emptied(u, h))
                dve.wait_ge(E("v2_tr"), j + 1)
                V(v.tensor_copy(vt2[:, :, j * P:j * P + P], PT2[:].rearrange("p (n c) -> p n c", n=8)), E("v2_rows"))

            def biased2(c):
                i, t = c // 4, c % 4
                dve.wait_ge(E("s_full"), len(quads) + c + 1)
                dve.wait_ge(E("exp_done"), len(quads) + c)
                for x, hh, ti in quad:
                    lo = P if 2 * t + ti == 0 else 0
                    col = c % 2 * 4 + x
                    V(v.tensor_tensor_reduce(out=neg2[:, x, lo:256], in0=S2[:, x * 256 + lo:x * 256 + 256], in1=alibi[:, i % 2, hh, lo:256],
                                             scale=-1.0, scalar=3e38, op0=ALU.add, op1=ALU.min, accum_out=negm[:, col:col + 1]))
                for hh in range(2):
                    cols = slice(c % 2 * 4 + 2 * hh, c % 2 * 4 + 2 * hh + 2)
                    V(v.tensor_scalar(negm[:, cols], negm[:, cols], neg_sink[:, 2 * i + hh:2 * i + hh + 1], None, ALU.min), E("ttr_done") if hh else None)

            def normalised2(c):
                t = c % 4
                dve.wait_ge(E("exp_done"), len(quads) + c + 1)
                den, es = den2[:, c % 2, 0:4], den2[:, c % 2, 4:8]
                V(v.tensor_tensor(den, den, es, ALU.add))
                V(v.reciprocal(den, den))
                todo = runs((1, 0) if t == 0 else (0, 0))
                for j, (sl, b0) in enumerate(todo):
                    rden = den[:, sl].unsqueeze(2)
                    V(v.tensor_tensor(pr2[:, c % 2, sl, b0 * P:256], pr2[:, c % 2, sl, b0 * P:256], rden.to_broadcast([P, 4 // len(todo), 256 - b0 * P]), ALU.mult),
                      E("pn_done") if j == len(todo) - 1 else None)

            def gated2(c):
                i, t = c // 4, c % 4
                dve.wait_ge(E("pv_full"), len(quads) + c + 1)
                cs = slice(256 * t, 256 * t + 256)
                V(v.scalar_tensor_tensor(ys[:, i, cs], PV[:, 0:256], 0.5, zs2[:, i % 2, cs], ALU.mult, ALU.mult), E("pv_free"))

            for s in range(4 * QP + 6):
                c = s - 3
                if s % 4 == 0 and s // 4 < QP:
                    i = s // 4
                    for hh in range(2):
                        slope = 2.0 ** (-8.0 * (2 * i + hh + 1) / 16)
                        V(v.tensor_scalar(alibi[:, i % 2, hh, :], far, -slope, None, ALU.mult))
                if s % 4 in (3, 0) and 0 < s <= 4 * QP:
                    i, h = (s - 1) // 4, (s - 1) % 2
                    dve.wait_ge(E("scaled_used"), 100 + 2 * i + h + 1)
                    z = zs2[:, i % 2, HALF * h:HALF * h + HALF]
                    V(v.scalar_tensor_tensor(z, z, 1.0, scaled_s[:, h, :], ALU.add, ALU.mult))
                if 0 <= c - 1 < 4 * QP:
                    normalised2(c - 1)
                if 0 <= c < 4 * QP:
                    biased2(c)
                if 0 <= c - 3 < 4 * QP:
                    gated2(c - 3)
                if s < 4 * QP:
                    i, h = s // 4, s % 2
                    cs = slice(HALF * h, HALF * h + HALF)
                    u = U_QZ + s // 2
                    if s % 4 < 2:
                        wait_full(dve, u, h)
                        dve.wait_ge(E("s_full"), len(quads) + 4 * (i - 1))
                        V(v.scalar_tensor_tensor(q2[:, i % 2, cs], G[h][:], 0.125, nrs[:, cs], ALU.mult, ALU.mult), emptied(u, h))
                    else:
                        scaled(u, h, scaled_s)
            V(v.memset(stat[:, 382:383], 0.0), E("ys_done"))
            rstd()
            dve.wait_ge(E("x3_in"), 16)
            g_ = gain["b_post_g_2"]
            for h in range(2):
                cs = slice(HALF * h, HALF * h + HALF)
                for k in (1, 0, 3, 2, 5, 4, 7, 6):
                    V(v.scalar_tensor_tensor(y3[:, k, cs], y3[:, k, cs], g_[:, k:k + 1], nrs[:, cs], ALU.mult, ALU.mult), E("y3_normed") if k % 2 else None)
                    if k % 2 == 0:
                        V(v.tensor_tensor(y3[:, k, cs], y3[:, k, cs], x3[:, k, cs], ALU.add), E("x4"))

        @block.scalar
        def _(act):
            A = Own(act, E("act_chain"))
            a = nc.scalar
            act.dma_start(hot_sb[:], d["bucket_hot"]).then_inc(E("hot_in"), 16)
            act.dma_start(rb33[0:32, :], d["rel_bias"]).then_inc(E("hot_in"), 16)
            act.dma_start(prm[:, 0:129], d["channel_vectors"]).then_inc(E("prm_in"), 16)
            act.dma_start(sink, d["b_sinks_2"].to_broadcast([P, 16])).then_inc(E("prm_in"), 16)
            act.dma_start(cst[:], d["shape_consts"]).then_inc(E("c_in"), 16)
            for g in range(GROUPS):
                act.wait_ge(E("line_full"), g + 1)
                A(a.activation(lines[:, g, :], line_bank[g][0:8, 0:LINE], ACT.Copy))
                act.dma_start(lines_d[g], lines[:, g, :].unsqueeze(1).to_broadcast([8, P, LINE])).then_inc(E(f"lines_out{g}"), 16)
            act.wait_ge(E("prm_in"), 32)
            A(a.mul(half_w0, chan["rwkv_w0"], 0.5))
            A(a.mul(half_a0, chan["rwkv_a0"], 0.5))
            A(a.mul(neg_sink, sink, -1.0))
            A(a.mul(half_k_a, chan["rwkv_k_a"], 0.5))
            A(a.activation(less_k_a, half_k_a, ACT.Copy, bias=1.0, scale=-1.0))
            A(a.activation(less_mix, mix, ACT.Copy, bias=1.0, scale=-1.0))
            A(a.mul(half_ln_w, chan["rwkv_ln_w"], 0.5), E("prm_derived"))

            def load_table(func):
                A(a.activation(stat[:, 383:384], ones[:, 0:1], func))

            act.wait_ge(E("c_in"), 16)
            load_table(ACT.Sqrt)

            def row_squares(hf):
                for i in (4 * hf, 4 * hf + 1):
                    act.wait_ge(E(f"x_in{hf}"), 64)
                    A(a.activation(sq0[:], xt[:, i, :], ACT.Square, accum_out=stat[:, i:i + 1]), E("squares"))

            def row_roots(hf):
                cols = stat[:, 8 + 4 * hf:12 + 4 * hf]
                act.wait_ge(E("mean_sq0"), hf + 1)
                A(a.activation(cols, cols, ACT.Sqrt), E("sqrt0"))

            def h_high(hf):
                for k in range(8):
                    act.wait_ge(E("x_tr"), 8 * hf + k + 1)
                    A(a.activation(h1hi[:, k, HALF * hf:HALF * hf + HALF], setup_bank[k % 4], ACT.Copy, scale=gain["pre_norm_gain"][:, k:k + 1]), E("h1_hi"))
                    if hf == 0 and k == 0:
                        row_roots(1)

            row_squares(0)
            row_roots(0)
            row_squares(1)
            h_high(0)
            h_high(1)
            for g in range(GROUPS):
                act.wait_ge(E(f"lines_out{g}"), 16)

            def copy_back(c):
                p, g, t = quads[c]
                act.wait_ge(E("pt_full"), c + 1)
                if c > 0:
                    act.wait_ge(E("pv_full"), c)
                todo = runs([key_blocks(g, 2 * t + ti)[0] for ti in range(2)])
                src = PT2[:].rearrange("p (n k) -> p n k", n=4)
                for j, (sl, b0) in enumerate(todo):
                    A(a.activation(ptsb[:, sl, b0 * P:256], src[:, sl, b0 * P:256], ACT.Copy), E("pt_done") if j == len(todo) - 1 else None)

            def exps(c):
                p, g, t = quads[c]
                act.wait_ge(E("ttr_done"), c + 1)
                if c > 0:
                    act.wait_ge(E("pt_full"), c)
                if c - 3 > 0:
                    act.wait_ge(E("pv_full"), c - 3)
                for i, hh, ti in quad:
                    lo = key_blocks(g, 2 * t + ti)[0] * P
                    col = c % 4 * 4 + i
                    A(a.activation(prob[:, i, lo:256], negl[:, i, lo:256], ACT.Exp, bias=negm[:, col:col + 1], scale=-1.0, accum_out=den1[:, col:col + 1]),
                      E("exp_done") if i == 3 else None)
                cols = slice(c % 4 * 4, c % 4 * 4 + 4)
                for x, col in enumerate((den1, negm)):
                    A(a.activation(wide[:, c % 2, x], col[:, cols].rearrange("p (h t) -> p t h", h=2).unsqueeze(3).to_broadcast([P, 2, 2, 64]), ACT.Copy))

            def raw_half(u, h, dst, mixed_sb, col):
                cs = slice(HALF * h, HALF * h + HALF)
                wait_full(act, u, h)
                A(a.activation(dst[:, cs], G[h][:], ACT.Copy, scale=less_mix[:, col:col + 1]))
                A(a.activation(mixed_sb[:, cs], G[h][:], ACT.Copy, scale=mix[:, col:col + 1]), emptied(u, h))

            def first_half(i):
                raw_half(U_R + i // 2, i % 2, (lora[:], *raw_of)[i // 2], oF[:, 4 + i // 2, :], (12, 0, 4, 8)[i // 2])

            for s in range(A_END + 1):
                if s >= 25 and (s - 25) % 20 == 0:
                    p = (s - 25) // 20
                    act.wait_ge(E("fin_done"), p + 1)
                    act.dma_start(oA_d[p], og[:]).then_inc(E("oa_out"), 16)
                if s - 1 in slot_of:
                    copy_back(slot_of[s - 1])
                if s in slot_of:
                    exps(slot_of[s])
                if s - 2 in slot_of and quads[slot_of[s - 2]][1]:
                    c = slot_of[s - 2]
                    k = sum(1 for q in quads[:c] if q[1]) + 1
                    act.wait_ge(E("ab_ready"), k)
                    A(a.activation(eab[:], eab[:], ACT.Exp), E("eab_done"))
                if s < A_SLOTS:
                    u, h = s // 2, s % 2
                    p, r = u // 10, u % 10
                    g, gi = r // 3, 3 * p + r // 3
                    if r == 9:
                        wait_full(act, u, h)
                        if p > 0:
                            act.wait_ge(E("fin_done"), p)
                        A(a.activation(zs[:, HALF * h:HALF * h + HALF], G[h][:], ACT.Tanh, scale=0.5), E("z_tanh"))
                    elif r % 3 < 2:
                        wait_full(act, u, h)
                        if gi >= 2:
                            act.wait_ge(E("s_full"), 4 * (gi - 1))
                        dst = (qT, kT)[r % 3]
                        A(a.activation(perm_half(dst[:, gi % 2, :], g, h), nat_half(G[h][:], g), ACT.Copy, scale=(0.125, 1.0)[r % 3]), emptied(u, h))
                elif s < A_END:
                    first_half(s - A_SLOTS)
            act.wait_ge(E("oa_out"), 64)
            act.dma_start(upw[0:64, :], d["rwkv_w_up"][0]).then_inc(E("up_in"), 16)
            act.dma_start(upw[64:128, :], d["rwkv_a_up"][0]).then_inc(E("up_in"), 16)
            lo_, hi_ = slice(0, 64), slice(64, 128)

            def side_out(p, place):
                i0, i1 = SIDE[p][place]
                for e in range(i0 // 8, i1 // 8):
                    j, h = GATES_BEFORE[p] + e // 2, e % 2
                    i = j - GATES_BEFORE[p + 1]
                    u = U_SIDE[p] + e // 2
                    if u == U_SIDE[p + 1] - 1:
                        wait_full(act, u, h)
                        act.wait_ge(E("gate_out"), 32 * GATES_BEFORE[p + 1])
                        A(a.activation(oF[:, 4 + p, HALF * h:HALF * h + HALF], G[h][:], ACT.Tanh, scale=0.5), E("zr_tanh"))
                    elif i >= 0:
                        act.wait_ge(E("ak_ready"), p + 1)
                        if 3 * p + i > 0:
                            act.wait_ge(E("mixed_next"), 3 * p + i)
                        if i == 2:
                            act.wait_ge(E("vr_tr"), 5 * p + 5)
                        raw_half(u, h, raw_of[i], oF[:, 5 + p, :], 4 * i + p + 1)
                    else:
                        n = 2 * j + h
                        buf = oF[:, 4 + p, 0:HALF]
                        wait_full(act, u, h)
                        if 3 * p > 0:
                            act.wait_ge(E("mixed_next"), 3 * p)
                        if 16 * n > 0:
                            act.wait_ge(E("gate_out"), 16 * n)
                        A(a.activation(buf, G[h][:], ACT.Tanh, scale=0.5), emptied(u, h))
                        act.dma_start(gates_d[:, j, HALF * h:HALF * h + HALF], buf).then_inc(E("gate_out"), 16)

            for i in range(A_END - A_SLOTS, 8):
                first_half(i)
                if i == 5:
                    act.wait_ge(E("mixed"), 1)
                    A(a.activation(lora[0:64, :], lora[0:64, :], ACT.Tanh), E("lora_tanh"))
            half_rate = -0.5 * math.exp(-0.5)
            for p in range(PAIRS):
                one = slice(p, p + 1)
                if p == 0:
                    act.wait_ge(E("mixed"), 4)
                else:
                    act.wait_ge(E("mixed_next"), 3 * p)
                A(a.activation(ksq[:], rkT[:], ACT.Square, scale=chan["rwkv_k_k"][:, one]), E("k_sq"))
                act.wait_ge(E("a_full"), p + 1)
                A(a.activation(aT[:], PT2[:], ACT.Tanh, bias=half_a0[:, one], scale=0.5), E("a_tanh"))
                A(a.activation(kgain[:], aT[:], ACT.Identity, bias=less_k_a[:, one], scale=half_k_a[:, one]), E("k_gain"))
                act.wait_ge(E("lw_full"), p + 1)
                A(a.activation(logw[:], S2[:], ACT.Tanh, bias=half_w0[:, one], scale=0.5), E("lw_tanh"))
                A(a.activation(logw[:], logw[:], ACT.Copy, bias=half_rate, scale=half_rate), E("logw"))
                A(a.activation(aT[:], aT[:], ACT.Copy, bias=0.5, scale=0.5), E("a_sig"))
                side_out(p, "in")
                act.wait_ge(E("knorm_sb"), p + 1)
                A(a.activation(stat[:, 112:128], stat[:, 112:128], ACT.Sqrt), E("k_sqrt"))
                act.wait_ge(E("cum"), p + 1)
                A(a.activation(ec[:], cum[:], ACT.Exp))
                A(a.activation(logw[:], logw[:], ACT.Exp))
                A(a.activation(cum[:], cum[:], ACT.Exp, scale=-1.0), E("exps"))
                side_out(p, "norm")
                side_out(p, "bonus")
                side_out(p, "amat0")
                for f in range(4):
                    act.wait_ge(E("bk_tr"), 4 * p + f + 1)
                    A(a.activation(BKt[:, 4 * f:4 * f + 4, :], (PV, MB)[f % 2][:].rearrange("p (n c) -> p n c", n=4), ACT.Copy), E("bk_rows"))
                    if f == 1:
                        side_out(p, "amat1")
                side_out(p, "amat2")
                side_out(p, "amat3")
                for f in range(5):
                    bank = (PV, MB)[f % 2][:].rearrange("p (w x c) -> p w x c", w=4, x=2)
                    act.wait_ge(E("vr_tr"), 5 * p + f + 1)
                    w0, w1 = 4 * f, min(4 * f + 4, 17)
                    s0 = 1 if w0 == 0 else 0
                    for kind in range(2):
                        A(a.activation(SV[lo_, 1, kind, w0 + s0 - 1:w1 - 1, :], bank[lo_, s0:w1 - w0, 1, :], ACT.Copy), E("vr_odd") if kind else None)
                for f in range(5):
                    side_out(p, f"rows{f}")
                for i in range(22):
                    side_out(p, f"inv{i}")
                if p == PAIRS - 1:
                    act.wait_ge(E("inv_sb"), 12 * PAIRS)
                    for k in range(4):
                        act.dma_start(oA[k][:], oA_d[k]).then_inc(E("oa_in"), 16)
                for c in range(NCH):
                    side_out(p, f"scan{3 * c}")
                    act.wait_ge(E("su_full"), NCH * p + c + 1)
                    A(a.activation(SV[hi_, 1, 1, c, :], MB[hi_, 0:C], ACT.Copy), E("su_odd"))
                    side_out(p, f"scan{3 * c + 1}")
                    side_out(p, f"scan{3 * c + 2}")
                act.wait_ge(E("y_full"), p + 1)
                A(a.activation(yT[:], S2[:], ACT.Copy), E("y_sb"))
                if p == PAIRS - 1:
                    act.wait_ge(E("oa_in"), 64)
                    for k in range(3):
                        A(a.activation(ohi[:, k, :], oA[k][:], ACT.Copy), E("high_part"))
                act.wait_ge(E("centred_full"), p + 1)
                A(a.activation(ysq[:], PT2[:], ACT.Square), E("y_sq"))
                load_table(ACT.Sqrt)
                act.wait_ge(E("y_var"), p + 1)
                A(a.activation(stat[:, 128:144], stat[:, 128:144], ACT.Sqrt), E("y_sd"))
                if p < PAIRS - 1:
                    for f in range(4):
                        side_out(p + 1, f"pre{f}")

            act.wait_ge(w_used, U_M)
            for j in range(4):
                act.dma_start(gates[:, 4 * j:4 * j + 4, :], gates_d[:, 4 * j:4 * j + 4, :]).then_inc(E(f"gates_in{j}"), 16)
            for k in range(3, 8):
                if k - 3 > 0:
                    act.wait_ge(E("pair_done"), k - 3)
                if k >= 6:
                    act.wait_ge(E("low_part"), PART["o"] + 3 * (k - 6) + 1)
                A(a.activation(ohi[:, k, :], oF[:, k, :] if k >= 4 else oA[k][:], ACT.Copy), E("high_part"))
            for j in range(KT):
                act.wait_ge(E("merged"), j + 1)
                A(a.activation(mhi[:, j, :], gates[:, 2 * j + 1, :], ACT.Copy, scale=0.5), E("high_part"))
            act.wait_ge(w_used, U_O)
            for n in range(8):
                act.dma_start(xt2[:, n, :], d["x"][0, n * P:(n + 1) * P, :]).then_inc(E(f"x_in{n // 4}"), 16)

            sq_n = [0, 0]

            def square(src, k):
                n = sq_n[1]
                if k < 2:
                    if SUMS_BEFORE[n] > 0:
                        act.wait_ge(E("sq_used"), SUMS_BEFORE[n])
                elif BY_POOL[n]:
                    act.wait_ge(E("sq_added"), ADDS * (n // 2) + k - 1)
                else:
                    act.wait_ge(E("sq_used"), SUMS_BEFORE[n] + k - 1)
                A(a.activation(sq_buf[min(k, 1) if BY_POOL[n] else k % 2][:], src[:, k, :], ACT.Square), E("sq"))

            def root():
                sq_n[1] += 1
                act.wait_ge(E("norm_var"), sq_n[1])
                A(a.activation(stat[:, 344:352], stat[:, 344:352], ACT.Sqrt), E("norm_sd"))
                act.wait_ge(E("rstd_full"), sq_n[1])
                A(a.activation(nrs[:], S2[:], ACT.Copy), E("nrs"))

            def product_tile(u, dst, j):
                for h in range(2):
                    wait_full(act, u, h)
                    A(a.activation(dst[:, j, HALF * h:HALF * h + HALF], G[h][:], ACT.Copy), emptied(u, h))
                square(dst, j)

            for j in range(KT):
                product_tile(U_O + j, y1, j)
            root()
            g2 = gain["a_pre_g_2"]
            for k in range(KT):
                act.wait_ge(E("x2"), k + 1)
                act.dma_start(x2_d[:, k, :], y1[:, k, :]).then_inc(E("x2_out"), 16)
                A(a.activation(h2hi[:, k, :], y1[:, k, :], ACT.Copy, scale=g2[:, k:k + 1]), E("high_part"))
                square(y1, k)
            root()
            load_table(ACT.Gelu_apprx_tanh)
            act.wait_ge(E("x2_out"), 16 * KT)

            act.wait_ge(E("low_part"), PART["h2"] + 8)
            act.dma_start(wsr[:], d["a_w_s_2"][0].rearrange("g t s -> t g s")).then_inc(E("ws_in"), 16)
            act.dma_start(bsb[:], d["a_b_s_2"][0:1].to_broadcast([P, 8, P])).then_inc(E("ws_in"), 16)
            for i in range(16):
                if 2 * i > 0:
                    act.wait_ge(E("vg_tr"), 2 * i)
                for h in range(2):
                    act.wait_ge(g_evac[h], outs_before[U_V + i] + 1)
                    A(a.activation(vg[:, HALF * h:HALF * h + HALF], scaled_g[:, h, :], ACT.Gelu_apprx_tanh), E("scaled_used"))
            for i in range(16):
                if i > 0:
                    act.wait_ge(E("u_used"), i)
                for h in range(2):
                    act.wait_ge(g_evac[h], outs_before[U_UZ + 2 * i] + 1)
                    A(a.activation(ug[:, HALF * h:HALF * h + HALF], scaled_g[:, h, :], ACT.Gelu_apprx_tanh), E("scaled_used"))
                if i == 0:
                    load_table(ACT.Sqrt)
                    act.wait_ge(E("ln_var"), 1)
                    A(a.activation(stat[:, 336:344], stat[:, 336:344], ACT.Sqrt), E("ln_sd"))
                    act.wait_ge(E("ln_stats"), 1)
                    for n in range(4, 8):
                        A(a.activation(vln[:, n, :], vln[:, n, :], ACT.Identity, bias=stat[:, 344 + n:345 + n], scale=stat[:, 336 + n:337 + n]), E("v_normed_act"))
                if i > 0:
                    act.wait_ge(E("y_mlp"), i)
                for h in range(2):
                    act.wait_ge(g_evac[h], outs_before[U_UZ + 2 * i + 1] + 1)
                    A(a.activation(zg[:, HALF * h:HALF * h + HALF], scaled_g[:, h, :], ACT.Tanh, scale=0.5), E("scaled_used"))
            act.wait_ge(w_used, U_AO)
            for i in range(16):
                act.wait_ge(E("y_mlp"), i + 1)
                A(a.activation(yhi[:, i, :].rearrange("p (n t) -> p n t", n=8), vln[:, :, i * P:i * P + P], ACT.Copy), E("high_part"))
            load_table(ACT.Sqrt)
            for j in range(KT):
                if j == KT - 1:
                    act.wait_ge(w_used, U_KV - 1)
                    act.dma_start(res[:], x2_d).then_inc(E("res_in"), 16)
                product_tile(U_AO + 2 * j + 1, y2, j)
            root()
            for k in range(KT):
                act.wait_ge(E("x3"), k + 1)
                act.dma_start(x3_d[:, k, :], y2[:, k, :]).then_inc(E("x3_out"), 16)
                A(a.activation(xnhi[:, k, :], y2[:, k, :], ACT.Copy), E("high_part"))
                square(y2, k)
            root()
            load_table(ACT.Exp)
            act.wait_ge(E("x3_out"), 16 * KT)

            lo_ = slice(0, 64)
            act.wait_ge(E("low_by_pool"), 8)
            for j in range(2):
                for h in range(2):
                    act.wait_ge(g_evac[h], outs_before[U_KV + j] + 1)
                    cs = slice(HALF * h, HALF * h + HALF)
                    for m in range(2):
                        src = scaled_s[(lo_, hi_)[m], h, :]
                        A(a.activation(kd[lo_, 2 * j + m, cs], src, ACT.Copy))
                        A(a.activation(kd[hi_, 2 * j + m, cs], src, ACT.Copy), E("scaled_used") if m else None)
            def copy_back2(c):
                act.wait_ge(E("pt_full"), len(quads) + c + 1)
                act.wait_ge(E("pv_full"), len(quads) + c)
                src = PT2[:].rearrange("p (n k) -> p n k", n=4)
                todo = runs((1, 0) if c % 4 == 0 else (0, 0))
                for j, (sl, b0) in enumerate(todo):
                    A(a.activation(pts2[:, sl, b0 * P:256], src[:, sl, b0 * P:256], ACT.Copy), E("pt_done") if j == len(todo) - 1 else None)

            def exps2(c):
                i, t = c // 4, c % 4
                act.wait_ge(E("ttr_done"), len(quads) + c + 1)
                act.wait_ge(E("pt_full"), len(quads) + c - 1)
                for x, hh, ti in quad:
                    lo = P if 2 * t + ti == 0 else 0
                    col = c % 2 * 4 + x
                    A(a.activation(pr2[:, c % 2, x, lo:256], neg2[:, x, lo:256], ACT.Exp, bias=negm[:, col:col + 1], scale=-1.0, accum_out=den2[:, c % 2, x:x + 1]))
                for hh in range(2):
                    cols = slice(c % 2 * 4 + 2 * hh, c % 2 * 4 + 2 * hh + 2)
                    A(a.activation(den2[:, c % 2, 4 + 2 * hh:6 + 2 * hh], negm[:, cols], ACT.Exp, bias=sink[:, 2 * i + hh:2 * i + hh + 1]),
                      E("exp_done") if hh else None)

            def high_of_y(k):
                act.wait_ge(w_used, U_BO)
                act.wait_ge(E("pv_free"), len(quads) + 4 * k + 4)
                A(a.activation(yshi[:, k, :], ys[:, k, :], ACT.Copy), E("high_part"))

            for s in range(4 * QP + 6):
                c = s - 3
                if 0 <= c - 2 < 4 * QP:
                    copy_back2(c - 2)
                if 0 <= c < 4 * QP:
                    exps2(c)
                if s < 4 * QP and s % 4 >= 2:
                    i, h = s // 4, s % 2
                    act.wait_ge(g_evac[h], outs_before[U_QZ + s // 2] + 1)
                    act.wait_ge(E("pv_free"), len(quads) + 4 * (i - 1))
                    A(a.activation(zs2[:, i % 2, HALF * h:HALF * h + HALF], scaled_s[:, h, :], ACT.Tanh, scale=0.5), E("scaled_used"))
                if s in (33, 34, 35):
                    high_of_y(2 * (s - 33))
                    high_of_y(2 * (s - 33) + 1)
            high_of_y(6)
            high_of_y(7)
            act.wait_ge(E("ys_done"), 1)
            act.dma_start(x3[:], x3_d).then_inc(E("x3_in"), 16)
            load_table(ACT.Sqrt)
            for j in range(KT):
                product_tile(U_BO + j, y3, j)
            root()
            for n in range(8):
                act.wait_ge(E("out_tr"), n + 1)
                A(a.activation(orow[:, n, :], (PT2, S2)[n % 2][:], ACT.Copy), E("rows_out"))
                act.dma_start(out[0, n * P:(n + 1) * P, :], orow[:, n, :]).then_inc(E("out_done"), 16)
            act.wait_ge(E("out_done"), 128)


_VECTORS = ["pre_norm_gain", "post_norm_gain", "a_pre_g_2", "a_post_g_2", "kv_norm_g_2", "b_pre_g_2", "b_post_g_2", "rwkv_shift_mix",
            "rwkv_w0", "rwkv_a0", "rwkv_k_k", "rwkv_k_a", "rwkv_r_k", "rwkv_ln_w", "rwkv_ln_b", "a_ln_g_2", "a_ln_b_2"]
_INS = ["x", "w_in", "rel_bias", "rwkv_w_up", "rwkv_a_up", "w_up_attn", "w_up_rwkv", "w_out", "a_w_in_2", "a_w_s_2", "a_b_s_2", "a_w_out_2",
        "w_k_2", "w_v_2", "b_w_in_2", "b_sinks_2", "b_w_out_2"]


def launch_arrays(inputs):
    packed, hot = shape_constants()
    vectors = np.concatenate([inputs[n].reshape(-1, P) for n in _VECTORS]).T
    named = [*((n, inputs[n]) for n in _INS), ("channel_vectors", vectors), ("shape_consts", packed), ("bucket_hot", hot)]
    return [(n, np.ascontiguousarray(a)) for n, a in named]


def kernel(**inputs):
    import numpy as _np
    import concourse.bacc as _bacc
    from concourse import mybir as _mybir
    from concourse.bass_utils import run_bass_kernel_spmd as _run

    nc = _bacc.Bacc("TRN2", target_bir_lowering=False, num_devices=1)
    arrays, aps = {}, {}
    for name, a in launch_arrays({n: _np.asarray(x) for n, x in inputs.items()}):
        arrays[f"in_{name}"] = a
        aps[name] = nc.dram_tensor(f"in_{name}", a.shape, _mybir.dt.from_np(a.dtype), kind="ExternalInput").ap()
    out = nc.dram_tensor("out_0", (1, T, D), F32, kind="ExternalOutput").ap()
    build(nc, aps, out)
    r = _run(nc, [arrays], core_ids=[0])
    return r.results[0]["out_0"]
```
